# Optimizing a Trainium2 kernel written in Bass

```python
import math
import jax, jax.numpy as jnp
from jax import lax
import numpy as np

D_MODEL = 1024
BATCH = 1
SEQ = 1024
DEPTH = 1
DEC_BATCH = 8
DEC_SEQ = 8
PAST_LEN = 4096
PAGE_SIZE = 128

NSA_HEADS = 8
NSA_KV_HEADS = 2
NSA_GROUP = NSA_HEADS // NSA_KV_HEADS
HEAD_DIM = 64
CMP_BLOCK = 32
SEL_BLOCK = 64
TOP_K = 16
WINDOW = 512
WIN_QBLOCK = 128
SEL_QBLOCK = 64
GLA_HEADS = 4
GLA_DK = 64
GLA_DV = 128
GLA_RANK = 16
GLA_TAU = 16.0
GLA_CHUNK = 64
MIX_WIDTH = NSA_HEADS * HEAD_DIM + GLA_HEADS * GLA_DV
D_FF = -(-(8 * D_MODEL) // (3 * 256)) * 256
KV_WIDTH = NSA_KV_HEADS * HEAD_DIM
IN_WIDTHS = (NSA_HEADS * HEAD_DIM, 6 * KV_WIDTH, 3 * NSA_HEADS, GLA_HEADS * GLA_DK, GLA_HEADS * GLA_DK, GLA_HEADS * GLA_DV, GLA_HEADS * GLA_DV, GLA_RANK)
IN_WIDTH = sum(IN_WIDTHS)
SPLIT_POINTS = tuple(int(v) for v in np.cumsum(IN_WIDTHS)[:-1])
EPS = 1e-6
NEG_INF = -1e30
FORCE_SCORE = 1e4
SCALE = HEAD_DIM ** -0.5

kernel_name = 'hybrid_nsa_gla_decode_step'

def rms_norm(x, g):
    xf = x.astype(jnp.float32)
    y = xf * lax.rsqrt(jnp.mean(xf * xf, axis=-1, keepdims=True) + EPS)
    return (y * g.astype(jnp.float32)).astype(x.dtype)

def alibi_slopes():
    h = jnp.arange(1, NSA_HEADS + 1, dtype=jnp.float32)
    return (2.0 ** (-8.0 * h / NSA_HEADS)).reshape(NSA_KV_HEADS, NSA_GROUP)

def compressed_branch(q, q_pos, k_c, v_c, w_pos, slopes):
    B, L = k_c.shape[:2]
    n_cmp = L // CMP_BLOCK
    kb = k_c[:, :n_cmp * CMP_BLOCK].reshape(B, n_cmp, CMP_BLOCK, NSA_KV_HEADS, HEAD_DIM)
    vb = v_c[:, :n_cmp * CMP_BLOCK].reshape(B, n_cmp, CMP_BLOCK, NSA_KV_HEADS, HEAD_DIM)
    kc = jnp.einsum('bnckd,c->bnkd', kb, w_pos[0])
    vc = jnp.einsum('bnckd,c->bnkd', vb, w_pos[1])
    end_pos = (jnp.arange(n_cmp) + 1) * CMP_BLOCK - 1
    dist = (q_pos[:, None] - end_pos[None, :]).astype(jnp.float32)
    valid = (dist >= 0)[None, :, None, None, :]
    s = jnp.einsum('btkgd,bnkd->btkgn', q, kc).astype(jnp.float32) * SCALE
    s = s - slopes[None, None, :, :, None] * dist[None, :, None, None, :]
    p = jax.nn.softmax(jnp.where(valid, s, NEG_INF), axis=-1)
    p = jnp.where(valid, p, 0.0)
    o = jnp.einsum('btkgn,bnkd->btkgd', p.astype(vc.dtype), vc)
    return o, p

def select_blocks(p_cmp, q_pos, L):
    B, T = p_cmp.shape[:2]
    n_cmp = p_cmp.shape[-1]
    ratio = SEL_BLOCK // CMP_BLOCK
    n_sel = -(-L // SEL_BLOCK)
    imp = p_cmp.sum(axis=3)
    imp = jnp.pad(imp, ((0, 0), (0, 0), (0, 0), (0, n_sel * ratio - n_cmp)))
    imp = imp.reshape(B, T, NSA_KV_HEADS, n_sel, ratio).sum(-1)
    blk = jnp.arange(n_sel)[None, :]
    cur = (q_pos // SEL_BLOCK)[:, None]
    forced = (blk == 0) | (blk == cur) | (blk == cur - 1)
    valid = blk <= cur
    score = jnp.where(forced[None, :, None, :], FORCE_SCORE, jnp.where(valid[None, :, None, :], imp, NEG_INF))
    _, idx = lax.top_k(score, min(TOP_K, n_sel))
    return idx

def selected_branch(q, q_pos, idx, k_s, v_s, slopes):
    B, L = k_s.shape[:2]
    T = q.shape[1]
    n_sel = -(-L // SEL_BLOCK)
    padn = n_sel * SEL_BLOCK - L
    kt = jnp.pad(k_s, ((0, 0), (0, padn), (0, 0), (0, 0))).reshape(B, n_sel, SEL_BLOCK, NSA_KV_HEADS, HEAD_DIM).transpose(0, 3, 1, 2, 4)
    vt = jnp.pad(v_s, ((0, 0), (0, padn), (0, 0), (0, 0))).reshape(B, n_sel, SEL_BLOCK, NSA_KV_HEADS, HEAD_DIM).transpose(0, 3, 1, 2, 4)
    qb = math.gcd(T, SEL_QBLOCK)
    nb = T // qb
    n_k = idx.shape[-1]
    bi = jnp.arange(B)[:, None, None, None]
    hi = jnp.arange(NSA_KV_HEADS)[None, None, :, None]

    def one_block(args):
        qi, pi, ii = args
        ksel = kt[bi, hi, ii]
        vsel = vt[bi, hi, ii]
        kpos = ii[..., None] * SEL_BLOCK + jnp.arange(SEL_BLOCK)
        dist = (pi[None, :, None, None, None] - kpos).astype(jnp.float32)
        valid = (dist >= 0)[:, :, :, None]
        s = jnp.einsum('btkgd,btkjsd->btkgjs', qi, ksel).astype(jnp.float32) * SCALE
        s = s - slopes[None, None, :, :, None, None] * dist[:, :, :, None]
        s = jnp.where(valid, s, NEG_INF)
        p = jax.nn.softmax(s.reshape(B, qb, NSA_KV_HEADS, NSA_GROUP, n_k * SEL_BLOCK), axis=-1)
        p = p.reshape(B, qb, NSA_KV_HEADS, NSA_GROUP, n_k, SEL_BLOCK)
        return jnp.einsum('btkgjs,btkjsd->btkgd', p.astype(vsel.dtype), vsel)

    xs = (q.reshape((B, nb, qb) + q.shape[2:]).swapaxes(0, 1),
          q_pos.reshape(nb, qb),
          idx.reshape(B, nb, qb, NSA_KV_HEADS, n_k).swapaxes(0, 1))
    o = lax.map(one_block, xs)
    return o.swapaxes(0, 1).reshape(q.shape)

def window_attend(q, q_pos, k, v, k_pos, slopes):
    dist = q_pos[:, :, None] - k_pos[:, None, :]
    valid = ((dist >= 0) & (dist < WINDOW) & (k_pos[:, None, :] >= 0))[None, :, :, None, None, :]
    s = jnp.einsum('bntkgd,bnskd->bntkgs', q, k).astype(jnp.float32) * SCALE
    s = s - slopes[None, None, None, :, :, None] * dist.astype(jnp.float32)[None, :, :, None, None, :]
    p = jax.nn.softmax(jnp.where(valid, s, NEG_INF), axis=-1)
    return jnp.einsum('bntkgs,bnskd->bntkgd', p.astype(v.dtype), v)

def window_prompt(q, k_w, v_w, slopes):
    B, T = q.shape[:2]
    wb = math.gcd(T, WIN_QBLOCK)
    nb = T // wb
    kp = jnp.pad(k_w, ((0, 0), (WINDOW, 0), (0, 0), (0, 0)))
    vp = jnp.pad(v_w, ((0, 0), (WINDOW, 0), (0, 0), (0, 0)))
    idx = jnp.arange(nb)[:, None] * wb + jnp.arange(wb + WINDOW)[None, :]
    q_pos = jnp.arange(T).reshape(nb, wb)
    o = window_attend(q.reshape((B, nb, wb) + q.shape[2:]), q_pos, kp[:, idx], vp[:, idx], idx - WINDOW, slopes)
    return o.reshape(q.shape)

def gla_recurrence(q, k, v, log_a, s0):
    B, T = q.shape[:2]
    c = math.gcd(T, GLA_CHUNK)
    n = T // c
    causal = jnp.tril(jnp.ones((c, c), dtype=bool))[None, :, :, None, None]

    def to_chunks(a):
        return a.reshape((B, n, c) + a.shape[2:]).swapaxes(0, 1)

    def step(S, xs):
        qc, kc, vc, lac = xs
        cum = jnp.cumsum(lac, axis=1)
        inter = jnp.einsum('bthd,bhde->bthe', qc * jnp.exp(cum), S)
        diff = cum[:, :, None] - cum[:, None, :]
        decay = jnp.exp(jnp.where(causal, diff, NEG_INF))
        A = jnp.einsum('bthd,bshd,btshd->btsh', qc, kc, decay)
        intra = jnp.einsum('btsh,bshe->bthe', A, vc)
        last = cum[:, -1]
        S_new = jnp.exp(last)[..., None] * S + jnp.einsum('bshd,bshe->bhde', kc * jnp.exp(last[:, None] - cum), vc)
        return S_new, inter + intra

    S, o = lax.scan(step, s0, (to_chunks(q), to_chunks(k), to_chunks(v), to_chunks(log_a)))
    return o.swapaxes(0, 1).reshape(B, T, GLA_HEADS, GLA_DV), S

def trunk_layer(x, q_pos, past_kv, win_buf, gla_s0, ln_mix, w_in, q_norm, k_norm, cmp_pos_w, w_a2, b_a, gla_norm, w_out, ln_ffn, w_gate, w_up, w_down):
    B, T, _ = x.shape
    slopes = alibi_slopes()
    h = rms_norm(x, ln_mix)
    q, kv, gate, gq, gk, gv, gg, ga = jnp.split(h @ w_in, SPLIT_POINTS, axis=-1)
    q = rms_norm(q.reshape(B, T, NSA_KV_HEADS, NSA_GROUP, HEAD_DIM), q_norm)
    kv = kv.reshape(B, T, 6, NSA_KV_HEADS, HEAD_DIM)
    k_n = rms_norm(kv[:, :, 0::2], k_norm[:, None, :])
    kv = jnp.stack([k_n, kv[:, :, 1::2]], axis=3).reshape(B, T, 6, NSA_KV_HEADS, HEAD_DIM)
    new_rows = kv[:, :, :4]
    win_rows = kv[:, :, 4:]
    if past_kv is None:
        full = new_rows
        o_w = window_prompt(q, win_rows[:, :, 0], win_rows[:, :, 1], slopes)
        keep = min(WINDOW, T)
        new_win = win_rows[:, T - keep:]
    else:
        full = jnp.concatenate([past_kv, new_rows], axis=1)
        buf = jnp.concatenate([win_buf, win_rows], axis=1)
        n_buf = buf.shape[1]
        k_pos = past_kv.shape[1] - win_buf.shape[1] + jnp.arange(n_buf)
        o_w = window_attend(q[:, None], q_pos[None], buf[:, None, :, 0], buf[:, None, :, 1], k_pos[None], slopes)[:, 0]
        keep = min(WINDOW, n_buf)
        new_win = buf[:, n_buf - keep:]
    L = full.shape[1]
    o_c, p_c = compressed_branch(q, q_pos, full[:, :, 0], full[:, :, 1], cmp_pos_w, slopes)
    idx = select_blocks(p_c, q_pos, L)
    o_s = selected_branch(q, q_pos, idx, full[:, :, 2], full[:, :, 3], slopes)
    g = jax.nn.sigmoid(gate.reshape(B, T, 3, NSA_KV_HEADS, NSA_GROUP, 1))
    o_nsa = (g[:, :, 0] * o_c + g[:, :, 1] * o_s + g[:, :, 2] * o_w).reshape(B, T, NSA_HEADS * HEAD_DIM)
    gq = gq.reshape(B, T, GLA_HEADS, GLA_DK).astype(jnp.float32) * (GLA_DK ** -0.5)
    gk = gk.reshape(B, T, GLA_HEADS, GLA_DK).astype(jnp.float32)
    gv = gv.reshape(B, T, GLA_HEADS, GLA_DV).astype(jnp.float32)
    log_a = jax.nn.log_sigmoid((ga @ w_a2 + b_a).astype(jnp.float32)).reshape(B, T, GLA_HEADS, GLA_DK) / GLA_TAU
    o_g, s_new = gla_recurrence(gq, gk, gv, log_a, gla_s0.astype(jnp.float32))
    o_g = rms_norm(o_g, gla_norm) * jax.nn.silu(gg.reshape(B, T, GLA_HEADS, GLA_DV).astype(jnp.float32))
    o_g = o_g.reshape(B, T, GLA_HEADS * GLA_DV).astype(x.dtype)
    x = x + jnp.concatenate([o_nsa.astype(x.dtype), o_g], axis=-1) @ w_out
    h2 = rms_norm(x, ln_ffn)
    x = x + (jax.nn.silu(h2 @ w_gate) * (h2 @ w_up)) @ w_down
    return x, new_rows, new_win, s_new

def setup_inputs(seed: int = 0) -> dict:
    key = jax.random.key(seed)
    ks = jax.random.split(key, 20)
    f32 = jnp.float32
    n_pages = PAST_LEN // PAGE_SIZE
    n_used = DEC_BATCH * n_pages
    n_phys = n_used + n_used // 4
    win_buf = min(WINDOW, PAST_LEN)

    def nrm(k, shape, scale):
        return jax.random.normal(k, shape, f32) * scale

    return {
        'x_prompt': nrm(ks[0], (BATCH, SEQ, D_MODEL), 1.0),
        'x_sample': nrm(ks[1], (DEC_BATCH, DEC_SEQ, D_MODEL), 1.0),
        'cache_nsa_kv': nrm(ks[2], (DEPTH, n_phys, PAGE_SIZE, 4, NSA_KV_HEADS, HEAD_DIM), 1.0),
        'state_nsa_win': nrm(ks[3], (DEPTH, DEC_BATCH, win_buf, 2, NSA_KV_HEADS, HEAD_DIM), 1.0),
        'state_gla': nrm(ks[4], (DEPTH, DEC_BATCH, GLA_HEADS, GLA_DK, GLA_DV), 0.1),
        'page_table': jax.random.permutation(ks[5], n_phys)[:n_used].reshape(DEC_BATCH, n_pages).astype(jnp.int32),
        'ln_mix': 1.0 + nrm(ks[6], (DEPTH, D_MODEL), 0.02),
        'w_in': nrm(ks[7], (DEPTH, D_MODEL, IN_WIDTH), D_MODEL ** -0.5),
        'q_norm': 1.0 + nrm(ks[8], (DEPTH, HEAD_DIM), 0.02),
        'k_norm': 1.0 + nrm(ks[9], (DEPTH, 3, HEAD_DIM), 0.02),
        'cmp_pos_w': (1.0 + nrm(ks[10], (DEPTH, 2, CMP_BLOCK), 0.1)) / CMP_BLOCK,
        'w_a2': nrm(ks[11], (DEPTH, GLA_RANK, GLA_HEADS * GLA_DK), GLA_RANK ** -0.5),
        'b_a': nrm(ks[12], (DEPTH, GLA_HEADS * GLA_DK), 0.01),
        'gla_norm': 1.0 + nrm(ks[13], (DEPTH, GLA_DV), 0.02),
        'w_out': nrm(ks[14], (DEPTH, MIX_WIDTH, D_MODEL), MIX_WIDTH ** -0.5),
        'ln_ffn': 1.0 + nrm(ks[15], (DEPTH, D_MODEL), 0.02),
        'w_gate': nrm(ks[16], (DEPTH, D_MODEL, D_FF), D_MODEL ** -0.5),
        'w_up': nrm(ks[17], (DEPTH, D_MODEL, D_FF), D_MODEL ** -0.5),
        'w_down': nrm(ks[18], (DEPTH, D_FF, D_MODEL), D_FF ** -0.5),
    }

def reference(x_prompt, x_sample, cache_nsa_kv, state_nsa_win, state_gla, page_table, ln_mix, w_in, q_norm, k_norm, cmp_pos_w, w_a2, b_a, gla_norm, w_out, ln_ffn, w_gate, w_up, w_down):
    B, T = x_prompt.shape[:2]
    DB, TS = x_sample.shape[:2]
    n_pages = page_table.shape[1]
    past_len = n_pages * cache_nsa_kv.shape[2]
    pos_p = jnp.arange(T)
    pos_s = past_len + jnp.arange(TS)
    s0_p = jnp.zeros((B, GLA_HEADS, GLA_DK, GLA_DV), jnp.float32)
    yp, ys = x_prompt, x_sample
    rows_p, win_p, gla_p, rows_s, win_s, gla_s = [], [], [], [], [], []
    for l in range(DEPTH):
        w = (ln_mix[l], w_in[l], q_norm[l], k_norm[l], cmp_pos_w[l], w_a2[l], b_a[l], gla_norm[l], w_out[l], ln_ffn[l], w_gate[l], w_up[l], w_down[l])
        yp, r_p, nw_p, st_p = trunk_layer(yp, pos_p, None, None, s0_p, *w)
        past = cache_nsa_kv[l][page_table].reshape(DB, past_len, 4, NSA_KV_HEADS, HEAD_DIM)
        ys, r_s, nw_s, st_s = trunk_layer(ys, pos_s, past, state_nsa_win[l], state_gla[l], *w)
        rows_p.append(r_p)
        win_p.append(nw_p)
        gla_p.append(st_p.astype(state_gla.dtype))
        rows_s.append(r_s)
        win_s.append(nw_s)
        gla_s.append(st_s.astype(state_gla.dtype))
    return (yp, ys, jnp.stack(rows_p), jnp.stack(win_p), jnp.stack(gla_p), jnp.stack(rows_s), jnp.stack(win_s), jnp.stack(gla_s))


_drawn_inputs = setup_inputs


def setup_inputs(seed=0):
    import zlib

    import numpy as np

    out = dict(_drawn_inputs(seed))
    spreads = {}
    factors = {'q_norm': 8.0,
     'k_norm': 3.85,
     'cmp_pos_w': 8.0,
     'b_a': 8.0,
     'gla_norm': 6.401,
     'ln_ffn': 4.129}
    for name, (base, spread) in spreads.items():
        noise = np.random.default_rng([zlib.crc32(name.encode()), seed]).standard_normal(out[name].shape)
        drawn = base * np.exp(spread * noise) if base else spread * noise
        out[name] = __import__('jax').numpy.asarray(drawn.astype(out[name].dtype))
    for name, factor in factors.items():
        out[name] = (out[name] * factor).astype(out[name].dtype)
    return out
```

```python
from contextlib import ExitStack, contextmanager

import concourse.bass as bass
from concourse import mybir

F32 = mybir.dt.float32
F32R = mybir.dt.float32r
I32 = mybir.dt.int32
U32 = mybir.dt.uint32
ALU = mybir.AluOpType
ACT = mybir.ActivationFunctionType
AX = mybir.AxisListType

P = 128
BANK = 512
D_MODEL = 1024
KT = D_MODEL // P
SEQ = 1024
DEC_BATCH = 8
DEC_SEQ = 8
SAMPLE_ROWS = DEC_BATCH * DEC_SEQ
PROMPT_TILES = SEQ // P
TILES = PROMPT_TILES + 1
TOKENS = SEQ + SAMPLE_ROWS
ROWS = [P] * PROMPT_TILES + [SAMPLE_ROWS]
PAST_LEN = 4096
PAGE_SIZE = 128
N_PAGES = PAST_LEN // PAGE_SIZE
HEADS = 8
KV_HEADS = 2
GROUP = HEADS // KV_HEADS
HD = 64
CMP_BLOCK = 32
SEL_BLOCK = 64
WINDOW = 512
GLA_HEADS = 4
DK = 64
DV = 128
RANK = 16
TAU = 16.0
CHUNK = 64
D_FF = 2816
FT = D_FF // P
EPS = 1e-6
MASKED = -1e30
SCALE = HD ** -0.5
SLOPES = [2.0 ** (-8.0 * (h + 1) / HEADS) for h in range(HEADS)]

Q0 = 0
KV0 = HEADS * HD
KV_COLS = 6 * KV_HEADS * HD
GATE0 = KV0 + KV_COLS
GQ0 = GATE0 + 3 * HEADS
GK0 = GQ0 + GLA_HEADS * DK
GV0 = GK0 + GLA_HEADS * DK
GG0 = GV0 + GLA_HEADS * DV
GA0 = GG0 + GLA_HEADS * DV
IN_WIDTH = GA0 + RANK

PIECES = [(0, 3 * P), (3 * P, 3 * P), (6 * P, TOKENS - 6 * P)]


class Turns:

    def __init__(self, banks, filled, evacuated, order):
        self.banks, self.filled, self.evacuated = banks, filled, evacuated
        self.turn = {key: (n % len(banks), n // len(banks)) for n, key in enumerate(order)}
        assert len(self.turn) == len(order)

    def bank(self, *key):
        return self.banks[self.turn[key][0]]

    def is_filled(self, *key):
        return self.filled[self.turn[key][0]]

    def is_evacuated(self, *key):
        return self.evacuated[self.turn[key][0]]

    def wait_free(self, pe, *key):
        b, use = self.turn[key]
        if use:
            pe.wait_ge(self.evacuated[b], use)

    def wait_filled(self, eng, *key):
        b, use = self.turn[key]
        eng.wait_ge(self.filled[b], use + 1)

    def wait_evacuated(self, eng, *key):
        b, use = self.turn[key]
        eng.wait_ge(self.evacuated[b], use + 1)


def turns(nc, ctx, sem, name, count, order):
    banks = [ctx.enter_context(nc.psum_tensor(f"{name}{n}", [P, BANK], F32)) for n in range(count)]
    filled = [sem(f"{name}{n}_filled") for n in range(count)]
    evacuated = [sem(f"{name}{n}_evacuated") for n in range(count)]
    return Turns(banks, filled, evacuated, order)


@contextmanager
def stage_semaphores(nc, stage):
    taken = []

    def sem(name):
        taken.append(nc.alloc_semaphore(name=f"{stage}_{name}"))
        return taken[-1]

    yield sem
    nc.clear_and_free_semaphores(taken)
    nc.all_engine_barrier()


def broadcast(ap, shape):
    return ap.to_broadcast(shape)


NSA_WIDTH = HEADS * HD
COMPRESSED, SELECTED, SLIDING = range(3)
SLC_AT, WIN_AT, CMP_AT = 0, SEQ, SEQ + WINDOW + P
SCORE_COLS = CMP_AT + SEQ // CMP_BLOCK
N_CMP = SEQ // CMP_BLOCK
WIN_TILES = WINDOW // P + 1
IN_CHUNKS = [(c * BANK, min(BANK, IN_WIDTH - c * BANK)) for c in range(-(-IN_WIDTH // BANK))]
GLA_WIDTH = GLA_HEADS * DK


class Shared:

    def __init__(self, nc, ctx, identity, minus_half):
        def sb(name, shape):
            return ctx.enter_context(nc.sbuf_tensor(name, shape, F32))

        self.identity = identity
        self.minus_half = minus_half
        self.proj0 = sb("proj0", [P, IN_WIDTH])
        self.q_paired = sb("q_paired", [P, NSA_WIDTH])
        self.gates = sb("gates0", [P, 3 * HEADS])
        self.cmp_w = sb("cmp_w", [P, 2, P // CMP_BLOCK])
        self.gla_gain = sb("gla_gain", [P, DV])
        self.w_a2 = sb("w_a2_sb", [RANK, GLA_WIDTH])
        self.b_a = sb("b_a_sb", [1, GLA_WIDTH])
        self.ones_row = sb("ones_row", [1, P])


def prompt_stage(nc, a, outs, mix_rows, x_rows, shared):
    identity, minus_half, proj0, q_paired = shared.identity, shared.minus_half, shared.proj0, shared.q_paired
    cmp_w, gla_gain, w_a2, b_a, ones_row = shared.cmp_w, shared.gla_gain, shared.w_a2, shared.b_a, shared.ones_row
    with ExitStack() as ctx:
        def sb(name, shape):
            return ctx.enter_context(nc.sbuf_tensor(name, shape, F32))

        sem = ctx.enter_context(stage_semaphores(nc, "prompt"))

        w_in = sb("w_in_sb", [P, KT, IN_WIDTH])
        ln_col = sb("ln_mix_col", [P, KT])
        q_gain = sb("q_gain", [P, HEADS, HD])
        k_gain = sb("k_gain", [P, 3, HD])
        slc_dist = sb("slc_dist", [P, SEQ])
        win_dist = sb("win_dist", [P, WINDOW + P])
        cmp_dist = sb("cmp_dist", [P, 2 * N_CMP - P // CMP_BLOCK])
        cum_upto = sb("cum_upto", [P, P])
        cum_from_mid = sb("cum_from_mid", [P, P])
        cum_after = sb("cum_after", [P, P])
        in_chunk = sb("in_chunk", [P, 2])
        x_in = sb("x_in", [P, D_MODEL])
        h_T = sb("h_T", [P, KT, P])
        mean_x = sb("mean_x", [P, TILES])
        rstd_x = sb("rstd_x", [P, TILES])
        proj = [proj0, sb("proj1", [P, IN_WIDTH])]
        norm_sq = sb("norm_sq", [P, NSA_WIDTH])
        norm_mean = sb("norm_mean", [P, 14])
        norm_rstd = sb("norm_rstd", [P, 14])
        gates = [shared.gates, sb("gates1", [P, 3 * HEADS])]
        q_T = sb("q_T", [P, HEADS, P])
        k_T = [sb("k_slc_T", [P, SEQ]), sb("k_win_T", [P, SEQ])]
        v_all = sb("v_all", [P, PROMPT_TILES, 2, KV_HEADS * HD])
        kc_T = sb("kc_T", [P, N_CMP])
        vc_T = sb("vc_T", [P, N_CMP])
        vc = sb("vc", [N_CMP, KV_HEADS * HD])
        scores = sb("scores", [P, SCORE_COLS])
        maxima = sb("maxima", [P, 3])
        neg_max = sb("neg_max", [P, 3])
        sums = sb("sums", [P, 3])
        weight = sb("branch_weight", [P, 3])
        probs_T = [sb(f"probs_T{n}", [P, BANK]) for n in range(3)]
        mix = sb("mix", [P, D_MODEL])
        ga_T = sb("ga_T", [RANK, P])
        z_min = sb("z_min", [P, GLA_WIDTH])
        log_a = sb("log_a", [P, GLA_WIDTH])
        q_decayed = sb("q_decayed", [P, 2, GLA_WIDTH])
        k_mid = sb("k_mid", [P, GLA_WIDTH])
        k_decay = sb("k_decay", [P, GLA_WIDTH])
        k_last = [sb(f"k_last{c}", [P, GLA_WIDTH]) for c in range(2)]
        decay = sb("decay", [P, 2, 2])
        q_mid_T = sb("q_mid_T", [P, 2, 2, P])
        k_mid_T = sb("k_mid_T", [P, 2, P])
        q_cum_T = [sb(f"q_cum_T{c}", [P, 2, P]) for c in range(2)]
        att_T = sb("gla_att_T", [P, GLA_HEADS, P])
        state = [sb(f"gla_state{n}", [P, 2, 2, DV]) for n in range(2)]
        o_gla = sb("o_gla", [P, GLA_HEADS, DV])
        norm_scratch = sb("o_squares", [P, GLA_HEADS, DV])
        o_mean = sb("o_mean", [P, GLA_HEADS])
        o_rstd = sb("o_rstd", [P, GLA_HEADS])
        silu = sb("gla_silu", [P, GLA_HEADS * DV])

        consts_landed = sem("consts_landed")
        w_in_landed = [sem(f"w_in_landed{k}") for k in range(KT)]
        x_landed = sem("x_landed")
        cleared = sem("consts_cleared")
        tables_step = sem("tables_step")
        tables_ready = sem("tables_ready")
        gain_ready = sem("gain_ready")
        sq_x_ready = sem("sq_x_ready")
        rstd_x_ready = sem("rstd_x_ready")
        h_T_ready = sem("h_T_ready")
        norm_step = sem("norm_step")
        norm_mean_ready = sem("norm_mean_ready")
        norm_rstd_ready = sem("norm_rstd_ready")
        qk_normed = sem("qk_normed")
        gate_exp = sem("gate_exp")
        gates_ready = sem("gates_ready")
        v_copied = sem("v_copied")
        rows_stored = [sem(f"rows_stored{n}") for n in range(2)]
        scores_filled = sem("scores_filled")
        scores_read = sem("scores_read")
        neg_max_ready = sem("neg_max_ready")
        probs_ready = sem("probs_ready")
        values_done = sem("values_done")
        weight_step = sem("weight_step")
        combined = sem("combined")
        mix_gla_ready = sem("mix_gla_ready")
        mix_stored = sem("mix_stored")
        state_stored = sem("state_stored")
        abs_step = sem("gla_abs_step")
        abs_ready = sem("gla_abs_ready")
        soft_step = sem("gla_soft_step")
        log_a_ready = sem("log_a_ready")
        exps_ready = sem("gla_exps_ready")
        decayed_ready = sem("gla_decayed_ready")
        k_last_ready = sem("k_last_ready")
        dve_tables = sem("dve_tables")
        att_ready = sem("gla_att_ready")
        state_ready = sem("gla_state_ready")
        silu_exp = sem("gla_silu_exp")
        silu_step = sem("gla_silu_step")
        silu_ready = sem("gla_silu_ready")
        o_copied = sem("o_gla_copied")
        o_mean_ready = sem("o_mean_ready")
        o_step = sem("o_step")

        slc_ps = ctx.enter_context(nc.psum_tensor("slc_ps", [P, 2 * BANK], F32))
        win_ps = ctx.enter_context(nc.psum_tensor("win_ps", [P, 2 * BANK], F32))
        o_ps = ctx.enter_context(nc.psum_tensor("o_ps", [P, BANK], F32))

        def key_tiles(i):
            first = max(0, i + 1 - WIN_TILES)
            return ([(SLC_AT + j * P, P, SELECTED, j) for j in range(i + 1)]
                    + [(WIN_AT + (j - first) * P, P, SLIDING, j) for j in range(first, i + 1)]
                    + [(CMP_AT, N_CMP, COMPRESSED, 0)])

        def key_groups(i):
            tiles = key_tiles(i)
            return [tiles[n:n + 4] for n in range(0, len(tiles), 4)]

        GLA_TURNS = [[("ga_T",)], [("z",)], [("cum", 0), ("cum", 1)], [("gla_T", 0), ("gla_T", 1)], [("att",)],
                     [("state", 0)], [("o",)], [("state", 1)]]
        order = [("x_T", 0, 0), ("x_T", 0, 1)] + [("proj", 0, c) for c in range(6)]
        group_no = {}
        for i in range(PROMPT_TILES):
            order += [("q_T", i), ("k_T", i), ("vc", i)]
            for h in range(HEADS):
                order += [("x_T", i + 1, 0), ("x_T", i + 1, 1)] if h == 0 else \
                    [("proj", i + 1, h - 1)] if h <= 6 else []
                order += [(key[0], i, *key[1:]) for key in GLA_TURNS[h]]
                for g in range(len(key_groups(i))):
                    group_no[i, h, g] = len(group_no)
                    order.append(("probs_T", i, h, g))
        ring = turns(nc, ctx, sem, "bank", 3, order)
        last_group = {(i, h): group_no[i, h, len(key_groups(i)) - 1] for i in range(PROMPT_TILES)
                      for h in range(HEADS)}

        CONSTS = 3 + 3 + 8
        block = ctx.enter_context(nc.Block())

        def branch_columns(i):
            return [(CMP_AT, N_CMP), (SLC_AT, (i + 1) * P), (WIN_AT, min(i + 1, WIN_TILES) * P)]

        def take_probs_T(eng, engine, i, h, parity):
            for g, group in enumerate(key_groups(i)):
                n = group_no[i, h, g]
                if n % 2 != parity:
                    continue
                if n >= 3:
                    eng.wait_ge(values_done, n - 2)
                ring.wait_filled(eng, "probs_T", i, h, g)
                whole = [m for m, t in enumerate(group) if t[1] == P]
                parts = [(P, 0, len(whole) * P)] if whole else []
                parts += [(N_CMP, m * P, P) for m, t in enumerate(group) if t[1] != P]
                for rows, at, cols in parts:
                    src = ring.bank("probs_T", i, h, g)[:rows, at:at + cols]
                    dst = probs_T[n % 3][:rows, at:at + cols]
                    if parity == 0:
                        last = nc.scalar.activation(dst, src, ACT.Copy)
                    else:
                        last = nc.vector.tensor_copy(dst, src)
                last.then_inc(ring.is_evacuated("probs_T", i, h, g), 1)

        @block.sync
        def _(sp):
            sp.dma_start(x_in[:, :], x_rows(0)).then_inc(x_landed, 16)
            sp.dma_start(ln_col[:, :], a["ln_mix"].rearrange("l (k p) -> p (l k)", p=P),
                         allow_slow_non_contiguous=True).then_inc(consts_landed, 16)
            for k in range(KT):
                sp.dma_start(w_in[:, k, :], a["w_in"][0, k * P:(k + 1) * P, :]).then_inc(w_in_landed[k], 16)
            sp.dma_start(q_gain[:, :, :], a["q_norm"].rearrange("l (a d) -> l a d", a=1).to_broadcast(
                [P, HEADS, HD])).then_inc(consts_landed, 16)
            sp.dma_start(k_gain[:, :, :], a["k_norm"].to_broadcast([P, 3, HD])).then_inc(consts_landed, 16)
            sp.dma_start(gla_gain[:, :], a["gla_norm"].to_broadcast([P, DV])).then_inc(consts_landed, 16)
            sp.dma_start(w_a2[:, :], a["w_a2"][0]).then_inc(consts_landed, 16)
            sp.dma_start(b_a[:, :], a["b_a"]).then_inc(consts_landed, 16)
            sp.wait_ge(cleared, 1)
            for which in range(2):
                for j in range(P // CMP_BLOCK):
                    sp.dma_start(cmp_w[j * CMP_BLOCK:(j + 1) * CMP_BLOCK, which, j:j + 1],
                                 a["cmp_pos_w"][0, which].rearrange("(c a) -> c a", a=1),
                                 allow_slow_non_contiguous=True).then_inc(consts_landed, 16)
            for i in range(TILES):
                r, n = ROWS[i], i % 2
                if i + 1 < TILES:
                    ring.wait_filled(sp, "x_T", i, 1)
                    sp.wait_ge(sq_x_ready, i + 1)
                    sp.dma_start(x_in[:ROWS[i + 1], :], x_rows(i + 1)).then_inc(x_landed, 16)
                sp.wait_ge(qk_normed, 4 * (i + 1))
                rows = outs[2] if i < PROMPT_TILES else outs[5]
                rows = rows.rearrange("l b t s h d -> (l b t) (s h d)")
                at = i * P if i < PROMPT_TILES else 0
                sp.dma_start(rows[at:at + r, :], proj[n][:r, KV0:KV0 + 512]).then_inc(rows_stored[n], 16)
                if SEQ - WINDOW <= i * P < SEQ:
                    at = i * P - (SEQ - WINDOW)
                    sp.dma_start(outs[3].rearrange("l b t s h d -> (l b t) (s h d)")[at:at + P, :],
                                 proj[n][:, KV0 + 512:KV0 + 768]).then_inc(rows_stored[n], 16)
            sp.wait_ge(state_ready, 4 * 2 * PROMPT_TILES)
            for h in range(GLA_HEADS):
                sp.dma_start(outs[4][0, 0, h], state[0][64 * (h % 2):64 * (h % 2) + 64, h // 2, h % 2, :]).then_inc(
                    state_stored, 16)
            sp.wait_ge(state_stored, 16 * GLA_HEADS)
            sp.wait_ge(rows_stored[0], 16 * 7)
            sp.wait_ge(rows_stored[1], 16 * 6)

        def rows_stored_before(i):
            return 16 * sum(1 + (SEQ - WINDOW <= j * P < SEQ) for j in range(i % 2, i, 2))

        @block.gpsimd
        def _(pool):
            nc.gpsimd.memset(cmp_w[:, :, :], 0.0).then_inc(cleared, 1)
            for table, pattern, base in ((slc_dist, [[1, SEQ]], P - SEQ), (win_dist, [[1, WINDOW + P]], -WINDOW),
                                         (cmp_dist, [[CMP_BLOCK, 2 * N_CMP - 4]],
                                          CMP_BLOCK - 1 - CMP_BLOCK * (N_CMP - 4))):
                nc.gpsimd.iota(table[:, :], pattern=pattern, base=base, channel_multiplier=-1,
                               allow_small_or_imprecise_dtypes=True).then_inc(tables_step, 1)
            for m in (cum_upto, cum_after):
                nc.gpsimd.memset(m[:, :], 1.0 / TAU).then_inc(tables_step, 1)
            pool.wait_ge(tables_step, 5)
            for table, pattern, base in ((slc_dist, [[-1, SEQ]], SEQ - P), (win_dist, [[-1, WINDOW + P]], WINDOW),
                                         (cmp_dist, [[-CMP_BLOCK, 2 * N_CMP - 4]],
                                          CMP_BLOCK * (N_CMP - 4) - CMP_BLOCK + 1)):
                nc.gpsimd.affine_select(out=table[:, :], in_=table[:, :], compare_op=ALU.is_ge, fill=MASKED,
                                        base=base, pattern=pattern, channel_multiplier=1).then_inc(tables_step, 1)
            nc.gpsimd.affine_select(out=cum_upto[:, :], in_=cum_upto[:, :], compare_op=ALU.is_ge, fill=0.0, base=0,
                                    pattern=[[1, P]], channel_multiplier=-1).then_inc(tables_step, 1)
            nc.gpsimd.affine_select(out=cum_after[:, :], in_=cum_after[:, :], compare_op=ALU.is_ge, fill=0.0,
                                    base=-1, pattern=[[-1, P]], channel_multiplier=1).then_inc(tables_step, 1)
            pool.wait_ge(tables_step, 10)
            nc.gpsimd.affine_select(out=win_dist[:, :], in_=win_dist[:, :], compare_op=ALU.is_ge, fill=MASKED,
                                    base=-1, pattern=[[1, WINDOW + P]], channel_multiplier=-1).then_inc(
                                        tables_step, 1)
            nc.gpsimd.memset(cum_from_mid[:, :], 0.0)
            nc.gpsimd.memset(in_chunk[:, :], 0.0)
            nc.gpsimd.memset(ones_row[:, :], 1.0)
            nc.gpsimd.memset(kc_T[:, :], 0.0)
            nc.gpsimd.memset(vc_T[:, :], 0.0)
            nc.gpsimd.memset(q_T[:, :, :], 0.0)
            nc.gpsimd.memset(q_mid_T[:, :, :, :], 0.0)
            nc.gpsimd.memset(att_T[:, :, :], 0.0)
            for c in range(2):
                nc.gpsimd.memset(k_last[c][:, :], 0.0)
                nc.gpsimd.memset(q_cum_T[c][:, :, :], 0.0)
                nc.gpsimd.memset(state[c][:, :, :, :], 0.0).then_inc(tables_step, 1)
            def rstd_of(mean, out, r, count, step, value, ready):
                nc.gpsimd.tensor_scalar(out, mean, 1.0 / count, EPS, ALU.mult, ALU.add).then_inc(step, 1)
                pool.wait_ge(step, value)
                nc.gpsimd.tensor_tensor(out, out, minus_half[:r, 0:out.shape[1]], ALU.pow).then_inc(ready, 1)

            def x_rstd(i):
                r = ROWS[i]
                pool.wait_ge(sq_x_ready, i + 1)
                rstd_of(mean_x[:r, i:i + 1], rstd_x[:r, i:i + 1], r, 1, rstd_x_ready, 2 * i + 1, rstd_x_ready)

            def qk_rstd(i):
                r = ROWS[i]
                pool.wait_ge(norm_mean_ready, i + 1)
                rstd_of(norm_mean[:r, :], norm_rstd[:r, :], r, HD, norm_rstd_ready, 2 * i + 1, norm_rstd_ready)

            def copy_v(i):
                v = proj[i % 2][:, KV0:KV0 + KV_COLS].rearrange("p (s c) -> p s c", s=6)
                ring.wait_evacuated(pool, "proj", i, 2)
                nc.gpsimd.tensor_copy(v_all[:, i, :, :], v[:, 3:6:2, :]).then_inc(v_copied, 1)

            def finish_gla(i):
                pool.wait_ge(o_mean_ready, i + 1)
                rstd_of(o_mean[:, :], o_rstd[:, :], P, 1, o_step, 5 * i + 1, o_step)
                pool.wait_ge(o_step, 5 * i + 2)
                o_rstd_wide = broadcast(o_rstd[:, :].rearrange("p (h a) -> p h a", a=1), [P, GLA_HEADS, DV])
                nc.gpsimd.tensor_tensor(o_gla[:, :, :], o_gla[:, :, :], o_rstd_wide, ALU.mult).then_inc(o_step, 1)
                pool.wait_ge(o_step, 5 * i + 3)
                nc.gpsimd.tensor_tensor(o_gla[:, :, :], o_gla[:, :, :],
                                        broadcast(gla_gain[:, :].rearrange("p (a e) -> p a e", a=1),
                                                  [P, GLA_HEADS, DV]), ALU.mult).then_inc(o_step, 1)
                pool.wait_ge(o_step, 5 * i + 4)
                pool.wait_ge(silu_ready, i + 1)
                nc.gpsimd.tensor_tensor(o_gla[:, :, :], o_gla[:, :, :],
                                        silu[:, :].rearrange("p (h e) -> p h e", h=GLA_HEADS),
                                        ALU.mult).then_inc(o_step, 1)
                pool.wait_ge(o_step, 5 * i + 5)
                if i:
                    pool.wait_ge(mix_stored, 16 * i)
                nc.gpsimd.tensor_tensor(mix[:, NSA_WIDTH:].rearrange("p (h e) -> p h e", h=GLA_HEADS),
                                        o_gla[:, :, :], proj[i % 2][:, GG0:GG0 + 512].rearrange(
                                            "p (h e) -> p h e", h=GLA_HEADS), ALU.mult).then_inc(mix_gla_ready, 1)
                pool.wait_ge(mix_gla_ready, i + 1)
                pool.wait_ge(combined, HEADS * 3 * (i + 1))
                pool.dma_start(mix_rows[i * P:(i + 1) * P, :], mix[:, :]).then_inc(mix_stored, 16)

            x_rstd(0)
            copy_v(0)
            qk_rstd(0)
            for i in range(PROMPT_TILES):
                pr = proj[i % 2]
                x_rstd(i + 1)
                pool.wait_ge(silu_exp, i + 1)
                nc.gpsimd.tensor_scalar(silu[:, :], silu[:, :], 1.0, None, ALU.add).then_inc(silu_step, 1)
                pool.wait_ge(soft_step, 2 * (i + 1))
                nc.gpsimd.tensor_tensor(log_a[:, :], z_min[:, :], log_a[:, :], ALU.subtract).then_inc(log_a_ready, 1)
                pool.wait_ge(exps_ready, 4 * (i + 1))
                gq = pr[:, GQ0:GQ0 + GLA_WIDTH]
                gk = pr[:, GK0:GK0 + GLA_WIDTH]
                nc.gpsimd.tensor_tensor(q_decayed[:, 1, :], q_decayed[:, 1, :], gq, ALU.mult).then_inc(
                    decayed_ready, 1)
                nc.gpsimd.tensor_tensor(k_mid[:, :], k_mid[:, :], gk, ALU.mult).then_inc(decayed_ready, 1)
                nc.gpsimd.tensor_tensor(q_decayed[:, 0, :], q_decayed[:, 0, :], gq, ALU.mult).then_inc(
                    decayed_ready, 1)
                if i + 1 < PROMPT_TILES:
                    copy_v(i + 1)
                qk_rstd(i + 1)
                finish_gla(i)
            pool.wait_ge(mix_stored, 16 * PROMPT_TILES)

        @block.tensor
        def _(pe):
            def project_x_T(i):
                r = ROWS[i]
                pe.wait_ge(x_landed, 16 * (i + 1))
                for half in range(2):
                    ring.wait_free(pe, "x_T", i, half)
                    for j in range(4):
                        k = 4 * half + j
                        last = nc.tensor.transpose(ring.bank("x_T", i, half)[:, j * r:(j + 1) * r],
                                                   x_in[:r, k * P:(k + 1) * P], identity[:r, :r])
                    last.then_inc(ring.is_filled("x_T", i, half), 1)

            def project(i, c):
                r = ROWS[i]
                at, cols = IN_CHUNKS[c]
                pe.wait_ge(h_T_ready, 2 * (i + 1))
                ring.wait_free(pe, "proj", i, c)
                for k in range(KT):
                    if i == 0 and c == 0:
                        pe.wait_ge(w_in_landed[k], 16)
                    last = nc.tensor.matmul(ring.bank("proj", i, c)[:r, :cols], h_T[:, k, :r],
                                            w_in[:, k, at:at + cols], start=(k == 0), stop=(k == KT - 1))
                last.then_inc(ring.is_filled("proj", i, c), 1)

            def transpose_qk(i):
                pr = proj[i % 2]
                pe.wait_ge(qk_normed, 4 * (i + 1))
                ring.wait_free(pe, "q_T", i)
                bank = ring.bank("q_T", i)
                for j in range(GROUP):
                    last = nc.tensor.transpose(bank[:, j * P:(j + 1) * P], q_paired[:, j * P:(j + 1) * P],
                                               identity[:, :])
                last.then_inc(ring.is_filled("q_T", i), 1)
                ring.wait_free(pe, "k_T", i)
                bank = ring.bank("k_T", i)
                for n, stream in enumerate((2, 4)):
                    at = KV0 + stream * P
                    nc.tensor.transpose(bank[:, n * P:(n + 1) * P], pr[:, at:at + P], identity[:, :])
                for which in range(2):
                    at = KV0 + which * P
                    last = nc.tensor.matmul(bank[:, 2 * P + 4 * which:2 * P + 4 * which + 4], pr[:, at:at + P],
                                            cmp_w[:, which, :], start=True, stop=True)
                last.then_inc(ring.is_filled("k_T", i), 1)
                ring.wait_evacuated(pe, "k_T", i)
                ring.wait_free(pe, "vc", i)
                nc.tensor.transpose(ring.bank("vc", i)[:N_CMP, :P], vc_T[:, :], identity[:, :]).then_inc(
                    ring.is_filled("vc", i), 1)

            def head_scores(i, h):
                n = i * HEADS + h
                if n:
                    pe.wait_ge(scores_read, 3 * n)
                if h == 0:
                    ring.wait_evacuated(pe, "q_T", i)
                q = q_T[:, h, :]
                for at in range(0, (i + 1) * P, BANK):
                    cols = min(BANK, (i + 1) * P - at)
                    nc.tensor.matmul(slc_ps[:, at:at + cols], q, k_T[0][:, at:at + cols], start=True, stop=True)
                first = max(0, i + 1 - WIN_TILES) * P
                span = (i + 1) * P - first
                for at in range(0, span, BANK):
                    cols = min(BANK, span - at)
                    nc.tensor.matmul(win_ps[:, at:at + cols], q, k_T[1][:, first + at:first + at + cols],
                                     start=True, stop=True)
                nc.tensor.matmul(win_ps[:, WINDOW + P:WINDOW + P + N_CMP], q, kc_T[:, :], start=True,
                                 stop=True).then_inc(scores_filled, 1)

            def head_values(i, h):
                n = i * HEADS + h
                kv = h // GROUP
                pe.wait_ge(probs_ready, 3 * (n + 1))
                groups = key_groups(i)
                if h == 0:
                    ring.wait_evacuated(pe, "vc", i)
                    pe.wait_ge(v_copied, i + 1)

                def values(g):
                    ring.wait_evacuated(pe, "probs_T", i, h, g)
                    for m, (_, keys, branch, j) in enumerate(groups[g]):
                        v = vc[:, kv * HD:(kv + 1) * HD] if branch == COMPRESSED else \
                            v_all[:, j, branch - 1, kv * HD:(kv + 1) * HD]
                        same = [t for t in key_tiles(i) if t[2] == branch]
                        last = nc.tensor.matmul(o_ps[:, branch * HD:(branch + 1) * HD],
                                                probs_T[group_no[i, h, g] % 3][:keys, m * P:(m + 1) * P], v,
                                                start=(j == same[0][3]), stop=(j == same[-1][3]))
                    last.then_inc(values_done, 1)

                for g, group in enumerate(groups):
                    ring.wait_free(pe, "probs_T", i, h, g)
                    for m, (at, keys, branch, j) in enumerate(group):
                        last = nc.tensor.transpose(ring.bank("probs_T", i, h, g)[:keys, m * P:(m + 1) * P],
                                                   scores[:, at:at + keys], identity[:, :])
                    last.then_inc(ring.is_filled("probs_T", i, h, g), 1)
                    if g == 0 and n:
                        pe.wait_ge(combined, 3 * n)
                    if g:
                        values(g - 1)
                values(len(groups) - 1)

            def gla_step(i, h):
                pr = proj[i % 2]
                if h == 0:
                    ring.wait_free(pe, "ga_T", i)
                    nc.tensor.transpose(ring.bank("ga_T", i)[:RANK, :P], pr[:, GA0:GA0 + RANK],
                                        identity[:, :]).then_inc(ring.is_filled("ga_T", i), 1)
                elif h == 1:
                    ring.wait_evacuated(pe, "ga_T", i)
                    ring.wait_free(pe, "z", i)
                    z = ring.bank("z", i)[:, :GLA_WIDTH]
                    nc.tensor.matmul(z, ga_T[:, :], w_a2[:, :], start=True, stop=False)
                    nc.tensor.matmul(z, ones_row[:, :], b_a[:, :], start=False, stop=True).then_inc(
                        ring.is_filled("z", i), 1)
                elif h == 2:
                    pe.wait_ge(log_a_ready, i + 1)
                    ring.wait_free(pe, "cum", i, 0)
                    bank = ring.bank("cum", i, 0)
                    nc.tensor.matmul(bank[:, :GLA_WIDTH], cum_upto[:, :], log_a[:, :], start=True, stop=True)
                    nc.tensor.matmul(bank[:, GLA_WIDTH:], cum_from_mid[:, :], log_a[:, :], start=True,
                                     stop=True).then_inc(ring.is_filled("cum", i, 0), 1)
                    ring.wait_free(pe, "cum", i, 1)
                    bank = ring.bank("cum", i, 1)
                    nc.tensor.matmul(bank[:, :GLA_WIDTH], cum_after[:, :], log_a[:, :], start=True, stop=True)
                    for pair in range(2):
                        last = nc.tensor.matmul(bank[:, GLA_WIDTH + 2 * pair:GLA_WIDTH + 2 * pair + 2],
                                                log_a[:, pair * P:(pair + 1) * P], in_chunk[:, :],
                                                start=True, stop=True)
                    last.then_inc(ring.is_filled("cum", i, 1), 1)
                elif h == 3:
                    pe.wait_ge(decayed_ready, 3 * (i + 1))
                    ring.wait_free(pe, "gla_T", i, 0)
                    bank = ring.bank("gla_T", i, 0)
                    for pair in range(2):
                        cols = slice(pair * P, (pair + 1) * P)
                        nc.tensor.transpose(bank[:, pair * P:(pair + 1) * P], q_decayed[:, 1, cols], identity[:, :])
                    for pair in range(2):
                        cols = slice(pair * P, (pair + 1) * P)
                        last = nc.tensor.transpose(bank[:, (2 + pair) * P:(3 + pair) * P], k_mid[:, cols],
                                                   identity[:, :])
                    last.then_inc(ring.is_filled("gla_T", i, 0), 1)
                    ring.wait_free(pe, "gla_T", i, 1)
                    bank = ring.bank("gla_T", i, 1)
                    for pair in range(2):
                        cols = slice(pair * P, (pair + 1) * P)
                        last = nc.tensor.transpose(bank[:, pair * P:(pair + 1) * P], q_decayed[:, 0, cols],
                                                   identity[:, :])
                    last.then_inc(ring.is_filled("gla_T", i, 1), 1)
                elif h == 4:
                    ring.wait_evacuated(pe, "gla_T", i, 0)
                    ring.wait_free(pe, "att", i)
                    for pair in range(2):
                        last = nc.tensor.matmul(ring.bank("att", i)[:, 2 * pair * P:2 * (pair + 1) * P],
                                                k_mid_T[:, pair, :],
                                                q_mid_T[:, pair, :, :].rearrange("p h t -> p (h t)"),
                                                start=True, stop=True)
                    last.then_inc(ring.is_filled("att", i), 1)
                elif h == 5:
                    gla_state(i, 0)
                elif h == 6:
                    pe.wait_ge(att_ready, i + 1)
                    ring.wait_evacuated(pe, "gla_T", i, 1)
                    ring.wait_evacuated(pe, "state", i, 0)
                    ring.wait_free(pe, "o", i)
                    bank = ring.bank("o", i)
                    for g in range(GLA_HEADS):
                        nc.tensor.matmul(bank[:, g * DV:(g + 1) * DV], att_T[:, g, :],
                                         pr[:, GV0 + g * DV:GV0 + (g + 1) * DV], start=(g == 0), stop=False,
                                         skip_group_check=True)
                    for c in range(2):
                        for pair in range(2):
                            last = nc.tensor.matmul(bank[:, 2 * pair * DV:2 * (pair + 1) * DV],
                                                    q_cum_T[c][:, pair, :],
                                                    state[c][:, pair, :, :].rearrange("p h e -> p (h e)"),
                                                    start=False, stop=(c == 1), skip_group_check=True)
                    last.then_inc(ring.is_filled("o", i), 1)
                elif h == 7:
                    gla_state(i, 1)

            def gla_state(i, c):
                pe.wait_ge(k_last_ready, 2 * (i + 1))
                ring.wait_free(pe, "state", i, c)
                for pair in range(2):
                    last = nc.tensor.matmul(ring.bank("state", i, c)[:, 2 * pair * DV:2 * (pair + 1) * DV],
                                            k_last[c][:, pair * P:(pair + 1) * P],
                                            proj[i % 2][:, GV0 + 2 * pair * DV:GV0 + 2 * (pair + 1) * DV],
                                            start=True, stop=True)
                last.then_inc(ring.is_filled("state", i, c), 1)

            project_x_T(0)
            for c in range(6):
                project(0, c)
            pe.wait_ge(tables_ready, 1)
            pe.wait_ge(consts_landed, 16 * CONSTS)
            for i in range(PROMPT_TILES):
                transpose_qk(i)
                for h in range(HEADS):
                    head_scores(i, h)
                    if h == 0:
                        project_x_T(i + 1)
                    elif h <= 6:
                        project(i + 1, h - 1)
                    gla_step(i, h)
                    head_values(i, h)

        @block.scalar
        def _(act):
            def square_x(i):
                r = ROWS[i]
                act.wait_ge(x_landed, 16 * (i + 1))
                if i:
                    ring.wait_filled(act, "proj", i - 1, 5)
                nc.scalar.activation(h_T[:r, :, :].rearrange("p k t -> p (k t)"), x_in[:r, :], ACT.Square,
                                     scale=D_MODEL ** -0.5, accum_out=mean_x[:r, i:i + 1]).then_inc(sq_x_ready, 1)

            def take_projection(i, c):
                r, n = ROWS[i], i % 2
                at, cols = IN_CHUNKS[c]
                act.wait_ge(rstd_x_ready, 2 * (i + 1))
                if i >= 2 and c == 0:
                    act.wait_ge(rows_stored[n], rows_stored_before(i))
                    act.wait_ge(v_copied, i - 1)
                    act.wait_ge(mix_gla_ready, i - 1)
                    ring.wait_filled(act, "state", i - 2, 1)
                ring.wait_filled(act, "proj", i, c)
                nc.scalar.activation(proj[n][:r, at:at + cols], ring.bank("proj", i, c)[:r, :cols], ACT.Copy,
                                     scale=rstd_x[:r, i:i + 1]).then_inc(ring.is_evacuated("proj", i, c), 1)

            def gate_exponentials(i):
                r = ROWS[i]
                if i >= 2:
                    act.wait_ge(combined, 3 * HEADS * (i - 1))
                ring.wait_evacuated(act, "proj", i, 2)
                nc.scalar.activation(gates[i % 2][:r, :], proj[i % 2][:r, GATE0:GATE0 + 3 * HEADS], ACT.Exp,
                                     scale=-1.0).then_inc(gate_exp, 1)

            def take_qk_T(i):
                if i:
                    act.wait_ge(scores_filled, HEADS * i)
                else:
                    act.wait_ge(tables_ready, 1)
                ring.wait_filled(act, "q_T", i)
                bank = ring.bank("q_T", i)
                for kv in range(KV_HEADS):
                    rows = slice(kv * HD, (kv + 1) * HD)
                    last = nc.scalar.activation(q_T[rows, kv * GROUP:(kv + 1) * GROUP, :],
                                                bank[rows, :].rearrange("p (g t) -> p g t", g=GROUP), ACT.Copy)
                last.then_inc(ring.is_evacuated("q_T", i), 1)

            def exponentials(i, h):
                n = i * HEADS + h
                act.wait_ge(neg_max_ready, n + 1)
                if n:
                    act.wait_ge(combined, 3 * n)
                for branch, (at, cols) in enumerate(branch_columns(i)):
                    nc.scalar.activation(scores[:, at:at + cols], scores[:, at:at + cols], ACT.Exp,
                                         bias=neg_max[:, branch:branch + 1],
                                         accum_out=sums[:, branch:branch + 1]).then_inc(probs_ready, 1)

            def gla_step(i, h):
                if h == 0:
                    ring.wait_filled(act, "ga_T", i)
                    nc.scalar.activation(ga_T[:, :], ring.bank("ga_T", i)[:RANK, :P], ACT.Copy).then_inc(
                        ring.is_evacuated("ga_T", i), 1)
                    if i:
                        act.wait_ge(mix_gla_ready, i)
                    nc.scalar.activation(silu[:, :], proj[i % 2][:, GG0:GG0 + GLA_HEADS * DV], ACT.Exp,
                                         scale=-1.0).then_inc(silu_exp, 1)
                elif h == 1:
                    act.wait_ge(abs_ready, i + 1)
                    nc.scalar.activation(log_a[:, :], log_a[:, :], ACT.Exp).then_inc(soft_step, 1)
                    act.wait_ge(soft_step, 2 * i + 1)
                    nc.scalar.activation(log_a[:, :], log_a[:, :], ACT.Ln, bias=1.0).then_inc(soft_step, 1)
                elif h == 2:
                    if i:
                        ring.wait_filled(act, "gla_T", i - 1, 1)
                        act.wait_ge(k_last_ready, 2 * i)
                    ring.wait_filled(act, "cum", i, 0)
                    bank = ring.bank("cum", i, 0)
                    nc.scalar.activation(q_decayed[:, :, :].rearrange("p a c -> p (a c)"), bank[:, :],
                                         ACT.Exp).then_inc(exps_ready, 1)
                    act.wait_ge(exps_ready, 4 * i + 1)
                    nc.scalar.activation(k_mid[:, :], bank[:, GLA_WIDTH:], ACT.Exp, scale=-1.0).then_inc(
                        ring.is_evacuated("cum", i, 0), 1)
                    ring.wait_evacuated(act, "cum", i, 0)
                    act.sem_inc(exps_ready, 1)
                    if i:
                        act.wait_ge(state_ready, 8 * i)
                    ring.wait_filled(act, "cum", i, 1)
                    bank = ring.bank("cum", i, 1)
                    nc.scalar.activation(k_decay[:, :], bank[:, :GLA_WIDTH], ACT.Exp).then_inc(exps_ready, 1)
                    nc.scalar.activation(decay[:, :, :].rearrange("p a c -> p (a c)"),
                                         bank[:, GLA_WIDTH:GLA_WIDTH + 4], ACT.Exp).then_inc(
                                             ring.is_evacuated("cum", i, 1), 1)
                    ring.wait_evacuated(act, "cum", i, 1)
                    act.sem_inc(exps_ready, 1)
                elif h == 3:
                    if i:
                        ring.wait_filled(act, "o", i - 1)
                    ring.wait_filled(act, "gla_T", i, 0)
                    bank = ring.bank("gla_T", i, 0)
                    for head in range(2):
                        rows = slice(head * DK, (head + 1) * DK)
                        nc.scalar.activation(q_mid_T[rows, :, head, :],
                                             bank[rows, :2 * P].rearrange("p (a t) -> p a t", a=2), ACT.Copy,
                                             scale=DK ** -0.5)
                    nc.scalar.activation(k_mid_T[:, :, :].rearrange("p a t -> p (a t)"), bank[:, 2 * P:],
                                         ACT.Copy).then_inc(ring.is_evacuated("gla_T", i, 0), 1)
                    ring.wait_filled(act, "gla_T", i, 1)
                    bank = ring.bank("gla_T", i, 1)
                    for c in range(2):
                        cols = slice(c * CHUNK, (c + 1) * CHUNK)
                        last = nc.scalar.activation(q_cum_T[c][:, :, cols],
                                                    bank[:, :2 * P].rearrange("p (a t) -> p a t", a=2)[:, :, cols],
                                                    ACT.Copy, scale=DK ** -0.5)
                    last.then_inc(ring.is_evacuated("gla_T", i, 1), 1)
                elif h == 6:
                    if i:
                        act.wait_ge(mix_gla_ready, i)
                    ring.wait_filled(act, "o", i)
                    nc.scalar.activation(o_gla[:, :, :].rearrange("p h e -> p (h e)"), ring.bank("o", i)[:, :],
                                         ACT.Copy).then_inc(ring.is_evacuated("o", i), 1)
                elif h == 7:
                    ring.wait_evacuated(act, "o", i)
                    if i:
                        act.wait_ge(o_mean_ready, i)
                    for g in range(GLA_HEADS):
                        last = nc.scalar.activation(norm_scratch[:, g, :], o_gla[:, g, :], ACT.Square,
                                                    scale=DV ** -0.5, accum_out=o_mean[:, g:g + 1])
                    last.then_inc(o_mean_ready, 1)

            square_x(0)
            for c in range(6):
                take_projection(0, c)
            gate_exponentials(0)
            for i in range(PROMPT_TILES):
                take_qk_T(i)
                for h in range(HEADS):
                    exponentials(i, h)
                    if h == 0:
                        square_x(i + 1)
                    elif h <= 6:
                        take_projection(i + 1, h - 1)
                    if h == 5:
                        gate_exponentials(i + 1)
                    gla_step(i, h)
                    take_probs_T(act, nc.scalar, i, h, 0)

        @block.vector
        def _(dve):
            def take_x_T(i):
                r = ROWS[i]
                dve.wait_ge(sq_x_ready, i + 1)
                for half in range(2):
                    ring.wait_filled(dve, "x_T", i, half)
                    ln = broadcast(ln_col[:, 4 * half:4 * half + 4].rearrange("p (k a) -> p k a", a=1), [P, 4, r])
                    nc.vector.tensor_tensor(h_T[:, 4 * half:4 * half + 4, :r],
                                            ring.bank("x_T", i, half)[:, :4 * r].rearrange("p (k t) -> p k t", k=4),
                                            ln, ALU.mult).then_inc(ring.is_evacuated("x_T", i, half), 1)
                    ring.wait_evacuated(dve, "x_T", i, half)
                    dve.sem_inc(h_T_ready, 1)

            def norm_sums(i):
                r = ROWS[i]
                pr = proj[i % 2]
                ring.wait_evacuated(dve, "proj", i, 0)
                if i:
                    dve.wait_ge(norm_step, 4 * i)
                q = pr[:r, Q0:Q0 + NSA_WIDTH]
                nc.vector.tensor_tensor(norm_sq[:r, :], q, q, ALU.mult).then_inc(norm_step, 1)
                dve.wait_ge(norm_step, 4 * i + 1)
                nc.vector.tensor_reduce(norm_mean[:r, 0:8], norm_sq[:r, :].rearrange("p (h d) -> p h d", d=HD),
                                        AX.X, ALU.add).then_inc(norm_step, 1)
                ring.wait_evacuated(dve, "proj", i, 1)
                ring.wait_evacuated(dve, "proj", i, 2)
                dve.wait_ge(norm_step, 4 * i + 2)
                k = pr[:r, KV0:KV0 + KV_COLS].rearrange("p (s c) -> p s c", s=6)[:, 0:6:2, :]
                sq = norm_sq[:r, 0:3 * P].rearrange("p (s c) -> p s c", s=3)
                nc.vector.tensor_tensor(sq, k, k, ALU.mult).then_inc(norm_step, 1)
                dve.wait_ge(norm_step, 4 * i + 3)
                nc.vector.tensor_reduce(norm_mean[:r, 8:14], norm_sq[:r, 0:3 * P].rearrange("p (h d) -> p h d", d=HD),
                                        AX.X, ALU.add).then_inc(norm_step, 1)
                dve.wait_ge(norm_step, 4 * i + 4)
                dve.sem_inc(norm_mean_ready, 1)

            def apply_norms(i):
                r = ROWS[i]
                pr = proj[i % 2]
                q = pr[:r, Q0:Q0 + NSA_WIDTH].rearrange("p (h d) -> p h d", d=HD)
                dve.wait_ge(norm_rstd_ready, 2 * (i + 1))
                nc.vector.tensor_tensor(q, q, broadcast(norm_rstd[:r, 0:8].rearrange("p (h a) -> p h a", a=1),
                                                        [r, HEADS, HD]), ALU.mult).then_inc(qk_normed, 1)
                k = pr[:r, KV0:KV0 + KV_COLS].rearrange("p (s c) -> p s c", s=6)[:, 0:6:2, :]
                k4 = k.rearrange("p s (h d) -> p s h d", d=HD)
                r4 = norm_rstd[:r, 8:14].rearrange("p (s h a) -> p s h a", s=3, a=1)
                nc.vector.tensor_tensor(k4, k4, broadcast(r4, [r, 3, KV_HEADS, HD]), ALU.mult).then_inc(qk_normed, 1)
                dve.wait_ge(qk_normed, 4 * i + 2)
                if i:
                    ring.wait_filled(dve, "q_T", i - 1)
                nc.vector.tensor_tensor(
                    q_paired[:r, :].rearrange("p (g k d) -> p k g d", g=GROUP, k=KV_HEADS),
                    pr[:r, Q0:Q0 + NSA_WIDTH].rearrange("p (k g d) -> p k g d", k=KV_HEADS, g=GROUP),
                    q_gain[:r, :, :].rearrange("p (k g) d -> p k g d", k=KV_HEADS), ALU.mult).then_inc(qk_normed, 1)
                g4 = k_gain[:r, :, :].rearrange("p s (a d) -> p s a d", a=1)
                nc.vector.tensor_tensor(k4, k4, broadcast(g4, [r, 3, KV_HEADS, HD]), ALU.mult).then_inc(qk_normed, 1)
                g = gates[i % 2][:r, :]
                dve.wait_ge(gate_exp, i + 1)
                nc.vector.tensor_scalar(g, g, 1.0, None, ALU.add).then_inc(gates_ready, 1)
                dve.wait_ge(gates_ready, 2 * i + 1)
                nc.vector.reciprocal(g, g).then_inc(gates_ready, 1)

            def take_kc(i):
                ring.wait_filled(dve, "k_T", i)
                bank = ring.bank("k_T", i)
                blocks = slice(4 * i, 4 * i + 4)
                for n in range(2):
                    nc.vector.tensor_copy(k_T[n][:, i * P:(i + 1) * P], bank[:, n * P:(n + 1) * P])
                if i:
                    dve.wait_ge(scores_filled, HEADS * i)
                nc.vector.tensor_copy(kc_T[:, blocks], bank[:, 2 * P:2 * P + 4])
                nc.vector.tensor_copy(vc_T[:, blocks], bank[:, 2 * P + 4:2 * P + 8]).then_inc(
                    ring.is_evacuated("k_T", i), 1)
                ring.wait_filled(dve, "vc", i)
                if i:
                    dve.wait_ge(values_done, last_group[i - 1, HEADS - 1] + 1)
                nc.vector.tensor_copy(vc[:, :], ring.bank("vc", i)[:N_CMP, :P]).then_inc(
                    ring.is_evacuated("vc", i), 1)

            def bias_and_max(i, h):
                n = i * HEADS + h
                dve.wait_ge(scores_filled, n + 1)
                if n:
                    prev = (i, h - 1) if h else (i - 1, HEADS - 1)
                    ring.wait_filled(dve, "probs_T", *prev, len(key_groups(prev[0])) - 1)
                first = max(0, i + 1 - WIN_TILES)
                span = (i + 1 - first) * P
                for branch, (at, cols, ps, dist) in enumerate((
                        (CMP_AT, N_CMP, win_ps[:, WINDOW + P:WINDOW + P + N_CMP],
                         cmp_dist[:, N_CMP - 4 - 4 * i:2 * N_CMP - 4 - 4 * i]),
                        (SLC_AT, (i + 1) * P, slc_ps[:, 0:(i + 1) * P], slc_dist[:, SEQ - (i + 1) * P:]),
                        (WIN_AT, span, win_ps[:, 0:span], win_dist[:, WINDOW + P - span:]))):
                    nc.vector.tensor_tensor_reduce(out=scores[:, at:at + cols], in0=ps, in1=dist, scale=SLOPES[h],
                                                   scalar=MASKED, op0=ALU.add, op1=ALU.max,
                                                   accum_out=maxima[:, branch:branch + 1]).then_inc(scores_read, 1)
                dve.wait_ge(scores_read, 3 * (n + 1))
                nc.vector.tensor_scalar(neg_max[:, :], maxima[:, :], -1.0, 1e26, ALU.mult, ALU.min).then_inc(
                    neg_max_ready, 1)

            def combine(i, h):
                n = i * HEADS + h
                dve.wait_ge(probs_ready, 3 * (n + 1))
                nc.vector.tensor_scalar(weight[:, :], sums[:, :], 1e-30, None, ALU.max).then_inc(weight_step, 1)
                dve.wait_ge(weight_step, 3 * n + 1)
                nc.vector.reciprocal(weight[:, :], weight[:, :]).then_inc(weight_step, 1)
                dve.wait_ge(weight_step, 3 * n + 2)
                dve.wait_ge(gates_ready, 2 * (i + 1))
                nc.vector.tensor_tensor(weight[:, :], weight[:, :],
                                        gates[i % 2][:, :].rearrange("p (b h) -> p b h", b=3)[:, :, h],
                                        ALU.mult).then_inc(weight_step, 1)
                dve.wait_ge(weight_step, 3 * n + 3)
                dve.wait_ge(values_done, last_group[i, h] + 1)
                if h == 0 and i:
                    dve.wait_ge(mix_stored, 16 * i)
                out = mix[:, h * HD:(h + 1) * HD]
                nc.vector.tensor_scalar(out, o_ps[:, 0:HD], weight[:, 0:1], None, ALU.mult).then_inc(combined, 1)
                for branch in (1, 2):
                    dve.wait_ge(combined, 3 * n + branch)
                    nc.vector.scalar_tensor_tensor(out=out, in0=o_ps[:, branch * HD:(branch + 1) * HD],
                                                   scalar=weight[:, branch:branch + 1], in1=out, op0=ALU.mult,
                                                   op1=ALU.add).then_inc(combined, 1)

            def gla_step(i, h):
                if h == 0:
                    dve.wait_ge(silu_step, 2 * i + 1)
                    nc.vector.reciprocal(silu[:, :], silu[:, :]).then_inc(silu_step, 1)
                    dve.wait_ge(silu_step, 2 * i + 2)
                    dve.sem_inc(silu_ready, 1)
                elif h == 1:
                    if i:
                        dve.wait_ge(log_a_ready, i)
                        ring.wait_filled(dve, "cum", i - 1, 1)
                    ring.wait_filled(dve, "z", i)
                    z = ring.bank("z", i)[:, :GLA_WIDTH]
                    nc.vector.tensor_scalar(z_min[:, :], z, 0.0, None, ALU.min).then_inc(abs_step, 1)
                    dve.wait_ge(abs_step, i + 1)
                    nc.vector.scalar_tensor_tensor(out=log_a[:, :], in0=z, scalar=-1.0, in1=z_min[:, :],
                                                   op0=ALU.mult, op1=ALU.min).then_inc(ring.is_evacuated("z", i), 1)
                    ring.wait_evacuated(dve, "z", i)
                    dve.sem_inc(abs_ready, 1)
                elif h == 4:
                    if i:
                        ring.wait_filled(dve, "o", i - 1)
                    else:
                        dve.wait_ge(tables_ready, 1)
                    ring.wait_filled(dve, "att", i)
                    keep = broadcast(cum_upto[:, :].bitcast(U32).rearrange("p (a t) -> p a t", a=1),
                                     [P, GLA_HEADS, P])
                    nc.vector.copy_predicated(att_T[:, :, :], keep,
                                              ring.bank("att", i)[:, :].rearrange("p (h t) -> p h t", h=GLA_HEADS)
                                              ).then_inc(ring.is_evacuated("att", i), 1)
                    ring.wait_evacuated(dve, "att", i)
                    dve.sem_inc(att_ready, 1)
                elif h == 2:
                    if i:
                        ring.wait_filled(dve, "state", i - 1, 1)
                    dve.wait_ge(exps_ready, 4 * (i + 1))
                    for c in range(2):
                        rows = slice(c * CHUNK, (c + 1) * CHUNK)
                        nc.vector.tensor_tensor(k_last[c][rows, :], k_decay[rows, :],
                                                proj[i % 2][rows, GK0:GK0 + GLA_WIDTH], ALU.mult).then_inc(
                                                    k_last_ready, 1)
                elif h == 5:
                    update_state(i, 0)
                elif h == 7:
                    update_state(i, 1)

            def update_state(i, c):
                dve.wait_ge(exps_ready, 4 * (i + 1))
                if c == 1:
                    ring.wait_filled(dve, "o", i)
                elif i:
                    ring.wait_filled(dve, "o", i - 1)
                dve.wait_ge(state_ready, 4 * (2 * i + c)) if (i or c) else None
                ring.wait_filled(dve, "state", i, c)
                bank = ring.bank("state", i, c)[:, :].rearrange("p (a h e) -> p a h e", a=2, h=2)
                for pair in range(2):
                    for head in range(2):
                        rows = slice(head * DK, (head + 1) * DK)
                        last = nc.vector.scalar_tensor_tensor(
                            out=state[1 - c][rows, pair, head, :], in0=state[c][rows, pair, head, :],
                            scalar=decay[rows, pair, c:c + 1], in1=bank[rows, pair, head, :],
                            op0=ALU.mult, op1=ALU.add).then_inc(
                                state_ready if (pair, head) != (1, 1) else ring.is_evacuated("state", i, c), 1)
                ring.wait_evacuated(dve, "state", i, c)
                dve.sem_inc(state_ready, 1)

            dve.wait_ge(consts_landed, 16 * CONSTS)
            dve.wait_ge(tables_step, 13)
            nc.vector.memset(cum_upto[0:CHUNK, CHUNK:P], 0.0)
            nc.vector.memset(cum_after[CHUNK:P, 0:CHUNK], 0.0)
            for c in range(2):
                s0 = c * CHUNK
                nc.vector.memset(in_chunk[s0:s0 + CHUNK, c:c + 1], 1.0 / TAU)
                nc.vector.memset(cum_from_mid[s0:s0 + CHUNK // 2, s0:s0 + CHUNK], 1.0 / TAU).then_inc(dve_tables, 1)
            dve.wait_ge(dve_tables, 2)
            nc.vector.tensor_tensor(cum_from_mid[:, :], cum_upto[:, :], cum_from_mid[:, :],
                                    ALU.subtract).then_inc(tables_ready, 1)
            for h in range(HEADS):
                last = nc.vector.tensor_scalar(q_gain[:, h, :], q_gain[:, h, :], SCALE / SLOPES[h], None, ALU.mult)
            last.then_inc(gain_ready, 1)
            dve.wait_ge(gain_ready, 1)
            take_x_T(0)
            norm_sums(0)
            apply_norms(0)
            for i in range(PROMPT_TILES):
                take_kc(i)
                for h in range(HEADS):
                    bias_and_max(i, h)
                    if h == 0:
                        take_x_T(i + 1)
                    elif h == 5:
                        norm_sums(i + 1)
                    elif h == 6:
                        apply_norms(i + 1)
                    gla_step(i, h)
                    take_probs_T(dve, nc.vector, i, h, 1)
                    combine(i, h)


PAIRS = DEC_BATCH // 2
PAIR_ROWS = 2 * HEADS * DEC_SEQ
B_ROWS = HEADS * DEC_SEQ
PAGE_GROUP = 4
GROUPS = N_PAGES // PAGE_GROUP
KEYS = PAST_LEN + DEC_SEQ
N_SEL = -(-KEYS // SEL_BLOCK)
PAST_CMP = PAST_LEN // CMP_BLOCK
FORCE_SCORE = 1e4
RECENT = WINDOW + DEC_SEQ

NEG_T = 0
SLOPE = 1
NEG_SLOPE = 2
NEW_DIST = 3
WIN_OLD = NEW_DIST + DEC_SEQ
GROUP_SUM = WIN_OLD + DEC_SEQ
UPTO = GROUP_SUM + P
AFTER = UPTO + SAMPLE_ROWS
OF_SAMPLE = AFTER + SAMPLE_ROWS
IS_SAMPLE = OF_SAMPLE + DEC_BATCH
CONST_COLS = IS_SAMPLE + DEC_BATCH


def sample_constants():
    import numpy as np

    out = np.zeros((P, CONST_COLS), np.float32)
    row = np.arange(P)
    t = row % DEC_SEQ
    head = row // DEC_SEQ % HEADS
    out[:, NEG_T] = -t
    out[:, SLOPE] = np.array(SLOPES)[head]
    out[:, NEG_SLOPE] = -out[:, SLOPE]
    j = np.arange(DEC_SEQ)
    out[:, NEW_DIST:NEW_DIST + DEC_SEQ] = np.where(j <= t[:, None], j - t[:, None], MASKED)
    out[:, WIN_OLD:WIN_OLD + DEC_SEQ] = np.where(j > t[:, None], j - WINDOW - t[:, None], MASKED)
    kv = row // (GROUP * DEC_SEQ)
    out[:, GROUP_SUM:GROUP_SUM + P] = (kv[:, None] == kv) & (t[:, None] == t)
    s = np.arange(SAMPLE_ROWS)
    same = (s[:, None] // DEC_SEQ) == (s // DEC_SEQ)
    out[:SAMPLE_ROWS, UPTO:UPTO + SAMPLE_ROWS] = (same & (s[:, None] <= s)) / TAU
    out[:SAMPLE_ROWS, AFTER:AFTER + SAMPLE_ROWS] = (same & (s[:, None] > s)) / TAU
    mine = (s[:, None] // DEC_SEQ) == np.arange(DEC_BATCH)
    out[:SAMPLE_ROWS, OF_SAMPLE:OF_SAMPLE + DEC_BATCH] = mine / TAU
    out[:SAMPLE_ROWS, IS_SAMPLE:IS_SAMPLE + DEC_BATCH] = mine
    return out


def samples_stage(nc, a, outs, mix_rows, shared):
    proj, q_paired, identity = shared.proj0, shared.q_paired, shared.identity
    R = SAMPLE_ROWS
    branch_rows = nc.dram_tensor("branch_rows", (DEC_BATCH, KV_HEADS, GROUP, DEC_SEQ, 3, HD), F32,
                                 kind="Internal").ap()
    with ExitStack() as ctx:
        def sb(name, shape, dtype=F32):
            return ctx.enter_context(nc.sbuf_tensor(name, shape, dtype))

        sem = ctx.enter_context(stage_semaphores(nc, "samples"))

        consts = sb("sample_consts_sb", [P, CONST_COLS])
        pages = sb("page_numbers", [1, DEC_BATCH * N_PAGES], I32)
        slc_dist = sb("past_dist", [P, PAST_LEN])
        cmp_dist = sb("past_cmp_dist", [P, PAST_CMP])
        win_dist = sb("past_win_dist", [P, WINDOW])
        page = sb("pages", [P, 2 * PAGE_GROUP, 4 * KV_HEADS * HD])
        page_k_T = [sb(f"page_k_T{n}", [P, BANK]) for n in range(2)]
        values = [sb(f"values{n}", [P, 2, N_PAGES, KV_HEADS * HD]) for n in range(2)]
        kc_T = [sb(f"past_kc_T{n}", [P, 2, PAST_CMP]) for n in range(2)]
        vc_T = [sb(f"past_vc_T{n}", [P, 2, PAST_CMP]) for n in range(2)]
        vc = sb("past_vc", [P, 2, KV_HEADS * HD])
        slc = [sb(f"slc_scores{n}", [P, KEYS]) for n in range(2)]
        win = sb("win_scores", [P, RECENT])
        cmp = sb("cmp_scores", [P, PAST_CMP])
        win_kv = sb("win_kv", [P, 2, WINDOW // P, 2 * KV_HEADS * HD])
        win_k_T = sb("win_k_T", [P, 2, WINDOW])
        q_T = sb("sample_q_T", [P, DEC_BATCH, KV_HEADS, GROUP, DEC_SEQ])
        new_k_T = sb("new_k_T", [P, 2, SAMPLE_ROWS])
        new_v = sb("new_v", [DEC_SEQ, 2, DEC_BATCH, KV_HEADS * HD])
        probs_T = [sb(f"sample_probs_T{n}", [P, BANK]) for n in range(3)]
        maxima = sb("sample_maxima", [P, 4])
        neg_max = sb("sample_neg_max", [P, 3])
        sums = sb("sample_sums", [P, 3])
        weight = sb("sample_weight", [P, 3])
        ranking = sb("ranking", [P, N_SEL])
        top8 = sb("top8", [P, 8])
        unselected = sb("unselected", [P, N_SEL])
        branch_out = sb("branch_out", [P, 3, KV_HEADS * HD])
        mix = sb("sample_mix", [R, D_MODEL])
        ga_T = sb("sample_ga_T", [RANK, R])
        z_min = sb("sample_z_min", [R, GLA_WIDTH])
        log_a = sb("sample_log_a", [R, GLA_WIDTH])
        q_cum = sb("sample_q_cum", [R, GLA_WIDTH])
        k_cum = sb("sample_k_cum", [R, GLA_WIDTH])
        k_last = sb("sample_k_last", [R, GLA_WIDTH])
        decay = sb("sample_decay", [P, 2, DEC_BATCH])
        o_gla = sb("sample_o_gla", [R, GLA_HEADS, DV])
        o_mean = sb("sample_o_mean", [R, GLA_HEADS])
        o_rstd = sb("sample_o_rstd", [R, GLA_HEADS])
        silu = sb("sample_silu", [R, GLA_HEADS * DV])
        k_own = slc[1][:R, 0:DEC_BATCH * GLA_WIDTH].rearrange("p (b c) -> p b c", b=DEC_BATCH)
        at = DEC_BATCH * GLA_WIDTH
        q_own_T = slc[1][:, at:at + 2 * DEC_BATCH * (R + DEC_SEQ)].rearrange("p (a b t) -> p a b t", a=2, b=DEC_BATCH)
        at += 2 * DEC_BATCH * (R + DEC_SEQ)
        q_pair_T = slc[1][:, at:at + 4 * R].rearrange("p (a h t) -> p a h t", a=2, h=2)
        k_cum_T = slc[1][:, at + 4 * R:at + 6 * R].rearrange("p (a t) -> p a t", a=2)
        att_T = slc[1][:R, at + 6 * R:at + 10 * R].rearrange("p (h t) -> p h t", h=GLA_HEADS)
        squares = mix[:, 0:GLA_HEADS * DV].rearrange("p (h e) -> p h e", h=GLA_HEADS)
        branches = page[:R, 0:3, :]
        state = values[1][:, 0, :, :].rearrange("p n c -> p (n c)").rearrange(
            "p (a b h e) -> p a b h e", a=2, b=DEC_BATCH, h=2)

        consts_landed = sem("sample_consts_landed")
        pages_landed = sem("page_numbers_landed")
        page_landed = [sem(f"page_landed{n}") for n in range(2 * PAGE_GROUP)]
        state_cleared = sem("state_cleared")
        state_landed = sem("gla_state_landed")
        rows_out = sem("sample_rows_out")
        new_v_landed = sem("new_v_landed")
        win_landed = sem("win_kv_landed")
        tables_step = sem("sample_tables_step")
        tables_ready = sem("sample_tables_ready")
        pages_read = sem("pages_read")
        values_copied = sem("values_copied")
        setup_T = sem("setup_T_ready")
        cmp_T_filled = sem("cmp_T_filled")
        cmp_T_ready = sem("cmp_T_ready")
        scores_ready = sem("sample_scores_ready")
        dve_step = sem("sample_dve_step")
        neg_max_ready = sem("sample_neg_max_ready")
        probs_ready = sem("sample_probs_ready")
        cmp_normed = sem("cmp_probs_normed")
        values_done = sem("sample_values_done")
        branch_taken = sem("branch_taken")
        branch_stored = sem("branch_stored")
        branch_back = sem("branches_landed")
        mix_ready = sem("sample_mix_ready")
        mix_out = sem("sample_mix_out")
        soft_step = sem("sample_soft_step")
        abs_ready = sem("sample_abs_ready")
        log_a_ready = sem("sample_log_a_ready")
        exps_ready = sem("sample_exps_ready")
        decayed_ready = sem("sample_decayed_ready")
        k_own_ready = sem("k_own_ready")
        att_ready = sem("sample_att_ready")
        silu_step = sem("sample_silu_step")
        state_step = sem("sample_state_step")
        state_out = sem("sample_state_out")
        o_mean_ready = sem("sample_o_mean_ready")
        o_step = sem("sample_o_step")

        cmp_T_ps = ctx.enter_context(nc.psum_tensor("cmp_T_ps", [P, 2, PAST_CMP], F32))
        slc_out = ctx.enter_context(nc.psum_tensor("slc_out", [P, BANK], F32))
        short_out = ctx.enter_context(nc.psum_tensor("short_out", [P, BANK], F32))

        KEY_TILES = N_PAGES + 1
        SLC_TURNS = -(-KEY_TILES // 4)
        TAIL = [[("cmp",), ("new",)], [("win_k", 0), ("win_k", 1)], [("imp",), ("cmp_T",)],
                [("win", 0), ("win", 1)], [], [], [("win_T", 0), ("win_T", 1)]] + [
                    [("slc_T", g)] for g in range(SLC_TURNS)]
        GLA = [[("ga_T",)], [("z",)], [("cum",), ("decay",)], [("gla_T",)], [("att",)], [("o",)]] + [
            [("state", b)] for b in range(DEC_BATCH)]
        SLOTS = 2 * GROUPS
        assert len(TAIL) == SLOTS and len(GLA) <= SLOTS
        order = [("q_T",), ("new_k_T",)]
        for pair in range(PAIRS + 1):
            for slot in range(SLOTS):
                if pair < PAIRS:
                    order += [("page_T", pair, slot), ("page_scores", pair, slot)]
                if pair:
                    order += [(key[0], pair - 1, *key[1:]) for key in TAIL[slot]]
                elif slot < len(GLA):
                    order += GLA[slot]
        ring = turns(nc, ctx, sem, "sample_bank", 5, order)
        places = {}
        for pair in range(PAIRS):
            for key in [("cmp_T",), ("win_T", 0), ("win_T", 1)] + [("slc_T", g) for g in range(SLC_TURNS)]:
                places[(key[0], pair, *key[1:])] = len(places)
        N_PLACES_PER_PAIR = 3 + SLC_TURNS

        block = ctx.enter_context(nc.Block())
        samples = [2 * pair + b for pair in range(PAIRS) for b in range(2)]

        @block.sync
        def _(sp):
            sp.dma_start(pages[:, :], a["page_table"].rearrange("(a b) n -> a (b n)", a=1)).then_inc(pages_landed, 16)
            sp.dma_start(consts[:, :], a["sample_consts"]).then_inc(consts_landed, 16)
            sp.wait_ge(pages_landed, 16)

            def load_page(slot, n):
                number = nc.sync.value_load(pages[0:1, bass.ds(n, 1)], min_val=0,
                                            max_val=a["cache_nsa_kv"].shape[1] - 1)
                sp.dma_start(page[:, slot, :], a["cache_nsa_kv"][0, bass.ds(number, 1)].rearrange(
                    "a p s h d -> (a p) (s h d)")).then_inc(page_landed[slot], 16)

            for slot in range(2 * PAGE_GROUP):
                load_page(slot, slot)
            with nc.sync.Fori(1, DEC_BATCH * N_PAGES // (2 * PAGE_GROUP)) as it:
                for half in range(2):
                    sp.wait_ge(pages_read, 2 * it + half - 1)
                    sp.wait_ge(values_copied, 2 * it + half - 1)
                    sp.wait_ge(pages_landed, 16)
                    for j in range(PAGE_GROUP):
                        slot = half * PAGE_GROUP + j
                        load_page(slot, 2 * PAGE_GROUP * it + slot)
            sp.wait_ge(mix_ready, 3)
            sp.dma_start(mix_rows[SEQ:TOKENS, :], mix[:, :]).then_inc(mix_out, 16)
            sp.wait_ge(mix_out, 16)

        @block.gpsimd
        def _(pool):
            for table, pattern, base in ((slc_dist, [[1, PAST_LEN]], -PAST_LEN),
                                         (cmp_dist, [[CMP_BLOCK, PAST_CMP]], CMP_BLOCK - 1 - PAST_LEN),
                                         (win_dist, [[1, WINDOW]], -WINDOW)):
                nc.gpsimd.iota(table[:, :], pattern=pattern, base=base, channel_multiplier=0,
                               allow_small_or_imprecise_dtypes=True).then_inc(tables_step, 1)
            nc.gpsimd.memset(q_T[:, :, :, :, :], 0.0)
            nc.gpsimd.memset(q_pair_T[:, :, :, :], 0.0)
            nc.gpsimd.memset(q_own_T[:, :, :, :], 0.0)
            nc.gpsimd.memset(ranking[:, :], FORCE_SCORE)
            nc.gpsimd.memset(state, 0.0).then_inc(state_cleared, 1)
            nc.gpsimd.memset(att_T[:, :, :], 0.0).then_inc(tables_step, 1)
            pool.wait_ge(tables_step, 4)
            pool.wait_ge(consts_landed, 16)
            for table in (slc_dist, cmp_dist, win_dist):
                nc.gpsimd.tensor_scalar(table[:, :], table[:, :], consts[:, NEG_T:NEG_T + 1], None,
                                        ALU.add).then_inc(tables_step, 1)
            pool.wait_ge(tables_step, 7)
            nc.gpsimd.tensor_copy(win_dist[:, 0:DEC_SEQ], consts[:, WIN_OLD:WIN_OLD + DEC_SEQ]).then_inc(
                tables_ready, 1)

            def gla_decayed():
                gq, gk = proj[:R, GQ0:GQ0 + GLA_WIDTH], proj[:R, GK0:GK0 + GLA_WIDTH]
                pool.wait_ge(exps_ready, 4)
                for x, by in ((q_cum, gq), (k_cum, gk), (k_last, gk)):
                    nc.gpsimd.tensor_tensor(x[:, :], x[:, :], by, ALU.mult).then_inc(decayed_ready, 1)
                pool.wait_ge(decayed_ready, 3)

            def gla_finish():
                pool.wait_ge(o_mean_ready, GLA_HEADS)
                nc.gpsimd.tensor_scalar(o_rstd[:, :], o_mean[:, :], EPS, None, ALU.add).then_inc(o_step, 1)
                pool.wait_ge(o_step, 1)
                nc.gpsimd.tensor_tensor(o_rstd[:, :], o_rstd[:, :], shared.minus_half[:R, 0:GLA_HEADS],
                                        ALU.pow).then_inc(o_step, 1)
                pool.wait_ge(silu_step, 2)
                heads = [R, GLA_HEADS, DV]
                factors = [broadcast(o_rstd[:, :].rearrange("p (h a) -> p h a", a=1), heads),
                           broadcast(shared.gla_gain[:R, :].rearrange("p (a e) -> p a e", a=1), heads),
                           silu[:, :].rearrange("p (h e) -> p h e", h=GLA_HEADS),
                           proj[:R, GG0:GG0 + GLA_HEADS * DV].rearrange("p (h e) -> p h e", h=GLA_HEADS)]
                for n, factor in enumerate(factors):
                    pool.wait_ge(o_step, 2 + n)
                    out = o_gla[:, :, :] if n < 3 else mix[:, NSA_WIDTH:].rearrange("p (h e) -> p h e", h=GLA_HEADS)
                    nc.gpsimd.tensor_tensor(out, o_gla[:, :, :], factor, ALU.mult).then_inc(
                        o_step if n < 3 else mix_ready, 1)

            def store_branches(pair):
                pool.wait_ge(branch_taken, 3 * (pair + 1))
                for b in range(2):
                    for kv in range(KV_HEADS):
                        row = b * R + kv * GROUP * DEC_SEQ
                        pool.dma_start(branch_rows[2 * pair + b, kv].rearrange("g t s d -> (g t) s d"),
                                       branch_out[row:row + GROUP * DEC_SEQ, :, kv * HD:(kv + 1) * HD]).then_inc(
                                           branch_stored, 16)

            for pair in range(PAIRS):
                for slot in range(SLOTS):
                    b, g = slot // GROUPS, slot % GROUPS
                    n = pair * SLOTS + slot
                    half = n % 2
                    if slot == 0 and pair == 1:
                        pool.wait_ge(state_out, 16 * GLA_HEADS)
                    if slot % GROUPS == 0 and pair >= 2:
                        pool.wait_ge(values_done, N_PLACES_PER_PAIR * (pair - 1))
                    for j in range(PAGE_GROUP):
                        pool.wait_ge(page_landed[half * PAGE_GROUP + j], 16 * (n // 2 + 1))
                    nc.gpsimd.tensor_copy(
                        values[pair % 2][:, b, g * PAGE_GROUP:(g + 1) * PAGE_GROUP, :],
                        page[:, half * PAGE_GROUP:(half + 1) * PAGE_GROUP, 3 * P:4 * P]).then_inc(values_copied, 1)
                    if pair == 0 and slot == 1:
                        pool.wait_ge(soft_step, 2)
                        nc.gpsimd.tensor_tensor(log_a[:, :], z_min[:, :], log_a[:, :], ALU.subtract).then_inc(
                            log_a_ready, 1)
                    if pair == 0 and slot == 2:
                        gla_decayed()
                    if pair == 0 and slot == 8:
                        gla_finish()
                if pair:
                    store_branches(pair - 1)
            store_branches(PAIRS - 1)
            pool.wait_ge(branch_stored, 16 * 4 * PAIRS)
            for b in range(DEC_BATCH):
                pool.dma_start(branches[b * DEC_SEQ:(b + 1) * DEC_SEQ, :, :].rearrange("t s (h d) -> t s h d", d=HD),
                               branch_rows[b].rearrange("k g t s d -> t s (k g) d")).then_inc(branch_back, 16)

        @block.tensor
        def _(pe):
            ring.wait_free(pe, "q_T")
            for g in range(GROUP):
                last = nc.tensor.transpose(ring.bank("q_T")[:, g * R:(g + 1) * R], q_paired[:R, g * P:(g + 1) * P],
                                           identity[:R, :R])
            last.then_inc(ring.is_filled("q_T"), 1)
            for n, stream in enumerate((2, 4)):
                at = KV0 + stream * P
                last = nc.tensor.transpose(ring.bank("new_k_T")[:, n * R:(n + 1) * R], proj[:R, at:at + P],
                                           identity[:R, :R])
            last.then_inc(ring.is_filled("new_k_T"), 1)
            ring.wait_evacuated(pe, "q_T")
            ring.wait_evacuated(pe, "new_k_T")
            pe.wait_ge(consts_landed, 16)

            def q_of(pair, b):
                return q_T[:, 2 * pair + b, :, :, :].rearrange("p k g t -> p (k g t)")

            def page_group(pair, slot):
                b, g = slot // GROUPS, slot % GROUPS
                n = pair * SLOTS + slot
                half = n % 2
                for j in range(PAGE_GROUP):
                    pe.wait_ge(page_landed[half * PAGE_GROUP + j], 16 * (n // 2 + 1))
                ring.wait_free(pe, "page_T", pair, slot)
                for j in range(PAGE_GROUP):
                    last = nc.tensor.transpose(ring.bank("page_T", pair, slot)[:, j * P:(j + 1) * P],
                                               page[:, half * PAGE_GROUP + j, 2 * P:3 * P], identity[:, :])
                last.then_inc(ring.is_filled("page_T", pair, slot), 1)
                if g == 0 and (pair or b):
                    pe.wait_ge(cmp_T_ready, 2 * pair + b)
                for j in range(PAGE_GROUP):
                    for which in range(2):
                        at = 4 * (g * PAGE_GROUP + j)
                        last = nc.tensor.matmul(cmp_T_ps[:, which, at:at + 4],
                                                page[:, half * PAGE_GROUP + j, which * P:(which + 1) * P],
                                                shared.cmp_w[:, which, :], start=True, stop=True)
                last.then_inc(pages_read, 1)

            def page_scores(pair, slot):
                b = slot // GROUPS
                ring.wait_evacuated(pe, "page_T", pair, slot)
                ring.wait_free(pe, "page_scores", pair, slot)
                nc.tensor.matmul(ring.bank("page_scores", pair, slot)[b * R:(b + 1) * R, :], q_of(pair, b),
                                 page_k_T[slot % 2][:, :], start=True, stop=True).then_inc(
                                     ring.is_filled("page_scores", pair, slot), 1)

            def for_samples(pair, key, columns, moving):
                ring.wait_free(pe, *key)
                for b in range(2):
                    for at, x in zip(columns, moving(b)):
                        last = nc.tensor.matmul(ring.bank(*key)[b * R:(b + 1) * R, at:at + x.shape[-1]],
                                                q_of(pair, b), x, start=True, stop=True, skip_group_check=True)
                last.then_inc(ring.is_filled(*key), 1)

            def turn_probs(key, source, tiles):
                ring.wait_free(pe, *key)
                for m, (at, keys) in enumerate(tiles):
                    last = nc.tensor.transpose(ring.bank(*key)[:keys, m * P:(m + 1) * P], source[:, at:at + keys],
                                               identity[:, :])
                last.then_inc(ring.is_filled(*key), 1)

            def branch_values(key, out, tiles, first, final):
                ring.wait_evacuated(pe, *key)
                place = probs_T[places[key] % 3]
                for m, (keys, v) in enumerate(tiles):
                    for b in range(2):
                        last = nc.tensor.matmul(out[b * R:(b + 1) * R, :], place[:keys, m * P + b * R:m * P + (b + 1) * R],
                                                v(b), start=(first and m == 0), stop=(final and m == len(tiles) - 1),
                                                skip_group_check=True)
                last.then_inc(values_done, 1)

            def tail(pair, slot):
                b0 = 2 * pair
                if slot == 0:
                    pe.wait_ge(cmp_T_ready, 2 * (pair + 1))
                    for_samples(pair, ("cmp", pair), [0], lambda b: [kc_T[pair % 2][:, b, :]])
                    for_samples(pair, ("new", pair), [0, DEC_SEQ],
                                lambda b: [new_k_T[:, n, (b0 + b) * DEC_SEQ:(b0 + b + 1) * DEC_SEQ] for n in range(2)])
                elif slot == 1:
                    pe.wait_ge(win_landed, 32 * (pair + 1))
                    for b in range(2):
                        ring.wait_free(pe, "win_k", pair, b)
                        for j in range(WINDOW // P):
                            last = nc.tensor.transpose(ring.bank("win_k", pair, b)[:, j * P:(j + 1) * P],
                                                       win_kv[:, b, j, 0:P], identity[:, :])
                        last.then_inc(ring.is_filled("win_k", pair, b), 1)
                elif slot == 2:
                    pe.wait_ge(cmp_normed, pair + 1)
                    ring.wait_free(pe, "imp", pair)
                    bank = ring.bank("imp", pair)
                    nc.tensor.matmul(bank[:, 0:P], consts[:, GROUP_SUM:GROUP_SUM + P], cmp[:, :], start=True,
                                     stop=True)
                    for b in range(2):
                        last = nc.tensor.transpose(bank[:, (1 + b) * P:(2 + b) * P], vc_T[pair % 2][:, b, :],
                                                   identity[:, :])
                    last.then_inc(ring.is_filled("imp", pair), 1)
                    turn_probs(("cmp_T", pair), cmp, [(0, P)])
                elif slot == 3:
                    for b in range(2):
                        ring.wait_evacuated(pe, "win_k", pair, b)
                        ring.wait_free(pe, "win", pair, b)
                        nc.tensor.matmul(ring.bank("win", pair, b)[b * R:(b + 1) * R, :], q_of(pair, b),
                                         win_k_T[:, b, :], start=True, stop=True).then_inc(
                                             ring.is_filled("win", pair, b), 1)
                elif slot == 4:
                    ring.wait_evacuated(pe, "imp", pair)
                    if pair:
                        pe.wait_ge(branch_taken, 3 * pair)
                    branch_values(("cmp_T", pair), short_out[:, 0:P], [(P, lambda b: vc[:, b, :])], True, True)
                elif slot == 6:
                    pe.wait_ge(probs_ready, 3 * pair + 2)
                    turn_probs(("win_T", pair, 0), win, [(j * P, P) for j in range(4)])
                    turn_probs(("win_T", pair, 1), win, [(WINDOW, DEC_SEQ)])
                elif slot >= 7:
                    g = slot - 7
                    if g == 0:
                        branch_values(("win_T", pair, 0), short_out[:, P:2 * P],
                                      [(P, lambda b, j=j: win_kv[:, b, j, P:2 * P]) for j in range(4)], True, False)
                        pe.wait_ge(new_v_landed, 32)
                        branch_values(("win_T", pair, 1), short_out[:, P:2 * P],
                                      [(DEC_SEQ, lambda b: new_v[:, 1, b0 + b, :])], False, True)
                        pe.wait_ge(probs_ready, 3 * (pair + 1))
                    else:
                        slc_values(pair, g - 1)
                    tiles = [(4 * g + m) for m in range(4) if 4 * g + m < KEY_TILES]
                    turn_probs(("slc_T", pair, g), slc[pair % 2],
                               [(j * P, P if j < N_PAGES else DEC_SEQ) for j in tiles])
                    if g == SLC_TURNS - 1:
                        slc_values(pair, g)

            def slc_values(pair, g):
                tiles = [(4 * g + m) for m in range(4) if 4 * g + m < KEY_TILES]
                old = lambda b, j: values[pair % 2][:, b, j, :]
                new = lambda b, j: new_v[:, 0, 2 * pair + b, :]
                if g == 0:
                    pe.wait_ge(values_copied, SLOTS * (pair + 1))
                branch_values(("slc_T", pair, g), slc_out[:, 0:P],
                              [(P, lambda b, j=j: old(b, j)) if j < N_PAGES else (DEC_SEQ, lambda b, j=j: new(b, j))
                               for j in tiles], g == 0, g == SLC_TURNS - 1)

            def gla_step(slot):
                if slot == 0:
                    ring.wait_free(pe, "ga_T")
                    nc.tensor.transpose(ring.bank("ga_T")[:RANK, :R], proj[:R, GA0:GA0 + RANK],
                                        identity[:R, :R]).then_inc(ring.is_filled("ga_T"), 1)
                elif slot == 1:
                    ring.wait_evacuated(pe, "ga_T")
                    ring.wait_free(pe, "z")
                    z = ring.bank("z")[:R, :GLA_WIDTH]
                    nc.tensor.matmul(z, ga_T[:, :], shared.w_a2[:, :], start=True, stop=False)
                    nc.tensor.matmul(z, shared.ones_row[:, :R], shared.b_a[:, :], start=False, stop=True).then_inc(
                        ring.is_filled("z"), 1)
                elif slot == 2:
                    pe.wait_ge(log_a_ready, 1)
                    ring.wait_free(pe, "cum")
                    bank = ring.bank("cum")
                    nc.tensor.matmul(bank[:R, :GLA_WIDTH], consts[:R, UPTO:UPTO + R], log_a[:, :], start=True, stop=True)
                    nc.tensor.matmul(bank[:R, GLA_WIDTH:], consts[:R, AFTER:AFTER + R], log_a[:, :], start=True,
                                     stop=True).then_inc(ring.is_filled("cum"), 1)
                    ring.wait_free(pe, "decay")
                    for half in range(2):
                        last = nc.tensor.matmul(ring.bank("decay")[:, half * DEC_BATCH:(half + 1) * DEC_BATCH],
                                                log_a[:, half * P:(half + 1) * P],
                                                consts[:R, OF_SAMPLE:OF_SAMPLE + DEC_BATCH], start=True, stop=True)
                    last.then_inc(ring.is_filled("decay"), 1)
                elif slot == 3:
                    pe.wait_ge(decayed_ready, 3)
                    ring.wait_free(pe, "gla_T")
                    for n, x in enumerate((q_cum, k_cum)):
                        for half in range(2):
                            last = nc.tensor.transpose(ring.bank("gla_T")[:, (2 * n + half) * R:(2 * n + half + 1) * R],
                                                       x[:, half * P:(half + 1) * P], identity[:R, :R])
                    last.then_inc(ring.is_filled("gla_T"), 1)
                elif slot == 4:
                    ring.wait_evacuated(pe, "gla_T")
                    ring.wait_free(pe, "att")
                    for half in range(2):
                        last = nc.tensor.matmul(ring.bank("att")[:R, half * P:(half + 1) * P], k_cum_T[:, half, :],
                                                q_pair_T[:, half, :, :].rearrange("p h t -> p (h t)"),
                                                start=True, stop=True)
                    last.then_inc(ring.is_filled("att"), 1)
                elif slot == 5:
                    pe.wait_ge(att_ready, 1)
                    pe.wait_ge(state_landed, 16 * 4)
                    ring.wait_free(pe, "o")
                    bank = ring.bank("o")
                    for h in range(GLA_HEADS):
                        nc.tensor.matmul(bank[:R, h * DV:(h + 1) * DV], att_T[:, h, :],
                                         proj[:R, GV0 + h * DV:GV0 + (h + 1) * DV], start=(h == 0), stop=False,
                                         skip_group_check=True)
                    for b in range(DEC_BATCH):
                        for half in range(2):
                            own = q_own_T[:, half, :, :].rearrange("p b t -> p (b t)")[:, b * R:(b + 1) * R]
                            last = nc.tensor.matmul(bank[:R, 2 * half * DV:2 * (half + 1) * DV], own,
                                                    state[:, half, b, :, :].rearrange("p h e -> p (h e)"),
                                                    start=False, stop=(b == DEC_BATCH - 1), skip_group_check=True)
                    last.then_inc(ring.is_filled("o"), 1)
                else:
                    b = slot - 6
                    pe.wait_ge(k_own_ready, 1)
                    ring.wait_free(pe, "state", b)
                    for half in range(2):
                        last = nc.tensor.matmul(ring.bank("state", b)[:, 2 * half * DV:2 * (half + 1) * DV],
                                                k_own[:, b, half * P:(half + 1) * P],
                                                proj[:R, GV0 + 2 * half * DV:GV0 + 2 * (half + 1) * DV],
                                                start=True, stop=True)
                    last.then_inc(ring.is_filled("state", b), 1)

            for pair in range(PAIRS + 1):
                for slot in range(SLOTS):
                    if pair < PAIRS:
                        page_group(pair, slot)
                        page_scores(pair, slot)
                    if pair:
                        tail(pair - 1, slot)
                    elif slot < len(GLA):
                        gla_step(slot)

        def take_probs_T(eng, engine, key, tiles):
            n = places[key]
            if n >= 3:
                eng.wait_ge(values_done, n - 2)
            ring.wait_filled(eng, *key)
            whole = sum(k == P for k in tiles)
            parts = ([(P, 0, whole * P)] if whole else []) + [(k, m * P, P) for m, k in enumerate(tiles) if k != P]
            for rows, at, cols in parts:
                src, dst = ring.bank(*key)[:rows, at:at + cols], probs_T[n % 3][:rows, at:at + cols]
                if engine is nc.scalar:
                    last = nc.scalar.activation(dst, src, ACT.Copy)
                else:
                    last = nc.vector.tensor_copy(dst, src)
            last.then_inc(ring.is_evacuated(*key), 1)

        @block.scalar
        def _(act):
            act.wait_ge(state_cleared, 1)
            for h in range(GLA_HEADS):
                rows = slice(h % 2 * DK, (h % 2 + 1) * DK)
                act.dma_start(state[rows, h // 2, :, h % 2, :],
                              a["state_gla"][0, :, h].rearrange("b d e -> d b e")).then_inc(state_landed, 16)
            win_out = outs[6].rearrange("l b t s h d -> (l b) t (s h d)")
            state_win = a["state_nsa_win"].rearrange("l b t s h d -> (l b) t (s h d)")
            act.dma_start(win_out[:, WINDOW - DEC_SEQ:, :], proj[:R, KV0 + 4 * P:KV0 + 6 * P]).then_inc(rows_out, 16)
            act.dma_start(win_out[:, :WINDOW - DEC_SEQ, :], state_win[:, DEC_SEQ:, :]).then_inc(rows_out, 16)
            new_rows = outs[5].rearrange("l b t s h d -> (l t) b (s h d)")
            act.dma_start(new_v[:, 0, :, :], new_rows[:, :, 3 * P:4 * P]).then_inc(new_v_landed, 16)
            act.wait_ge(rows_out, 32)
            act.dma_start(new_v[:, 1, :, :], win_out[:, WINDOW - DEC_SEQ:, P:].rearrange("b t c -> t b c")).then_inc(
                new_v_landed, 16)

            act.wait_ge(tables_ready, 1)
            ring.wait_filled(act, "q_T")
            bank = ring.bank("q_T")[:, :GROUP * R].rearrange("p (g b t) -> p g b t", g=GROUP, b=DEC_BATCH)
            for kv in range(KV_HEADS):
                rows = slice(kv * HD, (kv + 1) * HD)
                for g in range(GROUP):
                    last = nc.scalar.activation(q_T[rows, :, kv, g, :], bank[rows, g, :, :], ACT.Copy)
            last.then_inc(ring.is_evacuated("q_T"), 1)
            ring.wait_filled(act, "new_k_T")
            nc.scalar.activation(new_k_T[:, :, :].rearrange("p n t -> p (n t)"), ring.bank("new_k_T")[:, :2 * R],
                                 ACT.Copy).then_inc(ring.is_evacuated("new_k_T"), 1)

            def take_page_T(pair, slot):
                n = pair * SLOTS + slot
                if n >= 2:
                    ring.wait_filled(act, "page_scores", (n - 2) // SLOTS, (n - 2) % SLOTS)
                ring.wait_filled(act, "page_T", pair, slot)
                nc.scalar.activation(page_k_T[slot % 2][:, :], ring.bank("page_T", pair, slot)[:, :],
                                     ACT.Copy).then_inc(ring.is_evacuated("page_T", pair, slot), 1)

            def take_cmp_T(pair, b):
                act.wait_ge(pages_read, pair * SLOTS + (b + 1) * GROUPS)
                if pair >= 2:
                    ring.wait_filled(act, "imp", pair - 2)
                nc.scalar.activation(kc_T[pair % 2][:, b, :], cmp_T_ps[:, 0, :], ACT.Copy)
                nc.scalar.activation(vc_T[pair % 2][:, b, :], cmp_T_ps[:, 1, :], ACT.Copy).then_inc(cmp_T_ready, 1)

            def exponentials(pair, branch):
                scores = (cmp, win, slc[pair % 2])[branch]
                act.wait_ge(neg_max_ready, 3 * pair + branch + 1)
                if pair:
                    act.wait_ge(branch_taken, 3 * pair)
                nc.scalar.activation(scores[:, :], scores[:, :], ACT.Exp, bias=neg_max[:, branch:branch + 1],
                                     scale=consts[:, SLOPE:SLOPE + 1], accum_out=sums[:, branch:branch + 1]).then_inc(probs_ready, 1)

            def load_win(pair):
                if pair:
                    act.wait_ge(values_done, N_PLACES_PER_PAIR * (pair - 1) + 3)
                for b in range(2):
                    act.dma_start(win_kv[:, b, :, :], state_win[2 * pair + b].rearrange(
                        "(j p) c -> p j c", p=P)).then_inc(win_landed, 16)

            def tail(pair, slot):
                if slot == 0:
                    exponentials(pair, 0)
                elif slot == 1:
                    for b in range(2):
                        ring.wait_filled(act, "win_k", pair, b)
                        if pair and b == 0:
                            ring.wait_filled(act, "win", pair - 1, 1)
                        nc.scalar.activation(win_k_T[:, b, :], ring.bank("win_k", pair, b)[:, :],
                                             ACT.Copy).then_inc(ring.is_evacuated("win_k", pair, b), 1)
                elif slot == 2:
                    take_probs_T(act, nc.scalar, ("cmp_T", pair), [P])
                elif slot == 4:
                    exponentials(pair, 1)
                elif slot == 5:
                    exponentials(pair, 2)
                elif slot == 6:
                    take_probs_T(act, nc.scalar, ("win_T", pair, 1), [DEC_SEQ])
                elif slot >= 7 and (slot - 7) % 2:
                    g = slot - 7
                    take_probs_T(act, nc.scalar, ("slc_T", pair, g),
                                 [P if j < N_PAGES else DEC_SEQ for j in range(4 * g, min(4 * g + 4, KEY_TILES))])
                if slot == 8 and pair + 1 < PAIRS:
                    load_win(pair + 1)

            def gla_step(slot):
                if slot == 0:
                    ring.wait_filled(act, "ga_T")
                    nc.scalar.activation(ga_T[:, :], ring.bank("ga_T")[:RANK, :R], ACT.Copy).then_inc(
                        ring.is_evacuated("ga_T"), 1)
                    nc.scalar.activation(silu[:, :], proj[:R, GG0:GG0 + GLA_HEADS * DV], ACT.Exp,
                                         scale=-1.0).then_inc(silu_step, 1)
                elif slot == 1:
                    act.wait_ge(abs_ready, 1)
                    nc.scalar.activation(log_a[:, :], log_a[:, :], ACT.Exp).then_inc(soft_step, 1)
                    act.wait_ge(soft_step, 1)
                    nc.scalar.activation(log_a[:, :], log_a[:, :], ACT.Ln, bias=1.0).then_inc(soft_step, 1)
                elif slot == 2:
                    ring.wait_filled(act, "cum")
                    bank = ring.bank("cum")
                    nc.scalar.activation(q_cum[:, :], bank[:R, :GLA_WIDTH], ACT.Exp).then_inc(exps_ready, 1)
                    nc.scalar.activation(k_cum[:, :], bank[:R, :GLA_WIDTH], ACT.Exp, scale=-1.0).then_inc(
                        exps_ready, 1)
                    nc.scalar.activation(k_last[:, :], bank[:R, GLA_WIDTH:], ACT.Exp).then_inc(
                        ring.is_evacuated("cum"), 1)
                    ring.wait_evacuated(act, "cum")
                    act.sem_inc(exps_ready, 1)
                    ring.wait_filled(act, "decay")
                    nc.scalar.activation(decay[:, :, :].rearrange("p a b -> p (a b)"),
                                         ring.bank("decay")[:, :2 * DEC_BATCH], ACT.Exp).then_inc(
                                             ring.is_evacuated("decay"), 1)
                    ring.wait_evacuated(act, "decay")
                    act.sem_inc(exps_ready, 1)
                elif slot == 3:
                    ring.wait_filled(act, "gla_T")
                    bank = ring.bank("gla_T")[:, :4 * R].rearrange("p (n a t) -> p n a t", n=2, a=2)
                    for head in range(2):
                        rows = slice(head * DK, (head + 1) * DK)
                        nc.scalar.activation(q_pair_T[rows, :, head, :], bank[rows, 0, :, :], ACT.Copy,
                                             scale=DK ** -0.5)
                    for half in range(2):
                        nc.scalar.activation(q_own_T[:, half, :, 0:DEC_SEQ],
                                             bank[:, 0, half, :].rearrange("p (b t) -> p b t", b=DEC_BATCH),
                                             ACT.Copy, scale=DK ** -0.5)
                    nc.scalar.activation(k_cum_T[:, :, :], bank[:, 1, :, :], ACT.Copy).then_inc(
                        ring.is_evacuated("gla_T"), 1)
                elif slot == 5:
                    ring.wait_filled(act, "o")
                    nc.scalar.activation(o_gla[:, :, :].rearrange("p h e -> p (h e)"), ring.bank("o")[:R, :],
                                         ACT.Copy).then_inc(ring.is_evacuated("o"), 1)
                    ring.wait_evacuated(act, "o")
                    for h in range(GLA_HEADS):
                        nc.scalar.activation(squares[:, h, :], o_gla[:, h, :], ACT.Square, scale=DV ** -0.5,
                                             accum_out=o_mean[:, h:h + 1]).then_inc(o_mean_ready, 1)

            load_win(0)
            for pair in range(PAIRS + 1):
                for slot in range(SLOTS):
                    if pair < PAIRS:
                        take_page_T(pair, slot)
                    if pair:
                        tail(pair - 1, slot)
                    elif slot < len(GLA):
                        gla_step(slot)
                    if pair < PAIRS and slot % GROUPS == GROUPS - 1:
                        take_cmp_T(pair, slot // GROUPS)
                if pair == 0:
                    ring.wait_evacuated(act, "state", DEC_BATCH - 1)
                    for h in range(GLA_HEADS):
                        rows = slice(h % 2 * DK, (h % 2 + 1) * DK)
                        act.dma_start(outs[7][0, :, h].rearrange("b d e -> d b e"),
                                      state[rows, h // 2, :, h % 2, :]).then_inc(state_out, 16)
            act.wait_ge(state_out, 16 * GLA_HEADS)

        @block.vector
        def _(dve):
            steps = [0]

            def done(instruction):
                steps[0] += 1
                instruction.then_inc(dve_step, 1)
                dve.wait_ge(dve_step, steps[0])

            def take_page_scores(pair, slot):
                b, g = slot // GROUPS, slot % GROUPS
                rows, cols = slice(b * R, (b + 1) * R), slice(g * BANK, (g + 1) * BANK)
                if pair == 1 and slot == 0:
                    ring.wait_filled(dve, "state", DEC_BATCH - 1)
                if pair >= 2 and slot == 0:
                    ring.wait_filled(dve, "slc_T", pair - 2, SLC_TURNS - 1)
                ring.wait_filled(dve, "page_scores", pair, slot)
                nc.vector.tensor_tensor(slc[pair % 2][rows, cols], ring.bank("page_scores", pair, slot)[rows, :],
                                        slc_dist[rows, cols], ALU.add).then_inc(
                                            ring.is_evacuated("page_scores", pair, slot), 1)

            def neg_of(branch, source):
                nc.vector.tensor_scalar(neg_max[:, branch:branch + 1], source, consts[:, NEG_SLOPE:NEG_SLOPE + 1], None,
                                        ALU.mult).then_inc(
                    neg_max_ready, 1)

            def biased(out, score, dist, at):
                return nc.vector.tensor_tensor_reduce(out=out, in0=score, in1=dist, scale=1.0,
                                                      scalar=MASKED, op0=ALU.add, op1=ALU.max,
                                                      accum_out=maxima[:, at:at + 1])

            def select_blocks(pair):
                ring.wait_filled(dve, "imp", pair)
                bank = ring.bank("imp", pair)
                nc.vector.tensor_copy(vc[:, :, :].rearrange("p b c -> p (b c)"), bank[:, P:3 * P])
                done(nc.vector.memset(ranking[:, :], FORCE_SCORE))
                nc.vector.tensor_reduce(ranking[:, 1:N_SEL - 2],
                                        bank[:, 2:PAST_CMP - 2].rearrange("p (n r) -> p n r", r=2), AX.X,
                                        ALU.add).then_inc(ring.is_evacuated("imp", pair), 1)
                ring.wait_evacuated(dve, "imp", pair)
                for _ in range(2):
                    done(nc.vector.max(top8[:, :], ranking[:, :]))
                    done(nc.vector.match_replace(ranking[:, :], top8[:, :], ranking[:, :], MASKED))
                done(nc.vector.tensor_scalar(unselected[:, :], ranking[:, :], -1e29, MASKED, ALU.is_gt, ALU.mult))

            def tail(pair, slot):
                s = slc[pair % 2]
                if slot == 0:
                    if pair:
                        ring.wait_filled(dve, "cmp_T", pair - 1)
                        dve.wait_ge(branch_taken, 3 * pair)
                        ring.wait_filled(dve, "win_T", pair - 1, 1)
                    ring.wait_filled(dve, "cmp", pair)
                    biased(cmp[:, :], ring.bank("cmp", pair)[:, :PAST_CMP], cmp_dist[:, :], 0).then_inc(
                        ring.is_evacuated("cmp", pair), 1)
                    ring.wait_evacuated(dve, "cmp", pair)
                    neg_of(0, maxima[:, 0:1])
                    ring.wait_filled(dve, "new", pair)
                    bank = ring.bank("new", pair)
                    new = consts[:, NEW_DIST:NEW_DIST + DEC_SEQ]
                    nc.vector.tensor_tensor(s[:, PAST_LEN:], bank[:, 0:DEC_SEQ], new, ALU.add)
                    nc.vector.tensor_tensor(win[:, WINDOW:], bank[:, DEC_SEQ:2 * DEC_SEQ], new, ALU.add).then_inc(
                        ring.is_evacuated("new", pair), 1)
                    dve.wait_ge(probs_ready, 3 * pair + 1)
                    done(nc.vector.reciprocal(weight[:, 0:1], sums[:, 0:1]))
                    nc.vector.tensor_scalar(cmp[:, :], cmp[:, :], weight[:, 0:1], None, ALU.mult).then_inc(
                        cmp_normed, 1)
                elif slot == 2:
                    select_blocks(pair)
                elif slot == 3:
                    for b in range(2):
                        rows = slice(b * R, (b + 1) * R)
                        ring.wait_filled(dve, "win", pair, b)
                        nc.vector.tensor_tensor(win[rows, :WINDOW], ring.bank("win", pair, b)[rows, :],
                                                win_dist[rows, :], ALU.add).then_inc(
                                                    ring.is_evacuated("win", pair, b), 1)
                    ring.wait_evacuated(dve, "win", pair, 0)
                    ring.wait_evacuated(dve, "win", pair, 1)
                    ring.wait_evacuated(dve, "new", pair)
                    done(nc.vector.tensor_reduce(maxima[:, 1:2], win[:, :], AX.X, ALU.max))
                    neg_of(1, maxima[:, 1:2])
                elif slot == 4:
                    ring.wait_evacuated(dve, "page_scores", pair, SLOTS - 1)
                    ring.wait_evacuated(dve, "new", pair)
                    old = s[:, :PAST_LEN].rearrange("p (n k) -> p n k", k=SEL_BLOCK)
                    flags = broadcast(unselected[:, 0:N_SEL - 1].rearrange("p (n a) -> p n a", a=1),
                                      [P, N_SEL - 1, SEL_BLOCK])
                    biased(old, old, flags, 2)
                    last = unselected[:, N_SEL - 1:N_SEL].to_broadcast([P, DEC_SEQ])
                    done(biased(s[:, PAST_LEN:], s[:, PAST_LEN:], last, 3))
                    done(nc.vector.tensor_tensor(maxima[:, 2:3], maxima[:, 2:3], maxima[:, 3:4], ALU.max))
                    neg_of(2, maxima[:, 2:3])
                elif slot == 6:
                    take_probs_T(dve, nc.vector, ("win_T", pair, 0), [P] * 4)
                elif slot >= 7 and (slot - 7) % 2 == 0:
                    g = slot - 7
                    take_probs_T(dve, nc.vector, ("slc_T", pair, g),
                                 [P if j < N_PAGES else DEC_SEQ for j in range(4 * g, min(4 * g + 4, KEY_TILES))])
                if slot == SLOTS - 1:
                    take_branches(pair)

            def take_branches(pair):
                dve.wait_ge(probs_ready, 3 * (pair + 1))
                done(nc.vector.reciprocal(weight[:, 1:3], sums[:, 1:3]))
                dve.wait_ge(values_done, N_PLACES_PER_PAIR * (pair + 1))
                if pair:
                    dve.wait_ge(branch_stored, 16 * 4 * pair)
                nc.vector.tensor_copy(branch_out[:, 0, :], short_out[:, 0:P]).then_inc(branch_taken, 1)
                nc.vector.tensor_scalar(branch_out[:, 2, :], short_out[:, P:2 * P], weight[:, 1:2], None,
                                        ALU.mult).then_inc(branch_taken, 1)
                nc.vector.tensor_scalar(branch_out[:, 1, :], slc_out[:, 0:P], weight[:, 2:3], None,
                                        ALU.mult).then_inc(branch_taken, 1)

            def gla_step(slot):
                if slot == 0:
                    dve.wait_ge(silu_step, 1)
                    done(nc.vector.tensor_scalar(silu[:, :], silu[:, :], 1.0, None, ALU.add))
                    nc.vector.reciprocal(silu[:, :], silu[:, :]).then_inc(silu_step, 1)
                elif slot == 1:
                    ring.wait_filled(dve, "z")
                    z = ring.bank("z")[:R, :GLA_WIDTH]
                    done(nc.vector.tensor_scalar(z_min[:, :], z, 0.0, None, ALU.min))
                    nc.vector.scalar_tensor_tensor(out=log_a[:, :], in0=z, scalar=-1.0, in1=z_min[:, :],
                                                   op0=ALU.mult, op1=ALU.min).then_inc(ring.is_evacuated("z"), 1)
                    ring.wait_evacuated(dve, "z")
                    dve.sem_inc(abs_ready, 1)
                elif slot == 3:
                    dve.wait_ge(decayed_ready, 3)
                    nc.vector.tensor_tensor(
                        k_own, broadcast(k_last[:, :].rearrange("p (a c) -> p a c", a=1), [R, DEC_BATCH, GLA_WIDTH]),
                        broadcast(consts[:R, IS_SAMPLE:IS_SAMPLE + DEC_BATCH].rearrange("p (b a) -> p b a", a=1),
                                  [R, DEC_BATCH, GLA_WIDTH]), ALU.mult).then_inc(k_own_ready, 1)
                elif slot == 4:
                    ring.wait_filled(dve, "att")
                    keep = broadcast(consts[:R, UPTO:UPTO + R].bitcast(U32).rearrange("p (a t) -> p a t", a=1),
                                     [R, GLA_HEADS, R])
                    nc.vector.copy_predicated(att_T[:, :, :], keep, ring.bank("att")[:R, :GLA_HEADS * R].rearrange(
                        "p (h t) -> p h t", h=GLA_HEADS)).then_inc(ring.is_evacuated("att"), 1)
                    ring.wait_evacuated(dve, "att")
                    dve.sem_inc(att_ready, 1)
                elif slot >= 6:
                    b = slot - 6
                    if b == 0:
                        ring.wait_filled(dve, "o")
                        dve.wait_ge(exps_ready, 4)
                    ring.wait_filled(dve, "state", b)
                    bank = ring.bank("state", b)[:, :].rearrange("p (a h e) -> p a h e", a=2, h=2)
                    for half in range(2):
                        for head in range(2):
                            rows = slice(head * DK, (head + 1) * DK)
                            last = nc.vector.scalar_tensor_tensor(
                                out=state[rows, half, b, head, :], in0=state[rows, half, b, head, :],
                                scalar=decay[rows, half, b:b + 1], in1=bank[rows, half, head, :],
                                op0=ALU.mult, op1=ALU.add)
                    last.then_inc(ring.is_evacuated("state", b), 1)

            dve.wait_ge(tables_ready, 1)
            for pair in range(PAIRS + 1):
                for slot in range(SLOTS):
                    if pair < PAIRS:
                        take_page_scores(pair, slot)
                    if pair:
                        tail(pair - 1, slot)
                    elif slot < len(GLA):
                        gla_step(slot)
            dve.wait_ge(branch_back, 16 * DEC_BATCH)
            gate = shared.gates[:R, :].rearrange("p (b h a) -> p b h a", b=3, a=1)
            wide = branches[:, :, :].rearrange("p b (h d) -> p b h d", d=HD)
            done(nc.vector.tensor_tensor(wide, wide, broadcast(gate, [R, 3, HEADS, HD]), ALU.mult))
            done(nc.vector.tensor_tensor(mix[:, 0:NSA_WIDTH], branches[:, 0, :], branches[:, 1, :], ALU.add))
            nc.vector.tensor_tensor(mix[:, 0:NSA_WIDTH], mix[:, 0:NSA_WIDTH], branches[:, 2, :], ALU.add).then_inc(
                mix_ready, 2)


def output_projection(nc, mix_rows, x_rows, x1_rows, w_out, ln_ffn, identity, minus_half, normed_hi, normed_lo):
    with ExitStack() as ctx:
        def sb(name, shape):
            return ctx.enter_context(nc.sbuf_tensor(name, shape, F32))

        sem = ctx.enter_context(stage_semaphores(nc, "output"))

        w_out_sb = sb("w_out_sb", [P, KT, D_MODEL])
        ln_col = sb("ln_ffn_col", [P, KT])
        mix = [sb(f"mix_in{n}", [P, D_MODEL]) for n in range(2)]
        x_in = [sb(f"x_res{n}", [P, D_MODEL]) for n in range(2)]
        mix_T = [sb(f"mix_T{n}", [P, KT, P]) for n in range(2)]
        x1 = [sb(f"x1_{n}", [P, D_MODEL]) for n in range(2)]
        x1n = [sb(f"x1n_{n}", [P, D_MODEL]) for n in range(2)]
        square = sb("x1_square", [P, D_MODEL])
        mean_sq = sb("x1_mean_sq", [P, TILES])
        rstd = sb("x1_rstd", [P, TILES])

        w_landed = [sem(f"w_out_landed{k}") for k in range(4)]
        ln_landed = sem("ln_ffn_landed")
        mix_landed = [sem(f"mix_landed{n}") for n in range(2)]
        x_landed = [sem(f"x_res_landed{n}") for n in range(2)]
        x1_stored = [sem(f"x1_stored{n}") for n in range(2)]
        mean_ready = sem("x1_mean_ready")
        rstd_ready = sem("x1_rstd_ready")
        x1n_ready = sem("x1n_ready")
        hi_ready = sem("normed_hi_ready")

        order = [("mix_T", 0, 0), ("mix_T", 0, 1)]
        for i in range(TILES):
            if i + 1 < TILES:
                order += [("mix_T", i + 1, 0), ("mix_T", i + 1, 1)]
            order += [("out", i, 0), ("out", i, 1)]
            if i:
                order += [("x1_T", i - 1, 0), ("x1_T", i - 1, 1)]
        order += [("x1_T", TILES - 1, 0), ("x1_T", TILES - 1, 1)]
        ring = turns(nc, ctx, sem, "out_bank", 8, order)

        block = ctx.enter_context(nc.Block())

        @block.sync
        def _(sp):
            sp.dma_start(ln_col[:, :], ln_ffn.rearrange("l (k p) -> p (l k)", p=P),
                         allow_slow_non_contiguous=True).then_inc(ln_landed, 16)
            for i in range(TILES):
                r, n = ROWS[i], i % 2
                if i >= 2:
                    ring.wait_filled(sp, "mix_T", i - 2, 1)
                    ring.wait_evacuated(sp, "out", i - 2, 1)
                sp.dma_start(mix[n][:r, :], mix_rows[i * P:i * P + r, :]).then_inc(mix_landed[n], 16)
                sp.dma_start(x_in[n][:r, :], x_rows(i)).then_inc(x_landed[n], 16)
                if i == 0:
                    for k in range(4):
                        sp.dma_start(w_out_sb[:, 2 * k:2 * k + 2, :], w_out[0, 2 * k * P:(2 * k + 2) * P, :].rearrange(
                            "(k p) n -> p k n", p=P)).then_inc(w_landed[k], 16)

        @block.gpsimd
        def _(pool):
            for i in range(TILES):
                r, n = ROWS[i], i % 2
                ring.wait_evacuated(pool, "out", i, 0)
                ring.wait_evacuated(pool, "out", i, 1)
                pool.dma_start(x1_rows[i * P:i * P + r, :], x1[n][:r, :]).then_inc(x1_stored[n], 16)
                pool.wait_ge(mean_ready, i + 1)
                nc.gpsimd.tensor_scalar(rstd[:r, i:i + 1], mean_sq[:r, i:i + 1], EPS, None,
                                        ALU.add).then_inc(rstd_ready, 1)
                pool.wait_ge(rstd_ready, 2 * i + 1)
                nc.gpsimd.tensor_tensor(rstd[:r, i:i + 1], rstd[:r, i:i + 1], minus_half[:r, 0:1],
                                        ALU.pow).then_inc(rstd_ready, 1)
            pool.wait_ge(x1_stored[0], 16 * 5)
            pool.wait_ge(x1_stored[1], 16 * 4)

        @block.tensor
        def _(pe):
            def transposes(key, source, r):
                for half in range(2):
                    ring.wait_free(pe, *key, half)
                    for j in range(4):
                        k = 4 * half + j
                        last = nc.tensor.transpose(ring.bank(*key, half)[:, j * r:(j + 1) * r],
                                                   source[:r, k * P:(k + 1) * P], identity[:r, :r])
                    last.then_inc(ring.is_filled(*key, half), 1)

            pe.wait_ge(mix_landed[0], 16)
            transposes(("mix_T", 0), mix[0], ROWS[0])
            for i in range(TILES):
                r, n = ROWS[i], i % 2
                if i + 1 < TILES:
                    pe.wait_ge(mix_landed[1 - n], 16 * ((i + 1) // 2 + 1))
                    transposes(("mix_T", i + 1), mix[1 - n], ROWS[i + 1])
                ring.wait_evacuated(pe, "mix_T", i, 0)
                ring.wait_evacuated(pe, "mix_T", i, 1)
                for c in range(2):
                    ring.wait_free(pe, "out", i, c)
                    for k in range(KT):
                        if i == 0 and c == 0 and k % 2 == 0:
                            pe.wait_ge(w_landed[k // 2], 16)
                        last = nc.tensor.matmul(ring.bank("out", i, c)[:r, :], mix_T[n][:, k, :r],
                                                w_out_sb[:, k, c * BANK:(c + 1) * BANK],
                                                start=(k == 0), stop=(k == KT - 1))
                    last.then_inc(ring.is_filled("out", i, c), 1)
                if i:
                    pe.wait_ge(x1n_ready, i)
                    transposes(("x1_T", i - 1), x1n[1 - n], ROWS[i - 1])
            pe.wait_ge(x1n_ready, TILES)
            transposes(("x1_T", TILES - 1), x1n[(TILES - 1) % 2], ROWS[TILES - 1])

        @block.scalar
        def _(act):
            def copy_mix_T(i):
                r = ROWS[i]
                if i >= 2:
                    ring.wait_filled(act, "out", i - 2, 1)
                for half in range(2):
                    ring.wait_filled(act, "mix_T", i, half)
                    nc.scalar.activation(mix_T[i % 2][:, 4 * half:4 * half + 4, :r],
                                         ring.bank("mix_T", i, half)[:, :4 * r].rearrange("p (k t) -> p k t", k=4),
                                         ACT.Copy).then_inc(ring.is_evacuated("mix_T", i, half), 1)

            copy_mix_T(0)
            for i in range(TILES):
                r = ROWS[i]
                if i + 1 < TILES:
                    copy_mix_T(i + 1)
                ring.wait_evacuated(act, "out", i, 0)
                ring.wait_evacuated(act, "out", i, 1)
                if i:
                    act.wait_ge(mean_ready, i)
                nc.scalar.activation(square[:r, :], x1[i % 2][:r, :], ACT.Square, scale=D_MODEL ** -0.5,
                                     accum_out=mean_sq[:r, i:i + 1]).then_inc(mean_ready, 1)

        @block.vector
        def _(dve):
            def scale_normed(i):
                r = ROWS[i]
                for half in range(2):
                    ring.wait_filled(dve, "x1_T", i, half)
                    ln = ln_col[:, 4 * half:4 * half + 4].rearrange("p (k a) -> p k a", a=1).to_broadcast([P, 4, r])
                    nc.vector.tensor_tensor(normed_hi[:, 4 * half:4 * half + 4, i * P:i * P + r],
                                            ring.bank("x1_T", i, half)[:, :4 * r].rearrange("p (k t) -> p k t", k=4),
                                            ln, ALU.mult).then_inc(hi_ready, 1)
                for half in range(2):
                    dve.wait_ge(hi_ready, 2 * i + half + 1)
                    for j in range(4):
                        k = 4 * half + j
                        hi = normed_hi[:, k, i * P:i * P + r].bitcast(F32)
                        last = nc.vector.scalar_tensor_tensor(
                            out=normed_lo[:, k, i * P:i * P + r], in0=ring.bank("x1_T", i, half)[:, j * r:(j + 1) * r],
                            scalar=ln_col[:, k:k + 1], in1=hi, op0=ALU.mult, op1=ALU.subtract)
                    last.then_inc(ring.is_evacuated("x1_T", i, half), 1)

            dve.wait_ge(ln_landed, 16)
            for i in range(TILES):
                r, n = ROWS[i], i % 2
                dve.wait_ge(x_landed[n], 16 * (i // 2 + 1))
                if i >= 2:
                    dve.wait_ge(x1_stored[n], 16 * (i // 2))
                    dve.wait_ge(mean_ready, i - 1)
                for c in range(2):
                    cols = slice(c * BANK, (c + 1) * BANK)
                    ring.wait_filled(dve, "out", i, c)
                    nc.vector.tensor_tensor(x1[n][:r, cols], ring.bank("out", i, c)[:r, :], x_in[n][:r, cols],
                                            ALU.add).then_inc(ring.is_evacuated("out", i, c), 1)
                if i:
                    scale_normed(i - 1)
                dve.wait_ge(rstd_ready, 2 * (i + 1))
                if i >= 2:
                    ring.wait_filled(dve, "x1_T", i - 2, 1)
                nc.vector.tensor_scalar(x1n[n][:r, :], x1[n][:r, :], rstd[:r, i:i + 1], None,
                                        ALU.mult).then_inc(x1n_ready, 1)
            scale_normed(TILES - 1)


def feed_forward_up(nc, normed_hi, normed_lo, hidden, w_gate, w_up):
    with ExitStack() as ctx:
        def sb(name, shape, dtype=F32):
            return ctx.enter_context(nc.sbuf_tensor(name, shape, dtype))

        sem = ctx.enter_context(stage_semaphores(nc, "ffn_up"))

        raw = sb("gate_up_raw", [P, 2, KT, P])
        hi = [sb(f"gate_up_hi{n}", [P, 2, KT, P], F32R) for n in range(2)]
        lo = [sb(f"gate_up_lo{n}", [P, 2, KT, P], F32R) for n in range(2)]
        silu = [sb(f"silu{c}", [P, 3 * P]) for c in range(3)]

        raw_landed = sem("raw_landed")
        hi_ready = sem("hi_ready")
        lo_ready = sem("lo_ready")
        products_ready = [sem(f"products_ready{c}") for c in range(3)]
        exp_ready = sem("silu_exp_ready")
        silu_step = sem("silu_step")
        hidden_ready = [sem(f"hidden_ready{c}") for c in range(3)]
        bank = [ctx.enter_context(nc.psum_tensor(f"up_bank{n}", [P, BANK], F32)) for n in range(6)]

        block = ctx.enter_context(nc.Block())

        @block.sync
        def _(sp):
            def load_raw(f):
                for m, w in enumerate((w_gate, w_up)):
                    sp.dma_start(raw[:, m, :, :], w[0, :, bass.ds(f * P, P)].rearrange(
                        "(k p) f -> p k f", p=P)).then_inc(raw_landed, 16)

            load_raw(0)
            with nc.sync.Fori(1, FT) as f:
                sp.wait_ge(lo_ready, f)
                sp.wait_ge(hi_ready, 1)
                load_raw(f)

        @block.tensor
        def _(pe):
            with nc.tensor.Fori(0, FT // 2) as it:
                for n in range(2):
                    pe.wait_ge(lo_ready, 2 * it + n + 1)
                    for c, (at, cols) in enumerate(PIECES):
                        pe.wait_ge(hidden_ready[c], 2 * it + n + 1)
                        for m in range(2):
                            out = bank[2 * c + m][:, :cols]
                            for k in range(KT):
                                w_hi, w_lo = hi[n][:, m, k, :], lo[n][:, m, k, :]
                                x_hi, x_lo = normed_hi[:, k, at:at + cols], normed_lo[:, k, at:at + cols]
                                nc.tensor.matmul(out, w_hi, x_lo, start=(k == 0), stop=False)
                                nc.tensor.matmul(out, w_hi, x_hi, start=False, stop=False)
                                last = nc.tensor.matmul(out, w_lo, x_hi, start=False, stop=(k == KT - 1))
                        last.then_inc(products_ready[c], 1)

        @block.scalar
        def _(act):
            def split_hi(n, f):
                act.wait_ge(raw_landed, 32 * f + 32)
                nc.scalar.activation(hi[n][:, :, :, :], raw[:, :, :, :], ACT.Copy).then_inc(hi_ready, 1)

            def exponentials(f):
                for c, (at, cols) in enumerate(PIECES):
                    act.wait_ge(products_ready[c], f + 1)
                    nc.scalar.activation(silu[c][:, :cols], bank[2 * c][:, :cols], ACT.Exp,
                                         scale=-1.0).then_inc(exp_ready, 1)

            for n in range(2):
                split_hi(n, n)
            with nc.scalar.Fori(0, FT // 2 - 1) as it:
                for n in range(2):
                    exponentials(2 * it + n)
                    split_hi(n, 2 * it + n + 2)
            exponentials(FT - 2)
            exponentials(FT - 1)

        @block.gpsimd
        def _(pool):
            with nc.gpsimd.Fori(0, FT // 2) as it:
                for n in range(2):
                    pool.wait_ge(hi_ready, 2 * it + n + 1)
                    nc.gpsimd.tensor_tensor(lo[n][:, :, :, :], raw[:, :, :, :], hi[n][:, :, :, :].bitcast(F32),
                                            ALU.subtract).then_inc(lo_ready, 1)

        @block.vector
        def _(dve):
            for c in range(3):
                dve.sem_inc(hidden_ready[c], 1)
            with nc.vector.Fori(0, FT) as f:
                for c, (at, cols) in enumerate(PIECES):
                    s = silu[c][:, :cols]
                    dve.wait_ge(exp_ready, 3 * f + c + 1)
                    nc.vector.tensor_scalar(s, s, 1.0, None, ALU.add).then_inc(silu_step, 1)
                    dve.wait_ge(silu_step, 9 * f + 3 * c + 1)
                    nc.vector.reciprocal(s, s).then_inc(silu_step, 1)
                    dve.wait_ge(silu_step, 9 * f + 3 * c + 2)
                    nc.vector.tensor_tensor(s, bank[2 * c][:, :cols], s, ALU.mult).then_inc(silu_step, 1)
                    dve.wait_ge(silu_step, 9 * f + 3 * c + 3)
                    nc.vector.tensor_tensor(hidden[:, bass.ds(f, 1), at:at + cols].rearrange("p a t -> p (a t)"),
                                            bank[2 * c + 1][:, :cols], s, ALU.mult).then_inc(hidden_ready[c], 1)


def feed_forward_down(nc, hidden, x1_rows, w_down, y_rows, identity):
    with ExitStack() as ctx:
        def sb(name, shape):
            return ctx.enter_context(nc.sbuf_tensor(name, shape, F32))

        sem = ctx.enter_context(stage_semaphores(nc, "ffn_down"))

        down_w = [sb(f"down_w{n}", [P, FT, P]) for n in range(2)]
        y_T = sb("y_T", [P, TOKENS])
        x1 = [sb(f"x1_slab{n}", [P, TILES, P]) for n in range(2)]

        down_landed = [sem(f"down_w_landed{n}") for n in range(2)]
        x1_landed = [sem(f"x1_slab_landed{n}") for n in range(2)]
        y_T_filled = [sem(f"y_T_filled{c}") for c in range(3)]
        y_T_ready = [sem(f"y_T_ready{c}") for c in range(3)]
        y_filled = [sem(f"y_filled{c}") for c in range(3)]
        y_ready = [sem(f"y_ready{c}") for c in range(3)]
        y_stored = [sem(f"y_stored{n}") for n in range(2)]
        bank = [ctx.enter_context(nc.psum_tensor(f"ffn_bank{n}", [P, BANK], F32)) for n in range(8)]

        block = ctx.enter_context(nc.Block())
        SLABS = D_MODEL // P

        def load_down(queue, n, m):
            queue.dma_start(down_w[n][:, :, :], w_down[0, :, bass.ds(m * P, P)].rearrange(
                "(k p) d -> p k d", p=P)).then_inc(down_landed[n], 16)

        def load_x1(queue, n, m):
            cols = bass.ds(m * P, P)
            queue.dma_start(x1[n][:, 0:PROMPT_TILES, :],
                            x1_rows[0:SEQ, cols].rearrange("(i p) d -> p i d", p=P)).then_inc(x1_landed[n], 16)
            queue.dma_start(x1[n][:SAMPLE_ROWS, PROMPT_TILES, :], x1_rows[SEQ:TOKENS, cols]).then_inc(
                x1_landed[n], 16)

        @block.sync
        def _(sp):
            for n in range(2):
                load_down(sp, n, n)

        @block.tensor
        def _(pe):
            for c in range(3):
                pe.sem_inc(y_filled[c], 1)
            with nc.tensor.Fori(0, SLABS // 2) as it:
                for n in range(2):
                    pe.wait_ge(down_landed[n], 16 * it + 16)
                    for c, (at, cols) in enumerate(PIECES):
                        pe.wait_ge(y_T_ready[c], 2 * it + n + 1)
                        for f in range(FT):
                            last = nc.tensor.matmul(bank[c][:, :cols], down_w[n][:, f, :],
                                                    hidden[:, f, at:at + cols], start=(f == 0), stop=(f == FT - 1))
                        last.then_inc(y_T_filled[c], 1)
                    for c, (at, cols) in enumerate(PIECES):
                        pe.wait_ge(y_T_ready[c], 2 * it + n + 2)
                        pe.wait_ge(y_ready[c], 2 * it + n + 1)
                        for t in range(3):
                            r = min(P, cols - t * P)
                            last = nc.tensor.transpose(bank[3 + c][:r, t * P:(t + 1) * P],
                                                       y_T[:, at + t * P:at + t * P + r], identity[:, :])
                        last.then_inc(y_filled[c], 1)

        @block.scalar
        def _(act):
            for c in range(3):
                act.sem_inc(y_T_ready[c], 1)
            def copy_y_T(m):
                for c, (at, cols) in enumerate(PIECES):
                    act.wait_ge(y_T_filled[c], m + 1)
                    act.wait_ge(y_filled[c], m + 1)
                    nc.scalar.activation(y_T[:, at:at + cols], bank[c][:, :cols], ACT.Copy).then_inc(
                        y_T_ready[c], 1)

            with nc.scalar.Fori(0, SLABS // 2 - 1) as it:
                for n in range(2):
                    copy_y_T(2 * it + n)
                    load_down(act, n, 2 * it + n + 2)
            copy_y_T(SLABS - 2)
            copy_y_T(SLABS - 1)

        @block.vector
        def _(dve):
            for c in range(3):
                dve.sem_inc(y_ready[c], 1)
            with nc.vector.Fori(0, SLABS // 2) as it:
                for n in range(2):
                    dve.wait_ge(x1_landed[n], 32 * it + 32)
                    for c, (at, cols) in enumerate(PIECES):
                        dve.wait_ge(y_filled[c], 2 * it + n + 2)
                        whole = cols // P
                        t0 = at // P
                        add = nc.vector.tensor_tensor(
                            x1[n][:, t0:t0 + whole, :], bank[3 + c][:, :whole * P].rearrange("p (i d) -> p i d", d=P),
                            x1[n][:, t0:t0 + whole, :], ALU.add)
                        if cols % P:
                            add = nc.vector.tensor_tensor(
                                x1[n][:SAMPLE_ROWS, t0 + whole, :],
                                bank[3 + c][:SAMPLE_ROWS, whole * P:(whole + 1) * P],
                                x1[n][:SAMPLE_ROWS, t0 + whole, :], ALU.add)
                        add.then_inc(y_ready[c], 1)

        @block.gpsimd
        def _(pool):
            def store_y(n, m):
                for c in range(3):
                    pool.wait_ge(y_ready[c], m + 2)
                cols = bass.ds(m * P, P)
                pool.dma_start(y_rows[0][0, :, cols].rearrange("(i p) d -> p i d", p=P),
                               x1[n][:, 0:PROMPT_TILES, :]).then_inc(y_stored[n], 16)
                pool.dma_start(y_rows[1].rearrange("b t d -> (b t) d")[:, cols],
                               x1[n][:SAMPLE_ROWS, PROMPT_TILES, :]).then_inc(y_stored[n], 16)

            for n in range(2):
                load_x1(pool, n, n)
            with nc.gpsimd.Fori(0, SLABS // 2 - 1) as it:
                for n in range(2):
                    store_y(n, 2 * it + n)
                    pool.wait_ge(y_stored[n], 32 * it + 32)
                    load_x1(pool, n, 2 * it + n + 2)
            for n in range(2):
                store_y(n, SLABS - 2 + n)
            pool.wait_ge(y_stored[0], 32 * SLABS // 2)
            pool.wait_ge(y_stored[1], 32 * SLABS // 2)


def program(nc, a, outs):
    mix_rows = nc.dram_tensor("mix_rows", (TOKENS, D_MODEL), F32, kind="Internal").ap()
    x1_rows = nc.dram_tensor("x1_rows", (TOKENS, D_MODEL), F32, kind="Internal").ap()

    def x_rows(i):
        if i < PROMPT_TILES:
            return a["x_prompt"][0, i * P:(i + 1) * P, :]
        return a["x_sample"].rearrange("b t d -> (b t) d")

    with ExitStack() as ctx:
        identity = ctx.enter_context(nc.sbuf_tensor("identity", [P, P], F32))
        minus_half = ctx.enter_context(nc.sbuf_tensor("minus_half", [P, 16], F32))
        make_constants(nc, identity, minus_half)
        with ExitStack() as attention:
            shared = Shared(nc, attention, identity, minus_half)
            prompt_stage(nc, a, outs, mix_rows, x_rows, shared)
            samples_stage(nc, a, outs, mix_rows, shared)
        normed_hi = ctx.enter_context(nc.sbuf_tensor("normed_hi", [P, KT, TOKENS], F32R))
        normed_lo = ctx.enter_context(nc.sbuf_tensor("normed_lo", [P, KT, TOKENS], F32R))
        output_projection(nc, mix_rows, x_rows, x1_rows, a["w_out"], a["ln_ffn"], identity, minus_half,
                          normed_hi, normed_lo)
        hidden = ctx.enter_context(nc.sbuf_tensor("hidden", [P, FT, TOKENS], F32))
        feed_forward_up(nc, normed_hi, normed_lo, hidden, a["w_gate"], a["w_up"])
        feed_forward_down(nc, hidden, x1_rows, a["w_down"], outs[0:2], identity)


def make_constants(nc, identity, minus_half):
    with stage_semaphores(nc, "constants") as sem, nc.Block() as block:
        cleared = sem("identity_cleared")

        @block.gpsimd
        def _(pool):
            nc.gpsimd.memset(minus_half[:, :], -0.5)
            nc.gpsimd.memset(identity[:, :], 0.0).then_inc(cleared, 1)
            pool.wait_ge(cleared, 1)
            nc.gpsimd.affine_select(out=identity[:, :], in_=identity[:, :], compare_op=ALU.not_equal, fill=1.0,
                                    base=0, pattern=[[-1, P]], channel_multiplier=1)


INPUTS = ["x_prompt", "x_sample", "cache_nsa_kv", "state_nsa_win", "state_gla", "page_table", "ln_mix", "w_in",
          "q_norm", "k_norm", "cmp_pos_w", "w_a2", "b_a", "gla_norm", "w_out", "ln_ffn", "w_gate", "w_up", "w_down"]
OUTPUTS = [(1, SEQ, D_MODEL), (DEC_BATCH, DEC_SEQ, D_MODEL), (1, 1, SEQ, 4, KV_HEADS, HD),
           (1, 1, WINDOW, 2, KV_HEADS, HD), (1, 1, GLA_HEADS, DK, DV), (1, DEC_BATCH, DEC_SEQ, 4, KV_HEADS, HD),
           (1, DEC_BATCH, WINDOW, 2, KV_HEADS, HD), (1, DEC_BATCH, GLA_HEADS, DK, DV)]


def kernel(**inputs):
    import numpy as np
    import concourse.bacc as bacc
    from concourse.bass_utils import run_bass_kernel_spmd

    nc = bacc.Bacc("TRN2", target_bir_lowering=False, num_devices=1)
    arrays, aps = {}, {}
    inputs["sample_consts"] = sample_constants()
    for name in [*INPUTS, "sample_consts"]:
        array = np.ascontiguousarray(inputs[name])
        arrays[f"in_{name}"] = array
        aps[name] = nc.dram_tensor(f"in_{name}", array.shape, mybir.dt.from_np(array.dtype), kind="ExternalInput").ap()
    outs = [nc.dram_tensor(f"out_{n}", shape, F32, kind="ExternalOutput").ap() for n, shape in enumerate(OUTPUTS)]
    program(nc, aps, outs)
    result = run_bass_kernel_spmd(nc, [arrays], core_ids=[0])
    return tuple(result.results[0][f"out_{n}"] for n in range(len(OUTPUTS)))
```

```python
from contextlib import ExitStack, contextmanager

import concourse.bass as bass
from concourse import mybir

F32 = mybir.dt.float32
F32R = mybir.dt.float32r
I32 = mybir.dt.int32
U32 = mybir.dt.uint32
ALU = mybir.AluOpType
ACT = mybir.ActivationFunctionType
AX = mybir.AxisListType

P = 128
BANK = 512
D_MODEL = 1024
KT = D_MODEL // P
SEQ = 1024
DEC_BATCH = 8
DEC_SEQ = 8
SAMPLE_ROWS = DEC_BATCH * DEC_SEQ
PROMPT_TILES = SEQ // P
TILES = PROMPT_TILES + 1
TOKENS = SEQ + SAMPLE_ROWS
ROWS = [P] * PROMPT_TILES + [SAMPLE_ROWS]
PAST_LEN = 4096
PAGE_SIZE = 128
N_PAGES = PAST_LEN // PAGE_SIZE
HEADS = 8
KV_HEADS = 2
GROUP = HEADS // KV_HEADS
HD = 64
CMP_BLOCK = 32
SEL_BLOCK = 64
WINDOW = 512
GLA_HEADS = 4
DK = 64
DV = 128
RANK = 16
TAU = 16.0
CHUNK = 64
D_FF = 2816
FT = D_FF // P
EPS = 1e-6
MASKED = -1e30
SCALE = HD ** -0.5
SLOPES = [2.0 ** (-8.0 * (h + 1) / HEADS) for h in range(HEADS)]

Q0 = 0
KV0 = HEADS * HD
KV_COLS = 6 * KV_HEADS * HD
GATE0 = KV0 + KV_COLS
GQ0 = GATE0 + 3 * HEADS
GK0 = GQ0 + GLA_HEADS * DK
GV0 = GK0 + GLA_HEADS * DK
GG0 = GV0 + GLA_HEADS * DV
GA0 = GG0 + GLA_HEADS * DV
IN_WIDTH = GA0 + RANK

PIECES = [(0, 3 * P), (3 * P, 3 * P), (6 * P, TOKENS - 6 * P)]


class Turns:

    def __init__(self, banks, filled, evacuated, order):
        self.banks, self.filled, self.evacuated = banks, filled, evacuated
        self.turn = {key: (n % len(banks), n // len(banks)) for n, key in enumerate(order)}
        assert len(self.turn) == len(order)

    def bank(self, *key):
        return self.banks[self.turn[key][0]]

    def is_filled(self, *key):
        return self.filled[self.turn[key][0]]

    def is_evacuated(self, *key):
        return self.evacuated[self.turn[key][0]]

    def wait_free(self, pe, *key):
        b, use = self.turn[key]
        if use:
            pe.wait_ge(self.evacuated[b], use)

    def wait_filled(self, eng, *key):
        b, use = self.turn[key]
        eng.wait_ge(self.filled[b], use + 1)

    def wait_evacuated(self, eng, *key):
        b, use = self.turn[key]
        eng.wait_ge(self.evacuated[b], use + 1)


def turns(nc, ctx, sem, name, count, order):
    banks = [ctx.enter_context(nc.psum_tensor(f"{name}{n}", [P, BANK], F32)) for n in range(count)]
    filled = [sem(f"{name}{n}_filled") for n in range(count)]
    evacuated = [sem(f"{name}{n}_evacuated") for n in range(count)]
    return Turns(banks, filled, evacuated, order)


@contextmanager
def stage_semaphores(nc, stage):
    taken = []

    def sem(name):
        taken.append(nc.alloc_semaphore(name=f"{stage}_{name}"))
        return taken[-1]

    yield sem
    nc.clear_and_free_semaphores(taken)
    nc.all_engine_barrier()


def broadcast(ap, shape):
    return ap.to_broadcast(shape)


NSA_WIDTH = HEADS * HD
COMPRESSED, SELECTED, SLIDING = range(3)
SLC_AT, WIN_AT, CMP_AT = 0, SEQ, SEQ + WINDOW + P
SCORE_COLS = CMP_AT + SEQ // CMP_BLOCK
N_CMP = SEQ // CMP_BLOCK
WIN_TILES = WINDOW // P + 1
IN_CHUNKS = [(c * BANK, min(BANK, IN_WIDTH - c * BANK)) for c in range(-(-IN_WIDTH // BANK))]
GLA_WIDTH = GLA_HEADS * DK
LAST_HEAD = (PROMPT_TILES - 1, HEADS - 1)


class Shared:

    def __init__(self, nc, ctx, identity, minus_half, gates):
        def sb(name, shape):
            return ctx.enter_context(nc.sbuf_tensor(name, shape, F32))

        self.identity = identity
        self.minus_half = minus_half
        self.proj0 = sb("proj0", [P, IN_WIDTH])
        self.q_paired = sb("q_paired", [P, NSA_WIDTH])
        self.gates = gates
        self.cmp_w = sb("cmp_w", [P, 2, P // CMP_BLOCK])
        self.gla_gain = sb("gla_gain", [P, DV])
        self.w_a2 = sb("w_a2_sb", [RANK, GLA_WIDTH])
        self.b_a = sb("b_a_sb", [1, GLA_WIDTH])
        self.ones_row = sb("ones_row", [1, P])


def prompt_stage(nc, a, outs, mix_rows, x_rows, shared):
    identity, minus_half, proj0, q_paired = shared.identity, shared.minus_half, shared.proj0, shared.q_paired
    cmp_w, gla_gain, w_a2, b_a, ones_row = shared.cmp_w, shared.gla_gain, shared.w_a2, shared.b_a, shared.ones_row
    with ExitStack() as ctx:
        def sb(name, shape):
            return ctx.enter_context(nc.sbuf_tensor(name, shape, F32))

        sem = ctx.enter_context(stage_semaphores(nc, "prompt"))

        w_in = sb("w_in_sb", [P, KT, IN_WIDTH])
        ln_col = sb("ln_mix_col", [P, KT])
        q_gain = sb("q_gain", [P, HEADS, HD])
        k_gain = sb("k_gain", [P, 3, HD])
        slc_dist = sb("slc_dist", [P, SEQ])
        win_dist = sb("win_dist", [P, WINDOW + P])
        cmp_dist = sb("cmp_dist", [P, 2 * N_CMP - P // CMP_BLOCK])
        cum_upto = sb("cum_upto", [P, P])
        cum_from_mid = sb("cum_from_mid", [P, P])
        cum_after = sb("cum_after", [P, P])
        in_chunk = sb("in_chunk", [P, 2])
        x_in = sb("x_in", [P, D_MODEL])
        h_T = sb("h_T", [P, KT, P])
        mean_x = sb("mean_x", [P, TILES])
        rstd_x = sb("rstd_x", [P, TILES])
        proj = [proj0, sb("proj1", [P, IN_WIDTH])]
        norm_sq = sb("norm_sq", [P, NSA_WIDTH])
        norm_mean = sb("norm_mean", [P, 14])
        norm_rstd = sb("norm_rstd", [P, 14])
        gates = [shared.gates, sb("gates1", [P, 3 * HEADS])]
        q_T = sb("q_T", [P, HEADS, P])
        k_T = [sb("k_slc_T", [P, SEQ]), sb("k_win_T", [P, SEQ])]
        v_all = sb("v_all", [P, PROMPT_TILES, 2, KV_HEADS * HD])
        kc_T = sb("kc_T", [P, N_CMP])
        vc_T = sb("vc_T", [P, N_CMP])
        vc = [sb(f"vc{n}", [N_CMP, KV_HEADS * HD]) for n in range(2)]
        scores = [sb(f"scores{n}", [P, SCORE_COLS]) for n in range(2)]
        maxima = sb("maxima", [P, 3])
        neg_max = [sb(f"neg_max{n}", [P, 3]) for n in range(2)]
        sums = [sb(f"sums{n}", [P, 3]) for n in range(2)]
        weight = sb("branch_weight", [P, 3])
        probs_T = [sb(f"probs_T{n}", [P, BANK]) for n in range(3)]
        mix = sb("mix", [P, D_MODEL])
        ga_T = sb("ga_T", [RANK, P])
        z_min = sb("z_min", [P, GLA_WIDTH])
        log_a = sb("log_a", [P, GLA_WIDTH])
        q_decayed = sb("q_decayed", [P, 2, GLA_WIDTH])
        k_mid = sb("k_mid", [P, GLA_WIDTH])
        k_decay = sb("k_decay", [P, GLA_WIDTH])
        k_last = [sb(f"k_last{c}", [P, GLA_WIDTH]) for c in range(2)]
        decay = sb("decay", [P, 2, 2])
        q_mid_T = sb("q_mid_T", [P, 2, 2, P])
        k_mid_T = sb("k_mid_T", [P, 2, P])
        q_cum_T = [sb(f"q_cum_T{c}", [P, 2, P]) for c in range(2)]
        att_T = sb("gla_att_T", [P, GLA_HEADS, P])
        state = [sb(f"gla_state{n}", [P, 2, 2, DV]) for n in range(2)]
        o_gla = sb("o_gla", [P, GLA_HEADS, DV])
        norm_scratch = q_decayed[:, :, :].rearrange("p a c -> p (a c)").rearrange("p (h e) -> p h e", h=GLA_HEADS)
        o_mean = sb("o_mean", [P, GLA_HEADS])
        o_rstd = sb("o_rstd", [P, GLA_HEADS])
        silu = sb("gla_silu", [P, GLA_HEADS * DV])

        consts_landed = sem("consts_landed")
        w_in_landed = [sem(f"w_in_landed{c}") for c in range(len(IN_CHUNKS))]
        x_landed = sem("x_landed")
        cleared = sem("consts_cleared")
        tables_step = sem("tables_step")
        tables_ready = sem("tables_ready")
        gain_ready = sem("gain_ready")
        sq_x_ready = sem("sq_x_ready")
        rstd_x_ready = sem("rstd_x_ready")
        h_T_ready = sem("h_T_ready")
        norm_step = sem("norm_step")
        norm_mean_ready = sem("norm_mean_ready")
        norm_rstd_ready = sem("norm_rstd_ready")
        qk_normed = sem("qk_normed")
        gate_exp = sem("gate_exp")
        gates_ready = sem("gates_ready")
        v_copied = sem("v_copied")
        rows_stored = [sem(f"rows_stored{n}") for n in range(2)]
        scores_filled = sem("scores_filled")
        scores_read = sem("scores_read")
        neg_max_ready = sem("neg_max_ready")
        probs_ready = sem("probs_ready")
        values_done = sem("values_done")
        weight_step = sem("weight_step")
        combined = sem("combined")
        mix_gla_ready = sem("mix_gla_ready")
        mix_stored = sem("mix_stored")
        state_stored = sem("state_stored")
        abs_step = sem("gla_abs_step")
        abs_ready = sem("gla_abs_ready")
        soft_step = sem("gla_soft_step")
        log_a_ready = sem("log_a_ready")
        exps_ready = sem("gla_exps_ready")
        decayed_ready = sem("gla_decayed_ready")
        k_last_ready = sem("k_last_ready")
        dve_tables = sem("dve_tables")
        att_ready = sem("gla_att_ready")
        state_ready = sem("gla_state_ready")
        silu_exp = sem("gla_silu_exp")
        silu_step = sem("gla_silu_step")
        silu_ready = sem("gla_silu_ready")
        o_copied = sem("o_gla_copied")
        o_mean_ready = sem("o_mean_ready")
        o_step = sem("o_step")

        slc_ps = ctx.enter_context(nc.psum_tensor("slc_ps", [P, 2 * BANK], F32))
        win_ps = ctx.enter_context(nc.psum_tensor("win_ps", [P, 2 * BANK], F32))
        o_ps = ctx.enter_context(nc.psum_tensor("o_ps", [P, BANK], F32))

        def key_tiles(i):
            first = max(0, i + 1 - WIN_TILES)
            return ([(SLC_AT + j * P, P, SELECTED, j) for j in range(i + 1)]
                    + [(WIN_AT + (j - first) * P, P, SLIDING, j) for j in range(first, i + 1)]
                    + [(CMP_AT, N_CMP, COMPRESSED, 0)])

        def key_groups(i):
            tiles = key_tiles(i)
            return [tiles[n:n + 4] for n in range(0, len(tiles), 4)]

        GLA_TURNS = [[("ga_T",)], [("z",)], [("cum", 0), ("cum", 1)], [("gla_T", 0), ("gla_T", 1)], [("att",)],
                     [("state", 0)], [("o",)], [("state", 1)]]
        order = [("x_T", 0, 0), ("x_T", 0, 1)] + [("proj", 0, c) for c in range(6)]
        order += [("q_T", 0), ("k_T", 0), ("vc", 0)]
        group_no = {}
        for i in range(PROMPT_TILES):
            for h in range(HEADS):
                order += [("x_T", i + 1, 0), ("x_T", i + 1, 1)] if h == 0 else \
                    [("proj", i + 1, h - 1)] if h <= 6 else []
                order += [(key[0], i, *key[1:]) for key in GLA_TURNS[h]]
                if h == HEADS - 1 and i + 1 < PROMPT_TILES:
                    order += [("q_T", i + 1), ("k_T", i + 1), ("vc", i + 1)]
                for g in range(len(key_groups(i))):
                    group_no[i, h, g] = len(group_no)
                    order.append(("probs_T", i, h, g))
        ring = turns(nc, ctx, sem, "bank", 3, order)

        def heads_from(i, h, by):
            return divmod(i * HEADS + h + by, HEADS)

        last_group = {(i, h): group_no[i, h, len(key_groups(i)) - 1] for i in range(PROMPT_TILES)
                      for h in range(HEADS)}

        CONSTS = 3 + 3 + 8
        block = ctx.enter_context(nc.Block())

        def branch_columns(i):
            return [(CMP_AT, N_CMP), (SLC_AT, (i + 1) * P), (WIN_AT, min(i + 1, WIN_TILES) * P)]

        def take_probs_T(eng, engine, i, h, parity):
            for g, group in enumerate(key_groups(i)):
                n = group_no[i, h, g]
                if n % 2 != parity:
                    continue
                if n >= 3:
                    eng.wait_ge(values_done, n - 2)
                ring.wait_filled(eng, "probs_T", i, h, g)
                whole = [m for m, t in enumerate(group) if t[1] == P]
                parts = [(P, 0, len(whole) * P)] if whole else []
                parts += [(N_CMP, m * P, P) for m, t in enumerate(group) if t[1] != P]
                for rows, at, cols in parts:
                    src = ring.bank("probs_T", i, h, g)[:rows, at:at + cols]
                    dst = probs_T[n % 3][:rows, at:at + cols]
                    if parity == 0:
                        last = nc.scalar.activation(dst, src, ACT.Copy)
                    else:
                        last = nc.vector.tensor_copy(dst, src)
                last.then_inc(ring.is_evacuated("probs_T", i, h, g), 1)

        @block.sync
        def _(sp):
            sp.dma_start(x_in[:, :], x_rows(0)).then_inc(x_landed, 16)
            sp.dma_start(ln_col[:, :], a["ln_mix"].rearrange("l (k p) -> p (l k)", p=P),
                         allow_slow_non_contiguous=True).then_inc(consts_landed, 16)

            def load_w_in(c):
                at, cols = IN_CHUNKS[c]
                sp.dma_start(w_in[:, :, at:at + cols], a["w_in"][0, :, at:at + cols].rearrange(
                    "(k p) n -> p k n", p=P)).then_inc(w_in_landed[c], 16)

            load_w_in(0)
            sp.dma_start(q_gain[:, :, :], a["q_norm"].rearrange("l (a d) -> l a d", a=1).to_broadcast(
                [P, HEADS, HD])).then_inc(consts_landed, 16)
            sp.dma_start(k_gain[:, :, :], a["k_norm"].to_broadcast([P, 3, HD])).then_inc(consts_landed, 16)
            sp.dma_start(gla_gain[:, :], a["gla_norm"].to_broadcast([P, DV])).then_inc(consts_landed, 16)
            sp.dma_start(w_a2[:, :], a["w_a2"][0]).then_inc(consts_landed, 16)
            sp.dma_start(b_a[:, :], a["b_a"]).then_inc(consts_landed, 16)
            sp.wait_ge(cleared, 1)
            for which in range(2):
                for j in range(P // CMP_BLOCK):
                    sp.dma_start(cmp_w[j * CMP_BLOCK:(j + 1) * CMP_BLOCK, which, j:j + 1],
                                 a["cmp_pos_w"][0, which].rearrange("(c a) -> c a", a=1),
                                 allow_slow_non_contiguous=True).then_inc(consts_landed, 16)
            for c in range(1, len(IN_CHUNKS)):
                load_w_in(c)
            for i in range(TILES):
                r, n = ROWS[i], i % 2
                if i + 1 < TILES:
                    ring.wait_filled(sp, "x_T", i, 1)
                    sp.wait_ge(sq_x_ready, i + 1)
                    sp.dma_start(x_in[:ROWS[i + 1], :], x_rows(i + 1)).then_inc(x_landed, 16)
                sp.wait_ge(qk_normed, 4 * (i + 1))
                rows = outs[2] if i < PROMPT_TILES else outs[5]
                rows = rows.rearrange("l b t s h d -> (l b t) (s h d)")
                at = i * P if i < PROMPT_TILES else 0
                sp.dma_start(rows[at:at + r, :], proj[n][:r, KV0:KV0 + 512]).then_inc(rows_stored[n], 16)
                if SEQ - WINDOW <= i * P < SEQ:
                    at = i * P - (SEQ - WINDOW)
                    sp.dma_start(outs[3].rearrange("l b t s h d -> (l b t) (s h d)")[at:at + P, :],
                                 proj[n][:, KV0 + 512:KV0 + 768]).then_inc(rows_stored[n], 16)
            sp.wait_ge(state_ready, 4 * 2 * PROMPT_TILES)
            for h in range(GLA_HEADS):
                sp.dma_start(outs[4][0, 0, h], state[0][64 * (h % 2):64 * (h % 2) + 64, h // 2, h % 2, :]).then_inc(
                    state_stored, 16)
            sp.wait_ge(state_stored, 16 * GLA_HEADS)
            sp.wait_ge(rows_stored[0], 16 * 7)
            sp.wait_ge(rows_stored[1], 16 * 6)

        def rows_stored_before(i):
            return 16 * sum(1 + (SEQ - WINDOW <= j * P < SEQ) for j in range(i % 2, i, 2))

        @block.gpsimd
        def _(pool):
            nc.gpsimd.memset(cmp_w[:, :, :], 0.0).then_inc(cleared, 1)
            for table, pattern, base in ((slc_dist, [[1, SEQ]], P - SEQ), (win_dist, [[1, WINDOW + P]], -WINDOW),
                                         (cmp_dist, [[CMP_BLOCK, 2 * N_CMP - 4]],
                                          CMP_BLOCK - 1 - CMP_BLOCK * (N_CMP - 4))):
                nc.gpsimd.iota(table[:, :], pattern=pattern, base=base, channel_multiplier=-1,
                               allow_small_or_imprecise_dtypes=True).then_inc(tables_step, 1)
            for m in (cum_upto, cum_after):
                nc.gpsimd.memset(m[:, :], 1.0 / TAU).then_inc(tables_step, 1)
            pool.wait_ge(tables_step, 5)
            for table, pattern, base in ((slc_dist, [[-1, SEQ]], SEQ - P), (win_dist, [[-1, WINDOW + P]], WINDOW),
                                         (cmp_dist, [[-CMP_BLOCK, 2 * N_CMP - 4]],
                                          CMP_BLOCK * (N_CMP - 4) - CMP_BLOCK + 1)):
                nc.gpsimd.affine_select(out=table[:, :], in_=table[:, :], compare_op=ALU.is_ge, fill=MASKED,
                                        base=base, pattern=pattern, channel_multiplier=1).then_inc(tables_step, 1)
            nc.gpsimd.affine_select(out=cum_upto[:, :], in_=cum_upto[:, :], compare_op=ALU.is_ge, fill=0.0, base=0,
                                    pattern=[[1, P]], channel_multiplier=-1).then_inc(tables_step, 1)
            nc.gpsimd.affine_select(out=cum_after[:, :], in_=cum_after[:, :], compare_op=ALU.is_ge, fill=0.0,
                                    base=-1, pattern=[[-1, P]], channel_multiplier=1).then_inc(tables_step, 1)
            pool.wait_ge(tables_step, 10)
            nc.gpsimd.affine_select(out=win_dist[:, :], in_=win_dist[:, :], compare_op=ALU.is_ge, fill=MASKED,
                                    base=-1, pattern=[[1, WINDOW + P]], channel_multiplier=-1).then_inc(
                                        tables_step, 1)
            nc.gpsimd.memset(cum_from_mid[:, :], 0.0)
            nc.gpsimd.memset(in_chunk[:, :], 0.0)
            nc.gpsimd.memset(ones_row[:, :], 1.0)
            nc.gpsimd.memset(kc_T[:, :], 0.0)
            nc.gpsimd.memset(vc_T[:, :], 0.0)
            nc.gpsimd.memset(q_T[:, :, :], 0.0)
            nc.gpsimd.memset(q_mid_T[:, :, :, :], 0.0)
            nc.gpsimd.memset(att_T[:, :, :], 0.0)
            for c in range(2):
                nc.gpsimd.memset(k_last[c][:, :], 0.0)
                nc.gpsimd.memset(q_cum_T[c][:, :, :], 0.0)
                nc.gpsimd.memset(state[c][:, :, :, :], 0.0).then_inc(tables_step, 1)
            def rstd_of(mean, out, r, count, step, value, ready):
                nc.gpsimd.tensor_scalar(out, mean, 1.0 / count, EPS, ALU.mult, ALU.add).then_inc(step, 1)
                pool.wait_ge(step, value)
                nc.gpsimd.tensor_tensor(out, out, minus_half[:r, 0:out.shape[1]], ALU.pow).then_inc(ready, 1)

            def x_rstd(i):
                r = ROWS[i]
                pool.wait_ge(sq_x_ready, i + 1)
                rstd_of(mean_x[:r, i:i + 1], rstd_x[:r, i:i + 1], r, 1, rstd_x_ready, 2 * i + 1, rstd_x_ready)

            def qk_rstd(i):
                r = ROWS[i]
                pool.wait_ge(norm_mean_ready, i + 1)
                rstd_of(norm_mean[:r, :], norm_rstd[:r, :], r, HD, norm_rstd_ready, 2 * i + 1, norm_rstd_ready)

            def copy_v(i):
                v = proj[i % 2][:, KV0:KV0 + KV_COLS].rearrange("p (s c) -> p s c", s=6)
                ring.wait_evacuated(pool, "proj", i, 2)
                nc.gpsimd.tensor_copy(v_all[:, i, :, :], v[:, 3:6:2, :]).then_inc(v_copied, 1)

            def finish_gla(i):
                pool.wait_ge(o_mean_ready, i + 1)
                rstd_of(o_mean[:, :], o_rstd[:, :], P, 1, o_step, 5 * i + 1, o_step)
                pool.wait_ge(o_step, 5 * i + 2)
                o_rstd_wide = broadcast(o_rstd[:, :].rearrange("p (h a) -> p h a", a=1), [P, GLA_HEADS, DV])
                nc.gpsimd.tensor_tensor(o_gla[:, :, :], o_gla[:, :, :], o_rstd_wide, ALU.mult).then_inc(o_step, 1)
                pool.wait_ge(o_step, 5 * i + 3)
                nc.gpsimd.tensor_tensor(o_gla[:, :, :], o_gla[:, :, :],
                                        broadcast(gla_gain[:, :].rearrange("p (a e) -> p a e", a=1),
                                                  [P, GLA_HEADS, DV]), ALU.mult).then_inc(o_step, 1)
                pool.wait_ge(o_step, 5 * i + 4)
                pool.wait_ge(silu_ready, i + 1)
                nc.gpsimd.tensor_tensor(o_gla[:, :, :], o_gla[:, :, :],
                                        silu[:, :].rearrange("p (h e) -> p h e", h=GLA_HEADS),
                                        ALU.mult).then_inc(o_step, 1)
                pool.wait_ge(o_step, 5 * i + 5)
                if i:
                    pool.wait_ge(mix_stored, 16 * i)
                nc.gpsimd.tensor_tensor(mix[:, NSA_WIDTH:].rearrange("p (h e) -> p h e", h=GLA_HEADS),
                                        o_gla[:, :, :], proj[i % 2][:, GG0:GG0 + 512].rearrange(
                                            "p (h e) -> p h e", h=GLA_HEADS), ALU.mult).then_inc(mix_gla_ready, 1)
                pool.wait_ge(mix_gla_ready, i + 1)
                pool.wait_ge(combined, HEADS * 3 * (i + 1))
                pool.dma_start(mix_rows[i * P:(i + 1) * P, :], mix[:, :]).then_inc(mix_stored, 16)

            x_rstd(0)
            copy_v(0)
            qk_rstd(0)
            for i in range(PROMPT_TILES):
                pr = proj[i % 2]
                x_rstd(i + 1)
                pool.wait_ge(silu_exp, i + 1)
                nc.gpsimd.tensor_scalar(silu[:, :], silu[:, :], 1.0, None, ALU.add).then_inc(silu_step, 1)
                pool.wait_ge(soft_step, 2 * (i + 1))
                nc.gpsimd.tensor_tensor(log_a[:, :], z_min[:, :], log_a[:, :], ALU.subtract).then_inc(log_a_ready, 1)
                pool.wait_ge(exps_ready, 4 * (i + 1))
                gq = pr[:, GQ0:GQ0 + GLA_WIDTH]
                gk = pr[:, GK0:GK0 + GLA_WIDTH]
                nc.gpsimd.tensor_tensor(q_decayed[:, 1, :], q_decayed[:, 1, :], gq, ALU.mult).then_inc(
                    decayed_ready, 1)
                nc.gpsimd.tensor_tensor(k_mid[:, :], k_mid[:, :], gk, ALU.mult).then_inc(decayed_ready, 1)
                nc.gpsimd.tensor_tensor(q_decayed[:, 0, :], q_decayed[:, 0, :], gq, ALU.mult).then_inc(
                    decayed_ready, 1)
                if i + 1 < PROMPT_TILES:
                    copy_v(i + 1)
                qk_rstd(i + 1)
                finish_gla(i)
            pool.wait_ge(mix_stored, 16 * PROMPT_TILES)

        @block.tensor
        def _(pe):
            def project_x_T(i):
                r = ROWS[i]
                pe.wait_ge(x_landed, 16 * (i + 1))
                for half in range(2):
                    ring.wait_free(pe, "x_T", i, half)
                    for j in range(4):
                        k = 4 * half + j
                        last = nc.tensor.transpose(ring.bank("x_T", i, half)[:, j * r:(j + 1) * r],
                                                   x_in[:r, k * P:(k + 1) * P], identity[:r, :r])
                    last.then_inc(ring.is_filled("x_T", i, half), 1)

            def project(i, c):
                r = ROWS[i]
                at, cols = IN_CHUNKS[c]
                pe.wait_ge(h_T_ready, 2 * (i + 1))
                ring.wait_free(pe, "proj", i, c)
                if i == 0:
                    pe.wait_ge(w_in_landed[c], 16)
                for k in range(KT):
                    last = nc.tensor.matmul(ring.bank("proj", i, c)[:r, :cols], h_T[:, k, :r],
                                            w_in[:, k, at:at + cols], start=(k == 0), stop=(k == KT - 1))
                last.then_inc(ring.is_filled("proj", i, c), 1)

            def transpose_qk(i):
                pr = proj[i % 2]
                pe.wait_ge(qk_normed, 4 * (i + 1))
                ring.wait_free(pe, "q_T", i)
                bank = ring.bank("q_T", i)
                for j in range(GROUP):
                    last = nc.tensor.transpose(bank[:, j * P:(j + 1) * P], q_paired[:, j * P:(j + 1) * P],
                                               identity[:, :])
                last.then_inc(ring.is_filled("q_T", i), 1)
                ring.wait_free(pe, "k_T", i)
                bank = ring.bank("k_T", i)
                for n, stream in enumerate((2, 4)):
                    at = KV0 + stream * P
                    nc.tensor.transpose(bank[:, n * P:(n + 1) * P], pr[:, at:at + P], identity[:, :])
                for which in range(2):
                    at = KV0 + which * P
                    last = nc.tensor.matmul(bank[:, 2 * P + 4 * which:2 * P + 4 * which + 4], pr[:, at:at + P],
                                            cmp_w[:, which, :], start=True, stop=True)
                last.then_inc(ring.is_filled("k_T", i), 1)
                ring.wait_evacuated(pe, "k_T", i)
                ring.wait_free(pe, "vc", i)
                nc.tensor.transpose(ring.bank("vc", i)[:N_CMP, :P], vc_T[:, :], identity[:, :]).then_inc(
                    ring.is_filled("vc", i), 1)

            def head_scores(i, h):
                n = i * HEADS + h
                if n:
                    pe.wait_ge(scores_read, 3 * n)
                if h == 0:
                    ring.wait_evacuated(pe, "q_T", i)
                q = q_T[:, h, :]
                for at in range(0, (i + 1) * P, BANK):
                    cols = min(BANK, (i + 1) * P - at)
                    nc.tensor.matmul(slc_ps[:, at:at + cols], q, k_T[0][:, at:at + cols], start=True, stop=True)
                first = max(0, i + 1 - WIN_TILES) * P
                span = (i + 1) * P - first
                for at in range(0, span, BANK):
                    cols = min(BANK, span - at)
                    nc.tensor.matmul(win_ps[:, at:at + cols], q, k_T[1][:, first + at:first + at + cols],
                                     start=True, stop=True)
                nc.tensor.matmul(win_ps[:, WINDOW + P:WINDOW + P + N_CMP], q, kc_T[:, :], start=True,
                                 stop=True).then_inc(scores_filled, 1)

            def head_values(i, h):
                n = i * HEADS + h
                kv = h // GROUP
                pe.wait_ge(probs_ready, 3 * (n + 1))
                groups = key_groups(i)
                if h == 0:
                    ring.wait_evacuated(pe, "vc", i)
                    pe.wait_ge(v_copied, i + 1)

                def values(g):
                    ring.wait_evacuated(pe, "probs_T", i, h, g)
                    for m, (_, keys, branch, j) in enumerate(groups[g]):
                        v = vc[i % 2][:, kv * HD:(kv + 1) * HD] if branch == COMPRESSED else \
                            v_all[:, j, branch - 1, kv * HD:(kv + 1) * HD]
                        same = [t for t in key_tiles(i) if t[2] == branch]
                        last = nc.tensor.matmul(o_ps[:, branch * HD:(branch + 1) * HD],
                                                probs_T[group_no[i, h, g] % 3][:keys, m * P:(m + 1) * P], v,
                                                start=(j == same[0][3]), stop=(j == same[-1][3]))
                    last.then_inc(values_done, 1)

                for g, group in enumerate(groups):
                    ring.wait_free(pe, "probs_T", i, h, g)
                    for m, (at, keys, branch, j) in enumerate(group):
                        last = nc.tensor.transpose(ring.bank("probs_T", i, h, g)[:keys, m * P:(m + 1) * P],
                                                   scores[n % 2][:, at:at + keys], identity[:, :])
                    last.then_inc(ring.is_filled("probs_T", i, h, g), 1)
                    if g == 0 and n:
                        pe.wait_ge(combined, 3 * n)
                    if g:
                        values(g - 1)
                values(len(groups) - 1)

            def gla_step(i, h):
                pr = proj[i % 2]
                if h == 0:
                    ring.wait_free(pe, "ga_T", i)
                    nc.tensor.transpose(ring.bank("ga_T", i)[:RANK, :P], pr[:, GA0:GA0 + RANK],
                                        identity[:, :]).then_inc(ring.is_filled("ga_T", i), 1)
                elif h == 1:
                    ring.wait_evacuated(pe, "ga_T", i)
                    ring.wait_free(pe, "z", i)
                    z = ring.bank("z", i)[:, :GLA_WIDTH]
                    nc.tensor.matmul(z, ga_T[:, :], w_a2[:, :], start=True, stop=False)
                    nc.tensor.matmul(z, ones_row[:, :], b_a[:, :], start=False, stop=True).then_inc(
                        ring.is_filled("z", i), 1)
                elif h == 2:
                    pe.wait_ge(log_a_ready, i + 1)
                    ring.wait_free(pe, "cum", i, 0)
                    bank = ring.bank("cum", i, 0)
                    nc.tensor.matmul(bank[:, :GLA_WIDTH], cum_upto[:, :], log_a[:, :], start=True, stop=True)
                    nc.tensor.matmul(bank[:, GLA_WIDTH:], cum_from_mid[:, :], log_a[:, :], start=True,
                                     stop=True).then_inc(ring.is_filled("cum", i, 0), 1)
                    ring.wait_free(pe, "cum", i, 1)
                    bank = ring.bank("cum", i, 1)
                    nc.tensor.matmul(bank[:, :GLA_WIDTH], cum_after[:, :], log_a[:, :], start=True, stop=True)
                    for pair in range(2):
                        last = nc.tensor.matmul(bank[:, GLA_WIDTH + 2 * pair:GLA_WIDTH + 2 * pair + 2],
                                                log_a[:, pair * P:(pair + 1) * P], in_chunk[:, :],
                                                start=True, stop=True)
                    last.then_inc(ring.is_filled("cum", i, 1), 1)
                elif h == 3:
                    pe.wait_ge(decayed_ready, 3 * (i + 1))
                    ring.wait_free(pe, "gla_T", i, 0)
                    bank = ring.bank("gla_T", i, 0)
                    for pair in range(2):
                        cols = slice(pair * P, (pair + 1) * P)
                        nc.tensor.transpose(bank[:, pair * P:(pair + 1) * P], q_decayed[:, 1, cols], identity[:, :])
                    for pair in range(2):
                        cols = slice(pair * P, (pair + 1) * P)
                        last = nc.tensor.transpose(bank[:, (2 + pair) * P:(3 + pair) * P], k_mid[:, cols],
                                                   identity[:, :])
                    last.then_inc(ring.is_filled("gla_T", i, 0), 1)
                    ring.wait_free(pe, "gla_T", i, 1)
                    bank = ring.bank("gla_T", i, 1)
                    for pair in range(2):
                        cols = slice(pair * P, (pair + 1) * P)
                        last = nc.tensor.transpose(bank[:, pair * P:(pair + 1) * P], q_decayed[:, 0, cols],
                                                   identity[:, :])
                    last.then_inc(ring.is_filled("gla_T", i, 1), 1)
                elif h == 4:
                    ring.wait_evacuated(pe, "gla_T", i, 0)
                    ring.wait_free(pe, "att", i)
                    for pair in range(2):
                        last = nc.tensor.matmul(ring.bank("att", i)[:, 2 * pair * P:2 * (pair + 1) * P],
                                                k_mid_T[:, pair, :],
                                                q_mid_T[:, pair, :, :].rearrange("p h t -> p (h t)"),
                                                start=True, stop=True)
                    last.then_inc(ring.is_filled("att", i), 1)
                elif h == 5:
                    gla_state(i, 0)
                elif h == 6:
                    pe.wait_ge(att_ready, i + 1)
                    ring.wait_evacuated(pe, "gla_T", i, 1)
                    ring.wait_evacuated(pe, "state", i, 0)
                    ring.wait_free(pe, "o", i)
                    bank = ring.bank("o", i)
                    for g in range(GLA_HEADS):
                        nc.tensor.matmul(bank[:, g * DV:(g + 1) * DV], att_T[:, g, :],
                                         pr[:, GV0 + g * DV:GV0 + (g + 1) * DV], start=(g == 0), stop=False,
                                         skip_group_check=True)
                    for c in range(2):
                        for pair in range(2):
                            last = nc.tensor.matmul(bank[:, 2 * pair * DV:2 * (pair + 1) * DV],
                                                    q_cum_T[c][:, pair, :],
                                                    state[c][:, pair, :, :].rearrange("p h e -> p (h e)"),
                                                    start=False, stop=(c == 1), skip_group_check=True)
                    last.then_inc(ring.is_filled("o", i), 1)
                elif h == 7:
                    gla_state(i, 1)

            def gla_state(i, c):
                pe.wait_ge(k_last_ready, 2 * (i + 1))
                ring.wait_free(pe, "state", i, c)
                for pair in range(2):
                    last = nc.tensor.matmul(ring.bank("state", i, c)[:, 2 * pair * DV:2 * (pair + 1) * DV],
                                            k_last[c][:, pair * P:(pair + 1) * P],
                                            proj[i % 2][:, GV0 + 2 * pair * DV:GV0 + 2 * (pair + 1) * DV],
                                            start=True, stop=True)
                last.then_inc(ring.is_filled("state", i, c), 1)

            project_x_T(0)
            for c in range(6):
                project(0, c)
            pe.wait_ge(tables_ready, 1)
            pe.wait_ge(consts_landed, 16 * CONSTS)
            transpose_qk(0)
            head_scores(0, 0)
            for i in range(PROMPT_TILES):
                for h in range(HEADS):
                    if h == 0:
                        project_x_T(i + 1)
                    elif h <= 6:
                        project(i + 1, h - 1)
                    gla_step(i, h)
                    if h == HEADS - 1 and i + 1 < PROMPT_TILES:
                        transpose_qk(i + 1)
                    if (i, h) != LAST_HEAD:
                        head_scores(*heads_from(i, h, 1))
                    head_values(i, h)

        @block.scalar
        def _(act):
            def square_x(i):
                r = ROWS[i]
                act.wait_ge(x_landed, 16 * (i + 1))
                if i:
                    ring.wait_filled(act, "proj", i - 1, 5)
                nc.scalar.activation(h_T[:r, :, :].rearrange("p k t -> p (k t)"), x_in[:r, :], ACT.Square,
                                     scale=D_MODEL ** -0.5, accum_out=mean_x[:r, i:i + 1]).then_inc(sq_x_ready, 1)

            def take_projection(i, c):
                r, n = ROWS[i], i % 2
                at, cols = IN_CHUNKS[c]
                act.wait_ge(rstd_x_ready, 2 * (i + 1))
                if i >= 2 and c == 0:
                    act.wait_ge(rows_stored[n], rows_stored_before(i))
                    act.wait_ge(v_copied, i - 1)
                    act.wait_ge(mix_gla_ready, i - 1)
                    ring.wait_filled(act, "state", i - 2, 1)
                ring.wait_filled(act, "proj", i, c)
                nc.scalar.activation(proj[n][:r, at:at + cols], ring.bank("proj", i, c)[:r, :cols], ACT.Copy,
                                     scale=rstd_x[:r, i:i + 1]).then_inc(ring.is_evacuated("proj", i, c), 1)

            def gate_exponentials(i):
                r = ROWS[i]
                if i >= 2:
                    act.wait_ge(combined, 3 * HEADS * (i - 1))
                ring.wait_evacuated(act, "proj", i, 2)
                nc.scalar.activation(gates[i % 2][:r, :], proj[i % 2][:r, GATE0:GATE0 + 3 * HEADS], ACT.Exp,
                                     scale=-1.0).then_inc(gate_exp, 1)

            def take_qk_T(i):
                if i:
                    act.wait_ge(scores_filled, HEADS * i)
                else:
                    act.wait_ge(tables_ready, 1)
                ring.wait_filled(act, "q_T", i)
                bank = ring.bank("q_T", i)
                for kv in range(KV_HEADS):
                    rows = slice(kv * HD, (kv + 1) * HD)
                    last = nc.scalar.activation(q_T[rows, kv * GROUP:(kv + 1) * GROUP, :],
                                                bank[rows, :].rearrange("p (g t) -> p g t", g=GROUP), ACT.Copy)
                last.then_inc(ring.is_evacuated("q_T", i), 1)

            def exponentials(i, h):
                n = i * HEADS + h
                act.wait_ge(neg_max_ready, n + 1)
                if n >= 2:
                    act.wait_ge(combined, 3 * (n - 1))
                s = scores[n % 2]
                for branch, (at, cols) in enumerate(branch_columns(i)):
                    nc.scalar.activation(s[:, at:at + cols], s[:, at:at + cols], ACT.Exp,
                                         bias=neg_max[n % 2][:, branch:branch + 1],
                                         accum_out=sums[n % 2][:, branch:branch + 1]).then_inc(probs_ready, 1)

            def gla_step(i, h):
                if h == 0:
                    ring.wait_filled(act, "ga_T", i)
                    nc.scalar.activation(ga_T[:, :], ring.bank("ga_T", i)[:RANK, :P], ACT.Copy).then_inc(
                        ring.is_evacuated("ga_T", i), 1)
                    if i:
                        act.wait_ge(mix_gla_ready, i)
                    nc.scalar.activation(silu[:, :], proj[i % 2][:, GG0:GG0 + GLA_HEADS * DV], ACT.Exp,
                                         scale=-1.0).then_inc(silu_exp, 1)
                elif h == 1:
                    act.wait_ge(abs_ready, i + 1)
                    nc.scalar.activation(log_a[:, :], log_a[:, :], ACT.Exp).then_inc(soft_step, 1)
                    act.wait_ge(soft_step, 2 * i + 1)
                    nc.scalar.activation(log_a[:, :], log_a[:, :], ACT.Ln, bias=1.0).then_inc(soft_step, 1)
                elif h == 2:
                    if i:
                        ring.wait_filled(act, "gla_T", i - 1, 1)
                        act.wait_ge(k_last_ready, 2 * i)
                    ring.wait_filled(act, "cum", i, 0)
                    bank = ring.bank("cum", i, 0)
                    nc.scalar.activation(q_decayed[:, :, :].rearrange("p a c -> p (a c)"), bank[:, :],
                                         ACT.Exp).then_inc(exps_ready, 1)
                    act.wait_ge(exps_ready, 4 * i + 1)
                    nc.scalar.activation(k_mid[:, :], bank[:, GLA_WIDTH:], ACT.Exp, scale=-1.0).then_inc(
                        ring.is_evacuated("cum", i, 0), 1)
                    ring.wait_evacuated(act, "cum", i, 0)
                    act.sem_inc(exps_ready, 1)
                    if i:
                        act.wait_ge(state_ready, 8 * i)
                    ring.wait_filled(act, "cum", i, 1)
                    bank = ring.bank("cum", i, 1)
                    nc.scalar.activation(k_decay[:, :], bank[:, :GLA_WIDTH], ACT.Exp).then_inc(exps_ready, 1)
                    nc.scalar.activation(decay[:, :, :].rearrange("p a c -> p (a c)"),
                                         bank[:, GLA_WIDTH:GLA_WIDTH + 4], ACT.Exp).then_inc(
                                             ring.is_evacuated("cum", i, 1), 1)
                    ring.wait_evacuated(act, "cum", i, 1)
                    act.sem_inc(exps_ready, 1)
                elif h == 3:
                    if i:
                        ring.wait_filled(act, "o", i - 1)
                    ring.wait_filled(act, "gla_T", i, 0)
                    bank = ring.bank("gla_T", i, 0)
                    for head in range(2):
                        rows = slice(head * DK, (head + 1) * DK)
                        nc.scalar.activation(q_mid_T[rows, :, head, :],
                                             bank[rows, :2 * P].rearrange("p (a t) -> p a t", a=2), ACT.Copy,
                                             scale=DK ** -0.5)
                    nc.scalar.activation(k_mid_T[:, :, :].rearrange("p a t -> p (a t)"), bank[:, 2 * P:],
                                         ACT.Copy).then_inc(ring.is_evacuated("gla_T", i, 0), 1)
                    ring.wait_filled(act, "gla_T", i, 1)
                    bank = ring.bank("gla_T", i, 1)
                    for c in range(2):
                        cols = slice(c * CHUNK, (c + 1) * CHUNK)
                        last = nc.scalar.activation(q_cum_T[c][:, :, cols],
                                                    bank[:, :2 * P].rearrange("p (a t) -> p a t", a=2)[:, :, cols],
                                                    ACT.Copy, scale=DK ** -0.5)
                    last.then_inc(ring.is_evacuated("gla_T", i, 1), 1)
                elif h == 6:
                    if i:
                        act.wait_ge(mix_gla_ready, i)
                    ring.wait_filled(act, "o", i)
                    nc.scalar.activation(o_gla[:, :, :].rearrange("p h e -> p (h e)"), ring.bank("o", i)[:, :],
                                         ACT.Copy).then_inc(ring.is_evacuated("o", i), 1)
                elif h == 7:
                    ring.wait_evacuated(act, "o", i)
                    if i:
                        act.wait_ge(o_mean_ready, i)
                    for g in range(GLA_HEADS):
                        last = nc.scalar.activation(norm_scratch[:, g, :], o_gla[:, g, :], ACT.Square,
                                                    scale=DV ** -0.5, accum_out=o_mean[:, g:g + 1])
                    last.then_inc(o_mean_ready, 1)

            square_x(0)
            for c in range(6):
                take_projection(0, c)
            gate_exponentials(0)
            take_qk_T(0)
            exponentials(0, 0)
            for i in range(PROMPT_TILES):
                for h in range(HEADS):
                    if h == 0:
                        square_x(i + 1)
                    elif h <= 6:
                        take_projection(i + 1, h - 1)
                    if h == 5:
                        gate_exponentials(i + 1)
                    gla_step(i, h)
                    if h == HEADS - 1 and i + 1 < PROMPT_TILES:
                        take_qk_T(i + 1)
                    take_probs_T(act, nc.scalar, i, h, 0)
                    if (i, h) != LAST_HEAD:
                        exponentials(*heads_from(i, h, 1))

        @block.vector
        def _(dve):
            def take_x_T(i):
                r = ROWS[i]
                dve.wait_ge(sq_x_ready, i + 1)
                for half in range(2):
                    ring.wait_filled(dve, "x_T", i, half)
                    ln = broadcast(ln_col[:, 4 * half:4 * half + 4].rearrange("p (k a) -> p k a", a=1), [P, 4, r])
                    nc.vector.tensor_tensor(h_T[:, 4 * half:4 * half + 4, :r],
                                            ring.bank("x_T", i, half)[:, :4 * r].rearrange("p (k t) -> p k t", k=4),
                                            ln, ALU.mult).then_inc(ring.is_evacuated("x_T", i, half), 1)
                    ring.wait_evacuated(dve, "x_T", i, half)
                    dve.sem_inc(h_T_ready, 1)

            def norm_sums(i):
                r = ROWS[i]
                pr = proj[i % 2]
                ring.wait_evacuated(dve, "proj", i, 0)
                if i:
                    dve.wait_ge(norm_step, 4 * i)
                q = pr[:r, Q0:Q0 + NSA_WIDTH]
                nc.vector.tensor_tensor(norm_sq[:r, :], q, q, ALU.mult).then_inc(norm_step, 1)
                dve.wait_ge(norm_step, 4 * i + 1)
                nc.vector.tensor_reduce(norm_mean[:r, 0:8], norm_sq[:r, :].rearrange("p (h d) -> p h d", d=HD),
                                        AX.X, ALU.add).then_inc(norm_step, 1)
                ring.wait_evacuated(dve, "proj", i, 1)
                ring.wait_evacuated(dve, "proj", i, 2)
                dve.wait_ge(norm_step, 4 * i + 2)
                k = pr[:r, KV0:KV0 + KV_COLS].rearrange("p (s c) -> p s c", s=6)[:, 0:6:2, :]
                sq = norm_sq[:r, 0:3 * P].rearrange("p (s c) -> p s c", s=3)
                nc.vector.tensor_tensor(sq, k, k, ALU.mult).then_inc(norm_step, 1)
                dve.wait_ge(norm_step, 4 * i + 3)
                nc.vector.tensor_reduce(norm_mean[:r, 8:14], norm_sq[:r, 0:3 * P].rearrange("p (h d) -> p h d", d=HD),
                                        AX.X, ALU.add).then_inc(norm_step, 1)
                dve.wait_ge(norm_step, 4 * i + 4)
                dve.sem_inc(norm_mean_ready, 1)

            def apply_norms(i):
                r = ROWS[i]
                pr = proj[i % 2]
                q = pr[:r, Q0:Q0 + NSA_WIDTH].rearrange("p (h d) -> p h d", d=HD)
                dve.wait_ge(norm_rstd_ready, 2 * (i + 1))
                nc.vector.tensor_tensor(q, q, broadcast(norm_rstd[:r, 0:8].rearrange("p (h a) -> p h a", a=1),
                                                        [r, HEADS, HD]), ALU.mult).then_inc(qk_normed, 1)
                k = pr[:r, KV0:KV0 + KV_COLS].rearrange("p (s c) -> p s c", s=6)[:, 0:6:2, :]
                k4 = k.rearrange("p s (h d) -> p s h d", d=HD)
                r4 = norm_rstd[:r, 8:14].rearrange("p (s h a) -> p s h a", s=3, a=1)
                nc.vector.tensor_tensor(k4, k4, broadcast(r4, [r, 3, KV_HEADS, HD]), ALU.mult).then_inc(qk_normed, 1)
                dve.wait_ge(qk_normed, 4 * i + 2)
                if i:
                    ring.wait_filled(dve, "q_T", i - 1)
                nc.vector.tensor_tensor(
                    q_paired[:r, :].rearrange("p (g k d) -> p k g d", g=GROUP, k=KV_HEADS),
                    pr[:r, Q0:Q0 + NSA_WIDTH].rearrange("p (k g d) -> p k g d", k=KV_HEADS, g=GROUP),
                    q_gain[:r, :, :].rearrange("p (k g) d -> p k g d", k=KV_HEADS), ALU.mult).then_inc(qk_normed, 1)
                g4 = k_gain[:r, :, :].rearrange("p s (a d) -> p s a d", a=1)
                nc.vector.tensor_tensor(k4, k4, broadcast(g4, [r, 3, KV_HEADS, HD]), ALU.mult).then_inc(qk_normed, 1)
                g = gates[i % 2][:r, :]
                dve.wait_ge(gate_exp, i + 1)
                nc.vector.tensor_scalar(g, g, 1.0, None, ALU.add).then_inc(gates_ready, 1)
                dve.wait_ge(gates_ready, 2 * i + 1)
                nc.vector.reciprocal(g, g).then_inc(gates_ready, 1)

            def take_kc(i):
                ring.wait_filled(dve, "k_T", i)
                bank = ring.bank("k_T", i)
                blocks = slice(4 * i, 4 * i + 4)
                for n in range(2):
                    nc.vector.tensor_copy(k_T[n][:, i * P:(i + 1) * P], bank[:, n * P:(n + 1) * P])
                if i:
                    dve.wait_ge(scores_filled, HEADS * i)
                nc.vector.tensor_copy(kc_T[:, blocks], bank[:, 2 * P:2 * P + 4])
                nc.vector.tensor_copy(vc_T[:, blocks], bank[:, 2 * P + 4:2 * P + 8]).then_inc(
                    ring.is_evacuated("k_T", i), 1)
                ring.wait_filled(dve, "vc", i)
                if i >= 2:
                    dve.wait_ge(values_done, last_group[i - 2, HEADS - 1] + 1)
                nc.vector.tensor_copy(vc[i % 2][:, :], ring.bank("vc", i)[:N_CMP, :P]).then_inc(
                    ring.is_evacuated("vc", i), 1)

            def bias_and_max(i, h):
                n = i * HEADS + h
                dve.wait_ge(scores_filled, n + 1)
                if n >= 2:
                    prev = heads_from(i, h, -2)
                    ring.wait_filled(dve, "probs_T", *prev, len(key_groups(prev[0])) - 1)
                first = max(0, i + 1 - WIN_TILES)
                span = (i + 1 - first) * P
                for branch, (at, cols, ps, dist) in enumerate((
                        (CMP_AT, N_CMP, win_ps[:, WINDOW + P:WINDOW + P + N_CMP],
                         cmp_dist[:, N_CMP - 4 - 4 * i:2 * N_CMP - 4 - 4 * i]),
                        (SLC_AT, (i + 1) * P, slc_ps[:, 0:(i + 1) * P], slc_dist[:, SEQ - (i + 1) * P:]),
                        (WIN_AT, span, win_ps[:, 0:span], win_dist[:, WINDOW + P - span:]))):
                    nc.vector.tensor_tensor_reduce(out=scores[n % 2][:, at:at + cols], in0=ps, in1=dist, scale=SLOPES[h],
                                                   scalar=MASKED, op0=ALU.add, op1=ALU.max,
                                                   accum_out=maxima[:, branch:branch + 1]).then_inc(scores_read, 1)
                dve.wait_ge(scores_read, 3 * (n + 1))
                nc.vector.tensor_scalar(neg_max[n % 2][:, :], maxima[:, :], -1.0, 1e26, ALU.mult, ALU.min).then_inc(
                    neg_max_ready, 1)

            def combine(i, h):
                n = i * HEADS + h
                dve.wait_ge(probs_ready, 3 * (n + 1))
                nc.vector.tensor_scalar(weight[:, :], sums[n % 2][:, :], 1e-30, None, ALU.max).then_inc(weight_step, 1)
                dve.wait_ge(weight_step, 3 * n + 1)
                nc.vector.reciprocal(weight[:, :], weight[:, :]).then_inc(weight_step, 1)
                dve.wait_ge(weight_step, 3 * n + 2)
                dve.wait_ge(gates_ready, 2 * (i + 1))
                nc.vector.tensor_tensor(weight[:, :], weight[:, :],
                                        gates[i % 2][:, :].rearrange("p (b h) -> p b h", b=3)[:, :, h],
                                        ALU.mult).then_inc(weight_step, 1)
                dve.wait_ge(weight_step, 3 * n + 3)
                dve.wait_ge(values_done, last_group[i, h] + 1)
                if h == 0 and i:
                    dve.wait_ge(mix_stored, 16 * i)
                out = mix[:, h * HD:(h + 1) * HD]
                nc.vector.tensor_scalar(out, o_ps[:, 0:HD], weight[:, 0:1], None, ALU.mult).then_inc(combined, 1)
                for branch in (1, 2):
                    dve.wait_ge(combined, 3 * n + branch)
                    nc.vector.scalar_tensor_tensor(out=out, in0=o_ps[:, branch * HD:(branch + 1) * HD],
                                                   scalar=weight[:, branch:branch + 1], in1=out, op0=ALU.mult,
                                                   op1=ALU.add).then_inc(combined, 1)

            def gla_step(i, h):
                if h == 0:
                    dve.wait_ge(silu_step, 2 * i + 1)
                    nc.vector.reciprocal(silu[:, :], silu[:, :]).then_inc(silu_step, 1)
                    dve.wait_ge(silu_step, 2 * i + 2)
                    dve.sem_inc(silu_ready, 1)
                elif h == 1:
                    if i:
                        dve.wait_ge(log_a_ready, i)
                        ring.wait_filled(dve, "cum", i - 1, 1)
                    ring.wait_filled(dve, "z", i)
                    z = ring.bank("z", i)[:, :GLA_WIDTH]
                    nc.vector.tensor_scalar(z_min[:, :], z, 0.0, None, ALU.min).then_inc(abs_step, 1)
                    dve.wait_ge(abs_step, i + 1)
                    nc.vector.scalar_tensor_tensor(out=log_a[:, :], in0=z, scalar=-1.0, in1=z_min[:, :],
                                                   op0=ALU.mult, op1=ALU.min).then_inc(ring.is_evacuated("z", i), 1)
                    ring.wait_evacuated(dve, "z", i)
                    dve.sem_inc(abs_ready, 1)
                elif h == 4:
                    if i:
                        ring.wait_filled(dve, "o", i - 1)
                    else:
                        dve.wait_ge(tables_ready, 1)
                    ring.wait_filled(dve, "att", i)
                    keep = broadcast(cum_upto[:, :].bitcast(U32).rearrange("p (a t) -> p a t", a=1),
                                     [P, GLA_HEADS, P])
                    nc.vector.copy_predicated(att_T[:, :, :], keep,
                                              ring.bank("att", i)[:, :].rearrange("p (h t) -> p h t", h=GLA_HEADS)
                                              ).then_inc(ring.is_evacuated("att", i), 1)
                    ring.wait_evacuated(dve, "att", i)
                    dve.sem_inc(att_ready, 1)
                elif h == 2:
                    if i:
                        ring.wait_filled(dve, "state", i - 1, 1)
                    dve.wait_ge(exps_ready, 4 * (i + 1))
                    for c in range(2):
                        rows = slice(c * CHUNK, (c + 1) * CHUNK)
                        nc.vector.tensor_tensor(k_last[c][rows, :], k_decay[rows, :],
                                                proj[i % 2][rows, GK0:GK0 + GLA_WIDTH], ALU.mult).then_inc(
                                                    k_last_ready, 1)
                elif h == 5:
                    update_state(i, 0)
                elif h == 7:
                    update_state(i, 1)

            def update_state(i, c):
                dve.wait_ge(exps_ready, 4 * (i + 1))
                if c == 1:
                    ring.wait_filled(dve, "o", i)
                elif i:
                    ring.wait_filled(dve, "o", i - 1)
                dve.wait_ge(state_ready, 4 * (2 * i + c)) if (i or c) else None
                ring.wait_filled(dve, "state", i, c)
                bank = ring.bank("state", i, c)[:, :].rearrange("p (a h e) -> p a h e", a=2, h=2)
                for pair in range(2):
                    for head in range(2):
                        rows = slice(head * DK, (head + 1) * DK)
                        last = nc.vector.scalar_tensor_tensor(
                            out=state[1 - c][rows, pair, head, :], in0=state[c][rows, pair, head, :],
                            scalar=decay[rows, pair, c:c + 1], in1=bank[rows, pair, head, :],
                            op0=ALU.mult, op1=ALU.add).then_inc(
                                state_ready if (pair, head) != (1, 1) else ring.is_evacuated("state", i, c), 1)
                ring.wait_evacuated(dve, "state", i, c)
                dve.sem_inc(state_ready, 1)

            dve.wait_ge(consts_landed, 16 * CONSTS)
            dve.wait_ge(tables_step, 13)
            nc.vector.memset(cum_upto[0:CHUNK, CHUNK:P], 0.0)
            nc.vector.memset(cum_after[CHUNK:P, 0:CHUNK], 0.0)
            for c in range(2):
                s0 = c * CHUNK
                nc.vector.memset(in_chunk[s0:s0 + CHUNK, c:c + 1], 1.0 / TAU)
                nc.vector.memset(cum_from_mid[s0:s0 + CHUNK // 2, s0:s0 + CHUNK], 1.0 / TAU).then_inc(dve_tables, 1)
            dve.wait_ge(dve_tables, 2)
            nc.vector.tensor_tensor(cum_from_mid[:, :], cum_upto[:, :], cum_from_mid[:, :],
                                    ALU.subtract).then_inc(tables_ready, 1)
            for h in range(HEADS):
                last = nc.vector.tensor_scalar(q_gain[:, h, :], q_gain[:, h, :], SCALE / SLOPES[h], None, ALU.mult)
            last.then_inc(gain_ready, 1)
            dve.wait_ge(gain_ready, 1)
            take_x_T(0)
            norm_sums(0)
            apply_norms(0)
            take_kc(0)
            bias_and_max(0, 0)
            for i in range(PROMPT_TILES):
                for h in range(HEADS):
                    if h == 0:
                        take_x_T(i + 1)
                    elif h == 5:
                        norm_sums(i + 1)
                    elif h == 6:
                        apply_norms(i + 1)
                    gla_step(i, h)
                    if h == HEADS - 1 and i + 1 < PROMPT_TILES:
                        take_kc(i + 1)
                    early = h >= 6
                    if early and (i, h) != LAST_HEAD:
                        bias_and_max(*heads_from(i, h, 1))
                    take_probs_T(dve, nc.vector, i, h, 1)
                    if not early:
                        bias_and_max(*heads_from(i, h, 1))
                    combine(i, h)


PAIRS = DEC_BATCH // 2
PAIR_ROWS = 2 * HEADS * DEC_SEQ
B_ROWS = HEADS * DEC_SEQ
PAGE_GROUP = 4
PAGE_PLACES = 4
GROUPS = N_PAGES // PAGE_GROUP
KEYS = PAST_LEN + DEC_SEQ
N_SEL = -(-KEYS // SEL_BLOCK)
PAST_CMP = PAST_LEN // CMP_BLOCK
PAGE_BLOCKS = PAGE_SIZE // CMP_BLOCK
QUADRANT = 32
QUADRANT_PAGES = QUADRANT // PAGE_BLOCKS
FORCE_SCORE = 1e4
RECENT = WINDOW + DEC_SEQ

NEG_T = 0
SLOPE = 1
NEG_SLOPE = 2
NEW_DIST = 3
WIN_OLD = NEW_DIST + DEC_SEQ
GROUP_SUM = WIN_OLD + DEC_SEQ
UPTO = GROUP_SUM + P
AFTER = UPTO + SAMPLE_ROWS
OF_SAMPLE = AFTER + SAMPLE_ROWS
IS_SAMPLE = OF_SAMPLE + DEC_BATCH
CONST_COLS = IS_SAMPLE + DEC_BATCH


def sample_constants():
    import numpy as np

    out = np.zeros((P, CONST_COLS), np.float32)
    row = np.arange(P)
    t = row % DEC_SEQ
    head = row // DEC_SEQ % HEADS
    out[:, NEG_T] = -t
    out[:, SLOPE] = np.array(SLOPES)[head]
    out[:, NEG_SLOPE] = -out[:, SLOPE]
    j = np.arange(DEC_SEQ)
    out[:, NEW_DIST:NEW_DIST + DEC_SEQ] = np.where(j <= t[:, None], j - t[:, None], MASKED)
    out[:, WIN_OLD:WIN_OLD + DEC_SEQ] = np.where(j > t[:, None], j - WINDOW - t[:, None], MASKED)
    kv = row // (GROUP * DEC_SEQ)
    out[:, GROUP_SUM:GROUP_SUM + P] = (kv[:, None] == kv) & (t[:, None] == t)
    s = np.arange(SAMPLE_ROWS)
    same = (s[:, None] // DEC_SEQ) == (s // DEC_SEQ)
    out[:SAMPLE_ROWS, UPTO:UPTO + SAMPLE_ROWS] = (same & (s[:, None] <= s)) / TAU
    out[:SAMPLE_ROWS, AFTER:AFTER + SAMPLE_ROWS] = (same & (s[:, None] > s)) / TAU
    mine = (s[:, None] // DEC_SEQ) == np.arange(DEC_BATCH)
    out[:SAMPLE_ROWS, OF_SAMPLE:OF_SAMPLE + DEC_BATCH] = mine / TAU
    out[:SAMPLE_ROWS, IS_SAMPLE:IS_SAMPLE + DEC_BATCH] = mine
    return out


def samples_stage(nc, a, outs, mix_rows, branch_rows, shared):
    proj, q_paired, identity = shared.proj0, shared.q_paired, shared.identity
    R = SAMPLE_ROWS
    with ExitStack() as ctx:
        def sb(name, shape, dtype=F32):
            return ctx.enter_context(nc.sbuf_tensor(name, shape, dtype))

        sem = ctx.enter_context(stage_semaphores(nc, "samples"))

        consts = sb("sample_consts_sb", [P, CONST_COLS])
        pages = sb("page_numbers", [1, DEC_BATCH * N_PAGES], I32)
        group_dist = sb("group_dist", [P, BANK])
        cmp_dist = sb("past_cmp_dist", [P, PAST_CMP])
        win_dist = sb("past_win_dist", [P, WINDOW])
        page = sb("pages", [P, PAGE_PLACES * PAGE_GROUP, 4 * KV_HEADS * HD])
        page_k_T = [sb(f"page_k_T{n}", [P, BANK]) for n in range(2)]
        values = [sb(f"values{n}", [P, 2, N_PAGES, KV_HEADS * HD]) for n in range(2)]
        kc_T = [sb(f"past_kc_T{n}", [P, 2, PAST_CMP]) for n in range(2)]
        kc = sb("past_kc", [P, 2, KV_HEADS * HD])
        vc = [sb(f"past_vc{n}", [P, 2, KV_HEADS * HD]) for n in range(2)]
        cmp_window = sb("cmp_window", [P, 2, 2 * QUADRANT - PAGE_BLOCKS])
        slc = [sb(f"slc_scores{n}", [P, KEYS]) for n in range(2)]
        win = sb("win_scores", [P, RECENT])
        cmp = sb("cmp_scores", [P, PAST_CMP])
        win_kv = sb("win_kv", [P, 2, WINDOW // P, 2 * KV_HEADS * HD])
        win_k_T = sb("win_k_T", [P, 2, WINDOW])
        q_T = sb("sample_q_T", [P, DEC_BATCH, KV_HEADS, GROUP, DEC_SEQ])
        new_k_T = sb("new_k_T", [P, 2, SAMPLE_ROWS])
        new_v = sb("new_v", [DEC_SEQ, 2, DEC_BATCH, KV_HEADS * HD])
        probs_T = [sb(f"sample_probs_T{n}", [P, BANK]) for n in range(3)]
        maxima = sb("sample_maxima", [P, 4])
        neg_max = sb("sample_neg_max", [P, 3])
        sums = sb("sample_sums", [P, 3])
        weight = sb("sample_weight", [P, 3])
        ranking = sb("ranking", [P, N_SEL])
        top8 = sb("top8", [P, 8])
        unselected = sb("unselected", [P, N_SEL])
        branch_out = sb("branch_out", [P, 3, KV_HEADS * HD])
        mix = sb("sample_mix", [R, GLA_HEADS * DV])
        ga_T = sb("sample_ga_T", [RANK, R])
        z_min = sb("sample_z_min", [R, GLA_WIDTH])
        log_a = sb("sample_log_a", [R, GLA_WIDTH])
        q_cum = sb("sample_q_cum", [R, GLA_WIDTH])
        k_cum = sb("sample_k_cum", [R, GLA_WIDTH])
        k_last = sb("sample_k_last", [R, GLA_WIDTH])
        decay = sb("sample_decay", [P, 2, DEC_BATCH])
        o_gla = sb("sample_o_gla", [R, GLA_HEADS, DV])
        o_mean = sb("sample_o_mean", [R, GLA_HEADS])
        o_rstd = sb("sample_o_rstd", [R, GLA_HEADS])
        silu = sb("sample_silu", [R, GLA_HEADS * DV])
        k_own = slc[1][:R, 0:DEC_BATCH * GLA_WIDTH].rearrange("p (b c) -> p b c", b=DEC_BATCH)
        at = DEC_BATCH * GLA_WIDTH
        q_own_T = slc[1][:, at:at + 2 * DEC_BATCH * (R + DEC_SEQ)].rearrange("p (a b t) -> p a b t", a=2, b=DEC_BATCH)
        at += 2 * DEC_BATCH * (R + DEC_SEQ)
        q_pair_T = slc[1][:, at:at + 4 * R].rearrange("p (a h t) -> p a h t", a=2, h=2)
        k_cum_T = slc[1][:, at + 4 * R:at + 6 * R].rearrange("p (a t) -> p a t", a=2)
        att_T = slc[1][:R, at + 6 * R:at + 10 * R].rearrange("p (h t) -> p h t", h=GLA_HEADS)
        squares = mix[:, :].rearrange("p (h e) -> p h e", h=GLA_HEADS)
        state = values[1][:, 0, :, :].rearrange("p n c -> p (n c)").rearrange(
            "p (a b h e) -> p a b h e", a=2, b=DEC_BATCH, h=2)

        consts_landed = sem("sample_consts_landed")
        pages_landed = sem("page_numbers_landed")
        page_landed = [sem(f"page_landed{n}") for n in range(PAGE_PLACES * PAGE_GROUP)]
        state_cleared = sem("state_cleared")
        state_landed = sem("gla_state_landed")
        rows_out = sem("sample_rows_out")
        new_rows_out = sem("new_rows_out")
        new_v_landed = sem("new_v_landed")
        win_landed = sem("win_kv_landed")
        cleared = sem("buffers_cleared")
        tables_step = sem("sample_tables_step")
        tables_ready = sem("sample_tables_ready")
        pages_read = sem("pages_read")
        values_copied = sem("values_copied")
        setup_T = sem("setup_T_ready")
        cmp_taken = sem("cmp_taken")
        window_ready = sem("cmp_window_ready")
        scores_ready = sem("sample_scores_ready")
        dve_step = sem("sample_dve_step")
        neg_max_ready = sem("sample_neg_max_ready")
        probs_ready = sem("sample_probs_ready")
        cmp_normed = sem("cmp_probs_normed")
        values_done = sem("sample_values_done")
        branch_taken = sem("branch_taken")
        branch_stored = sem("branch_stored")
        mix_ready = sem("sample_mix_ready")
        mix_out = sem("sample_mix_out")
        soft_step = sem("sample_soft_step")
        abs_ready = sem("sample_abs_ready")
        log_a_ready = sem("sample_log_a_ready")
        exps_ready = sem("sample_exps_ready")
        decayed_ready = sem("sample_decayed_ready")
        k_own_ready = sem("k_own_ready")
        att_ready = sem("sample_att_ready")
        silu_step = sem("sample_silu_step")
        state_step = sem("sample_state_step")
        state_out = sem("sample_state_out")
        o_mean_ready = sem("sample_o_mean_ready")
        o_step = sem("sample_o_step")

        cmp_ps = ctx.enter_context(nc.psum_tensor("cmp_ps", [PAST_CMP, 2, KV_HEADS * HD], F32))
        slc_out = ctx.enter_context(nc.psum_tensor("slc_out", [P, BANK], F32))
        short_out = ctx.enter_context(nc.psum_tensor("short_out", [P, BANK], F32))

        KEY_TILES = N_PAGES + 1
        SLC_TURNS = -(-KEY_TILES // 4)
        TAIL = [[("cmp",), ("new",)], [("win_k", 0), ("win_k", 1)], [("imp",), ("cmp_T",)],
                [("win", 0), ("win", 1)], [], [], [("win_T", 0), ("win_T", 1)]] + [
                    [("slc_T", g)] for g in range(SLC_TURNS)]
        GLA = [[("ga_T",)], [("z",)], [("cum",), ("decay",)], [("gla_T",)], [("att",)], [("o",)]] + [
            [("state", b)] for b in range(DEC_BATCH)]
        SLOTS = 2 * GROUPS
        assert len(TAIL) == SLOTS and len(GLA) <= SLOTS

        def scored(pair, slot):
            n = pair * SLOTS + slot
            return divmod(n - 1, SLOTS) if 1 <= n <= PAIRS * SLOTS else None

        def compressed(pair, slot):
            n = pair * SLOTS + slot
            return divmod(n // GROUPS - 1, 2) if n and n % GROUPS == 0 and n <= PAIRS * SLOTS else None

        order = [("q_T",), ("new_k_T",)]
        for pair in range(PAIRS + 1):
            for slot in range(SLOTS):
                if compressed(pair, slot):
                    order += [("kc_T", *compressed(pair, slot))]
                if pair < PAIRS:
                    order += [("page_T", pair, slot)]
                if scored(pair, slot):
                    order += [("page_scores", *scored(pair, slot))]
                if pair:
                    order += [(key[0], pair - 1, *key[1:]) for key in TAIL[slot]]
                elif slot < len(GLA):
                    order += GLA[slot]
        ring = turns(nc, ctx, sem, "sample_bank", 5, order)
        places = {}
        for pair in range(PAIRS):
            for key in [("cmp_T",), ("win_T", 0), ("win_T", 1)] + [("slc_T", g) for g in range(SLC_TURNS)]:
                places[(key[0], pair, *key[1:])] = len(places)
        N_PLACES_PER_PAIR = 3 + SLC_TURNS

        block = ctx.enter_context(nc.Block())
        samples = [2 * pair + b for pair in range(PAIRS) for b in range(2)]

        @block.sync
        def _(sp):
            sp.dma_start(pages[:, :], a["page_table"].rearrange("(a b) n -> a (b n)", a=1)).then_inc(pages_landed, 16)
            sp.dma_start(consts[:, :], a["sample_consts"]).then_inc(consts_landed, 16)
            sp.wait_ge(pages_landed, 16)

            def load_group(place, n):
                _, numbers = nc.values_load_multi_w_load_instructions(
                    pages[0:1, bass.ds(n, PAGE_GROUP)], engines=(mybir.EngineType.SP,), min_val=0,
                    max_val=a["cache_nsa_kv"].shape[1] - 1)
                for j, number in enumerate(numbers):
                    slot = place * PAGE_GROUP + j
                    sp.dma_start(page[:, slot, :], a["cache_nsa_kv"][0, bass.ds(number, 1)].rearrange(
                        "a p s h d -> (a p) (s h d)")).then_inc(page_landed[slot], 16)

            for place in range(PAGE_PLACES):
                load_group(place, place * PAGE_GROUP)
            with nc.sync.Fori(1, DEC_BATCH * N_PAGES // (PAGE_PLACES * PAGE_GROUP)) as it:
                for place in range(PAGE_PLACES):
                    sp.wait_ge(pages_read, PAGE_PLACES * (it - 1) + place + 1)
                    sp.wait_ge(values_copied, PAGE_PLACES * (it - 1) + place + 1)
                    sp.wait_ge(pages_landed, 16)
                    load_group(place, PAGE_PLACES * PAGE_GROUP * it + place * PAGE_GROUP)
            sp.wait_ge(mix_ready, 1)
            sp.dma_start(mix_rows[SEQ:TOKENS, NSA_WIDTH:], mix[:, :]).then_inc(mix_out, 16)
            sp.wait_ge(mix_out, 16)

        @block.gpsimd
        def _(pool):
            nc.gpsimd.memset(q_T[:, :, :, :, :], 0.0).then_inc(cleared, 1)
            nc.gpsimd.memset(cmp_window[:, :, :], 0.0).then_inc(window_ready, 1)
            pool.wait_ge(window_ready, 1)
            at = QUADRANT - PAGE_BLOCKS
            nc.gpsimd.tensor_copy(cmp_window[:, :, at:at + PAGE_BLOCKS], shared.cmp_w[:, :, :]).then_inc(
                window_ready, 1)
            nc.gpsimd.memset(state, 0.0).then_inc(state_cleared, 1)
            nc.gpsimd.memset(q_pair_T, 0.0)
            nc.gpsimd.memset(q_own_T, 0.0)
            nc.gpsimd.memset(att_T, 0.0).then_inc(cleared, 1)
            for table, pattern, base in ((group_dist, [[1, BANK]], -PAST_LEN),
                                         (cmp_dist, [[CMP_BLOCK, PAST_CMP]], CMP_BLOCK - 1 - PAST_LEN),
                                         (win_dist, [[1, WINDOW]], -WINDOW)):
                nc.gpsimd.iota(table[:, :], pattern=pattern, base=base, channel_multiplier=0,
                               allow_small_or_imprecise_dtypes=True).then_inc(tables_step, 1)
            pool.wait_ge(tables_step, 3)
            pool.wait_ge(consts_landed, 16)
            for table in (group_dist, cmp_dist, win_dist):
                nc.gpsimd.tensor_scalar(table[:, :], table[:, :], consts[:, NEG_T:NEG_T + 1], None,
                                        ALU.add).then_inc(tables_step, 1)
            pool.wait_ge(tables_step, 6)
            nc.gpsimd.tensor_copy(win_dist[:, 0:DEC_SEQ], consts[:, WIN_OLD:WIN_OLD + DEC_SEQ]).then_inc(
                tables_ready, 1)

            def gla_decayed():
                gq, gk = proj[:R, GQ0:GQ0 + GLA_WIDTH], proj[:R, GK0:GK0 + GLA_WIDTH]
                pool.wait_ge(exps_ready, 4)
                for x, by in ((q_cum, gq), (k_cum, gk), (k_last, gk)):
                    nc.gpsimd.tensor_tensor(x[:, :], x[:, :], by, ALU.mult).then_inc(decayed_ready, 1)
                pool.wait_ge(decayed_ready, 3)

            def gla_finish():
                pool.wait_ge(o_mean_ready, GLA_HEADS)
                nc.gpsimd.tensor_scalar(o_rstd[:, :], o_mean[:, :], EPS, None, ALU.add).then_inc(o_step, 1)
                pool.wait_ge(o_step, 1)
                nc.gpsimd.tensor_tensor(o_rstd[:, :], o_rstd[:, :], shared.minus_half[:R, 0:GLA_HEADS],
                                        ALU.pow).then_inc(o_step, 1)
                pool.wait_ge(silu_step, 2)
                heads = [R, GLA_HEADS, DV]
                factors = [broadcast(o_rstd[:, :].rearrange("p (h a) -> p h a", a=1), heads),
                           broadcast(shared.gla_gain[:R, :].rearrange("p (a e) -> p a e", a=1), heads),
                           silu[:, :].rearrange("p (h e) -> p h e", h=GLA_HEADS),
                           proj[:R, GG0:GG0 + GLA_HEADS * DV].rearrange("p (h e) -> p h e", h=GLA_HEADS)]
                for n, factor in enumerate(factors):
                    pool.wait_ge(o_step, 2 + n)
                    out = o_gla[:, :, :] if n < 3 else mix[:, :].rearrange("p (h e) -> p h e", h=GLA_HEADS)
                    nc.gpsimd.tensor_tensor(out, o_gla[:, :, :], factor, ALU.mult).then_inc(
                        o_step if n < 3 else mix_ready, 1)

            def store_branches(pair):
                pool.wait_ge(branch_taken, 3 * (pair + 1))
                for b in range(2):
                    for kv in range(KV_HEADS):
                        row = b * R + kv * GROUP * DEC_SEQ
                        pool.dma_start(branch_rows[2 * pair + b, kv].rearrange("g t s d -> (g t) s d"),
                                       branch_out[row:row + GROUP * DEC_SEQ, :, kv * HD:(kv + 1) * HD]).then_inc(
                                           branch_stored, 16)

            for pair in range(PAIRS):
                for slot in range(SLOTS):
                    b, g = slot // GROUPS, slot % GROUPS
                    n = pair * SLOTS + slot
                    place = n % PAGE_PLACES
                    if slot == 0 and pair == 1:
                        pool.wait_ge(state_out, 16 * GLA_HEADS)
                    if slot % GROUPS == 0 and pair >= 2:
                        pool.wait_ge(values_done, N_PLACES_PER_PAIR * (pair - 1))
                    for j in range(PAGE_GROUP):
                        pool.wait_ge(page_landed[place * PAGE_GROUP + j], 16 * (n // PAGE_PLACES + 1))
                    nc.gpsimd.tensor_copy(
                        values[pair % 2][:, b, g * PAGE_GROUP:(g + 1) * PAGE_GROUP, :],
                        page[:, place * PAGE_GROUP:(place + 1) * PAGE_GROUP, 3 * P:4 * P]).then_inc(values_copied, 1)
                    if pair == 0 and slot == 1:
                        pool.wait_ge(soft_step, 2)
                        nc.gpsimd.tensor_tensor(log_a[:, :], z_min[:, :], log_a[:, :], ALU.subtract).then_inc(
                            log_a_ready, 1)
                    if pair == 0 and slot == 2:
                        gla_decayed()
                    if pair == 0 and slot == 8:
                        gla_finish()
                if pair:
                    store_branches(pair - 1)
            store_branches(PAIRS - 1)
            pool.wait_ge(branch_stored, 16 * 4 * PAIRS)

        @block.tensor
        def _(pe):
            ring.wait_free(pe, "q_T")
            for g in range(GROUP):
                last = nc.tensor.transpose(ring.bank("q_T")[:, g * R:(g + 1) * R], q_paired[:R, g * P:(g + 1) * P],
                                           identity[:R, :R])
            last.then_inc(ring.is_filled("q_T"), 1)
            for n, stream in enumerate((2, 4)):
                at = KV0 + stream * P
                last = nc.tensor.transpose(ring.bank("new_k_T")[:, n * R:(n + 1) * R], proj[:R, at:at + P],
                                           identity[:R, :R])
            last.then_inc(ring.is_filled("new_k_T"), 1)
            ring.wait_evacuated(pe, "q_T")
            ring.wait_evacuated(pe, "new_k_T")
            pe.wait_ge(consts_landed, 16)

            def q_of(pair, b):
                return q_T[:, 2 * pair + b, :, :, :].rearrange("p k g t -> p (k g t)")

            def page_group(pair, slot):
                b, g = slot // GROUPS, slot % GROUPS
                n = pair * SLOTS + slot
                place = n % PAGE_PLACES
                for j in range(PAGE_GROUP):
                    pe.wait_ge(page_landed[place * PAGE_GROUP + j], 16 * (n // PAGE_PLACES + 1))
                ring.wait_free(pe, "page_T", pair, slot)
                for j in range(PAGE_GROUP):
                    last = nc.tensor.transpose(ring.bank("page_T", pair, slot)[:, j * P:(j + 1) * P],
                                               page[:, place * PAGE_GROUP + j, 2 * P:3 * P], identity[:, :])
                last.then_inc(ring.is_filled("page_T", pair, slot), 1)
                if g == 0 and (pair or b):
                    pe.wait_ge(cmp_taken, 2 * pair + b)
                for j in range(PAGE_GROUP):
                    n_page = g * PAGE_GROUP + j
                    place_in = n_page % QUADRANT_PAGES
                    rows = slice(n_page // QUADRANT_PAGES * QUADRANT, (n_page // QUADRANT_PAGES + 1) * QUADRANT)
                    at = QUADRANT - PAGE_BLOCKS - place_in * PAGE_BLOCKS
                    for which in range(2):
                        last = nc.tensor.matmul(cmp_ps[rows, which, :], cmp_window[:, which, at:at + QUADRANT],
                                                page[:, place * PAGE_GROUP + j, which * P:(which + 1) * P],
                                                start=(place_in == 0 and which == 0),
                                                stop=(place_in == QUADRANT_PAGES - 1), skip_group_check=True)
                last.then_inc(pages_read, 1)

            def transpose_kc(pair, b):
                pe.wait_ge(cmp_taken, 2 * pair + b + 1)
                ring.wait_free(pe, "kc_T", pair, b)
                nc.tensor.transpose(ring.bank("kc_T", pair, b)[:, :PAST_CMP], kc[:, b, :], identity[:, :]).then_inc(
                    ring.is_filled("kc_T", pair, b), 1)

            def page_scores(pair, slot):
                b = slot // GROUPS
                ring.wait_evacuated(pe, "page_T", pair, slot)
                ring.wait_free(pe, "page_scores", pair, slot)
                nc.tensor.matmul(ring.bank("page_scores", pair, slot)[b * R:(b + 1) * R, :], q_of(pair, b),
                                 page_k_T[slot % 2][:, :], start=True, stop=True).then_inc(
                                     ring.is_filled("page_scores", pair, slot), 1)

            def for_samples(pair, key, columns, moving):
                ring.wait_free(pe, *key)
                for b in range(2):
                    for at, x in zip(columns, moving(b)):
                        last = nc.tensor.matmul(ring.bank(*key)[b * R:(b + 1) * R, at:at + x.shape[-1]],
                                                q_of(pair, b), x, start=True, stop=True, skip_group_check=True)
                last.then_inc(ring.is_filled(*key), 1)

            def turn_probs(key, source, tiles):
                ring.wait_free(pe, *key)
                for m, (at, keys) in enumerate(tiles):
                    last = nc.tensor.transpose(ring.bank(*key)[:keys, m * P:(m + 1) * P], source[:, at:at + keys],
                                               identity[:, :])
                last.then_inc(ring.is_filled(*key), 1)

            def branch_values(key, out, tiles, first, final):
                ring.wait_evacuated(pe, *key)
                place = probs_T[places[key] % 3]
                for m, (keys, v) in enumerate(tiles):
                    for b in range(2):
                        last = nc.tensor.matmul(out[b * R:(b + 1) * R, :], place[:keys, m * P + b * R:m * P + (b + 1) * R],
                                                v(b), start=(first and m == 0), stop=(final and m == len(tiles) - 1),
                                                skip_group_check=True)
                last.then_inc(values_done, 1)

            def tail(pair, slot):
                b0 = 2 * pair
                if slot == 0:
                    for b in range(2):
                        ring.wait_evacuated(pe, "kc_T", pair, b)
                    for_samples(pair, ("cmp", pair), [0], lambda b: [kc_T[pair % 2][:, b, :]])
                    for_samples(pair, ("new", pair), [0, DEC_SEQ],
                                lambda b: [new_k_T[:, n, (b0 + b) * DEC_SEQ:(b0 + b + 1) * DEC_SEQ] for n in range(2)])
                elif slot == 1:
                    pe.wait_ge(win_landed, 32 * (pair + 1))
                    for b in range(2):
                        ring.wait_free(pe, "win_k", pair, b)
                        for j in range(WINDOW // P):
                            last = nc.tensor.transpose(ring.bank("win_k", pair, b)[:, j * P:(j + 1) * P],
                                                       win_kv[:, b, j, 0:P], identity[:, :])
                        last.then_inc(ring.is_filled("win_k", pair, b), 1)
                elif slot == 2:
                    pe.wait_ge(cmp_normed, pair + 1)
                    ring.wait_free(pe, "imp", pair)
                    bank = ring.bank("imp", pair)
                    nc.tensor.matmul(bank[:, 0:P], consts[:, GROUP_SUM:GROUP_SUM + P], cmp[:, :], start=True,
                                     stop=True).then_inc(ring.is_filled("imp", pair), 1)
                    turn_probs(("cmp_T", pair), cmp, [(0, P)])
                elif slot == 3:
                    for b in range(2):
                        ring.wait_evacuated(pe, "win_k", pair, b)
                        ring.wait_free(pe, "win", pair, b)
                        nc.tensor.matmul(ring.bank("win", pair, b)[b * R:(b + 1) * R, :], q_of(pair, b),
                                         win_k_T[:, b, :], start=True, stop=True).then_inc(
                                             ring.is_filled("win", pair, b), 1)
                elif slot == 4:
                    if pair:
                        pe.wait_ge(branch_taken, 3 * pair)
                    branch_values(("cmp_T", pair), short_out[:, 0:P], [(P, lambda b: vc[pair % 2][:, b, :])], True, True)
                elif slot == 6:
                    pe.wait_ge(probs_ready, 3 * pair + 2)
                    turn_probs(("win_T", pair, 0), win, [(j * P, P) for j in range(4)])
                    turn_probs(("win_T", pair, 1), win, [(WINDOW, DEC_SEQ)])
                elif slot >= 7:
                    g = slot - 7
                    if g == 0:
                        branch_values(("win_T", pair, 0), short_out[:, P:2 * P],
                                      [(P, lambda b, j=j: win_kv[:, b, j, P:2 * P]) for j in range(4)], True, False)
                        pe.wait_ge(new_v_landed, 32)
                        branch_values(("win_T", pair, 1), short_out[:, P:2 * P],
                                      [(DEC_SEQ, lambda b: new_v[:, 1, b0 + b, :])], False, True)
                        pe.wait_ge(probs_ready, 3 * (pair + 1))
                    else:
                        slc_values(pair, g - 1)
                    tiles = [(4 * g + m) for m in range(4) if 4 * g + m < KEY_TILES]
                    turn_probs(("slc_T", pair, g), slc[pair % 2],
                               [(j * P, P if j < N_PAGES else DEC_SEQ) for j in tiles])
                    if g == SLC_TURNS - 1:
                        slc_values(pair, g)

            def slc_values(pair, g):
                tiles = [(4 * g + m) for m in range(4) if 4 * g + m < KEY_TILES]
                old = lambda b, j: values[pair % 2][:, b, j, :]
                new = lambda b, j: new_v[:, 0, 2 * pair + b, :]
                if g == 0:
                    pe.wait_ge(values_copied, SLOTS * (pair + 1))
                branch_values(("slc_T", pair, g), slc_out[:, 0:P],
                              [(P, lambda b, j=j: old(b, j)) if j < N_PAGES else (DEC_SEQ, lambda b, j=j: new(b, j))
                               for j in tiles], g == 0, g == SLC_TURNS - 1)

            def gla_step(slot):
                if slot == 0:
                    ring.wait_free(pe, "ga_T")
                    nc.tensor.transpose(ring.bank("ga_T")[:RANK, :R], proj[:R, GA0:GA0 + RANK],
                                        identity[:R, :R]).then_inc(ring.is_filled("ga_T"), 1)
                elif slot == 1:
                    ring.wait_evacuated(pe, "ga_T")
                    ring.wait_free(pe, "z")
                    z = ring.bank("z")[:R, :GLA_WIDTH]
                    nc.tensor.matmul(z, ga_T[:, :], shared.w_a2[:, :], start=True, stop=False)
                    nc.tensor.matmul(z, shared.ones_row[:, :R], shared.b_a[:, :], start=False, stop=True).then_inc(
                        ring.is_filled("z"), 1)
                elif slot == 2:
                    pe.wait_ge(log_a_ready, 1)
                    ring.wait_free(pe, "cum")
                    bank = ring.bank("cum")
                    nc.tensor.matmul(bank[:R, :GLA_WIDTH], consts[:R, UPTO:UPTO + R], log_a[:, :], start=True, stop=True)
                    nc.tensor.matmul(bank[:R, GLA_WIDTH:], consts[:R, AFTER:AFTER + R], log_a[:, :], start=True,
                                     stop=True).then_inc(ring.is_filled("cum"), 1)
                    ring.wait_free(pe, "decay")
                    for half in range(2):
                        last = nc.tensor.matmul(ring.bank("decay")[:, half * DEC_BATCH:(half + 1) * DEC_BATCH],
                                                log_a[:, half * P:(half + 1) * P],
                                                consts[:R, OF_SAMPLE:OF_SAMPLE + DEC_BATCH], start=True, stop=True)
                    last.then_inc(ring.is_filled("decay"), 1)
                elif slot == 3:
                    pe.wait_ge(decayed_ready, 3)
                    ring.wait_free(pe, "gla_T")
                    for n, x in enumerate((q_cum, k_cum)):
                        for half in range(2):
                            last = nc.tensor.transpose(ring.bank("gla_T")[:, (2 * n + half) * R:(2 * n + half + 1) * R],
                                                       x[:, half * P:(half + 1) * P], identity[:R, :R])
                    last.then_inc(ring.is_filled("gla_T"), 1)
                elif slot == 4:
                    ring.wait_evacuated(pe, "gla_T")
                    ring.wait_free(pe, "att")
                    for half in range(2):
                        last = nc.tensor.matmul(ring.bank("att")[:R, half * P:(half + 1) * P], k_cum_T[:, half, :],
                                                q_pair_T[:, half, :, :].rearrange("p h t -> p (h t)"),
                                                start=True, stop=True)
                    last.then_inc(ring.is_filled("att"), 1)
                elif slot == 5:
                    pe.wait_ge(att_ready, 1)
                    pe.wait_ge(state_landed, 16 * 4)
                    ring.wait_free(pe, "o")
                    bank = ring.bank("o")
                    for h in range(GLA_HEADS):
                        nc.tensor.matmul(bank[:R, h * DV:(h + 1) * DV], att_T[:, h, :],
                                         proj[:R, GV0 + h * DV:GV0 + (h + 1) * DV], start=(h == 0), stop=False,
                                         skip_group_check=True)
                    for b in range(DEC_BATCH):
                        for half in range(2):
                            own = q_own_T[:, half, :, :].rearrange("p b t -> p (b t)")[:, b * R:(b + 1) * R]
                            last = nc.tensor.matmul(bank[:R, 2 * half * DV:2 * (half + 1) * DV], own,
                                                    state[:, half, b, :, :].rearrange("p h e -> p (h e)"),
                                                    start=False, stop=(b == DEC_BATCH - 1), skip_group_check=True)
                    last.then_inc(ring.is_filled("o"), 1)
                else:
                    b = slot - 6
                    pe.wait_ge(k_own_ready, 1)
                    ring.wait_free(pe, "state", b)
                    for half in range(2):
                        last = nc.tensor.matmul(ring.bank("state", b)[:, 2 * half * DV:2 * (half + 1) * DV],
                                                k_own[:, b, half * P:(half + 1) * P],
                                                proj[:R, GV0 + 2 * half * DV:GV0 + 2 * (half + 1) * DV],
                                                start=True, stop=True)
                    last.then_inc(ring.is_filled("state", b), 1)

            pe.wait_ge(window_ready, 2)
            for pair in range(PAIRS + 1):
                for slot in range(SLOTS):
                    if compressed(pair, slot):
                        transpose_kc(*compressed(pair, slot))
                    if pair < PAIRS:
                        page_group(pair, slot)
                    if scored(pair, slot):
                        page_scores(*scored(pair, slot))
                    if pair:
                        tail(pair - 1, slot)
                    elif slot < len(GLA):
                        gla_step(slot)

        def take_probs_T(eng, engine, key, tiles):
            n = places[key]
            if n >= 3:
                eng.wait_ge(values_done, n - 2)
            ring.wait_filled(eng, *key)
            whole = sum(k == P for k in tiles)
            parts = ([(P, 0, whole * P)] if whole else []) + [(k, m * P, P) for m, k in enumerate(tiles) if k != P]
            for rows, at, cols in parts:
                src, dst = ring.bank(*key)[:rows, at:at + cols], probs_T[n % 3][:rows, at:at + cols]
                if engine is nc.scalar:
                    last = nc.scalar.activation(dst, src, ACT.Copy)
                else:
                    last = nc.vector.tensor_copy(dst, src)
            last.then_inc(ring.is_evacuated(*key), 1)

        @block.scalar
        def _(act):
            act.wait_ge(cleared, 1)
            ring.wait_filled(act, "q_T")
            bank = ring.bank("q_T")[:, :GROUP * R].rearrange("p (g b t) -> p g b t", g=GROUP, b=DEC_BATCH)
            for kv in range(KV_HEADS):
                rows = slice(kv * HD, (kv + 1) * HD)
                for g in range(GROUP):
                    last = nc.scalar.activation(q_T[rows, :, kv, g, :], bank[rows, g, :, :], ACT.Copy)
            last.then_inc(ring.is_evacuated("q_T"), 1)
            ring.wait_filled(act, "new_k_T")
            nc.scalar.activation(new_k_T[:, :, :].rearrange("p n t -> p (n t)"), ring.bank("new_k_T")[:, :2 * R],
                                 ACT.Copy).then_inc(ring.is_evacuated("new_k_T"), 1)

            act.wait_ge(state_cleared, 1)
            for h in range(GLA_HEADS):
                rows = slice(h % 2 * DK, (h % 2 + 1) * DK)
                act.dma_start(state[rows, h // 2, :, h % 2, :],
                              a["state_gla"][0, :, h].rearrange("b d e -> d b e")).then_inc(state_landed, 16)
            win_out = outs[6].rearrange("l b t s h d -> (l b) t (s h d)")
            state_win = a["state_nsa_win"].rearrange("l b t s h d -> (l b) t (s h d)")
            act.dma_start(win_out[:, WINDOW - DEC_SEQ:, :], proj[:R, KV0 + 4 * P:KV0 + 6 * P]).then_inc(new_rows_out, 16)
            act.dma_start(win_out[:, :WINDOW - DEC_SEQ, :], state_win[:, DEC_SEQ:, :]).then_inc(rows_out, 16)
            new_rows = outs[5].rearrange("l b t s h d -> (l t) b (s h d)")
            act.dma_start(new_v[:, 0, :, :], new_rows[:, :, 3 * P:4 * P]).then_inc(new_v_landed, 16)
            act.wait_ge(new_rows_out, 16)
            act.dma_start(new_v[:, 1, :, :], win_out[:, WINDOW - DEC_SEQ:, P:].rearrange("b t c -> t b c")).then_inc(
                new_v_landed, 16)

            def take_page_T(pair, slot):
                n = pair * SLOTS + slot
                if n >= 2:
                    ring.wait_filled(act, "page_scores", (n - 2) // SLOTS, (n - 2) % SLOTS)
                ring.wait_filled(act, "page_T", pair, slot)
                nc.scalar.activation(page_k_T[slot % 2][:, :], ring.bank("page_T", pair, slot)[:, :],
                                     ACT.Copy).then_inc(ring.is_evacuated("page_T", pair, slot), 1)

            def take_cmp(pair, b):
                act.wait_ge(pages_read, pair * SLOTS + (b + 1) * GROUPS)
                if pair:
                    ring.wait_filled(act, "kc_T", pair - 1, b)
                if pair >= 2:
                    act.wait_ge(values_done, N_PLACES_PER_PAIR * (pair - 2) + 1)
                nc.scalar.activation(kc[:, b, :], cmp_ps[:, 0, :], ACT.Copy)
                nc.scalar.activation(vc[pair % 2][:, b, :], cmp_ps[:, 1, :], ACT.Copy).then_inc(cmp_taken, 1)

            def take_kc_T(pair, b):
                if pair >= 2:
                    ring.wait_filled(act, "cmp", pair - 2)
                ring.wait_filled(act, "kc_T", pair, b)
                nc.scalar.activation(kc_T[pair % 2][:, b, :], ring.bank("kc_T", pair, b)[:, :PAST_CMP],
                                     ACT.Copy).then_inc(ring.is_evacuated("kc_T", pair, b), 1)

            def exponentials(pair, branch):
                scores = (cmp, win, slc[pair % 2])[branch]
                act.wait_ge(neg_max_ready, 3 * pair + branch + 1)
                if pair:
                    act.wait_ge(branch_taken, 3 * pair)
                nc.scalar.activation(scores[:, :], scores[:, :], ACT.Exp, bias=neg_max[:, branch:branch + 1],
                                     scale=consts[:, SLOPE:SLOPE + 1], accum_out=sums[:, branch:branch + 1]).then_inc(probs_ready, 1)

            def load_win(pair):
                if pair:
                    act.wait_ge(values_done, N_PLACES_PER_PAIR * (pair - 1) + 3)
                for b in range(2):
                    act.dma_start(win_kv[:, b, :, :], state_win[2 * pair + b].rearrange(
                        "(j p) c -> p j c", p=P)).then_inc(win_landed, 16)

            def tail(pair, slot):
                if slot == 0:
                    exponentials(pair, 0)
                elif slot == 1:
                    for b in range(2):
                        ring.wait_filled(act, "win_k", pair, b)
                        if pair and b == 0:
                            ring.wait_filled(act, "win", pair - 1, 1)
                        nc.scalar.activation(win_k_T[:, b, :], ring.bank("win_k", pair, b)[:, :],
                                             ACT.Copy).then_inc(ring.is_evacuated("win_k", pair, b), 1)
                elif slot == 2:
                    take_probs_T(act, nc.scalar, ("cmp_T", pair), [P])
                elif slot == 4:
                    exponentials(pair, 1)
                elif slot == 5:
                    exponentials(pair, 2)
                elif slot == 6:
                    take_probs_T(act, nc.scalar, ("win_T", pair, 1), [DEC_SEQ])
                elif slot >= 7 and (slot - 7) % 2:
                    g = slot - 7
                    take_probs_T(act, nc.scalar, ("slc_T", pair, g),
                                 [P if j < N_PAGES else DEC_SEQ for j in range(4 * g, min(4 * g + 4, KEY_TILES))])
                if slot == 8 and pair + 1 < PAIRS:
                    load_win(pair + 1)

            def gla_step(slot):
                if slot == 0:
                    ring.wait_filled(act, "ga_T")
                    nc.scalar.activation(ga_T[:, :], ring.bank("ga_T")[:RANK, :R], ACT.Copy).then_inc(
                        ring.is_evacuated("ga_T"), 1)
                    nc.scalar.activation(silu[:, :], proj[:R, GG0:GG0 + GLA_HEADS * DV], ACT.Exp,
                                         scale=-1.0).then_inc(silu_step, 1)
                elif slot == 1:
                    act.wait_ge(abs_ready, 1)
                    nc.scalar.activation(log_a[:, :], log_a[:, :], ACT.Exp).then_inc(soft_step, 1)
                    act.wait_ge(soft_step, 1)
                    nc.scalar.activation(log_a[:, :], log_a[:, :], ACT.Ln, bias=1.0).then_inc(soft_step, 1)
                elif slot == 2:
                    ring.wait_filled(act, "cum")
                    bank = ring.bank("cum")
                    nc.scalar.activation(q_cum[:, :], bank[:R, :GLA_WIDTH], ACT.Exp).then_inc(exps_ready, 1)
                    nc.scalar.activation(k_cum[:, :], bank[:R, :GLA_WIDTH], ACT.Exp, scale=-1.0).then_inc(
                        exps_ready, 1)
                    nc.scalar.activation(k_last[:, :], bank[:R, GLA_WIDTH:], ACT.Exp).then_inc(
                        ring.is_evacuated("cum"), 1)
                    ring.wait_evacuated(act, "cum")
                    act.sem_inc(exps_ready, 1)
                    ring.wait_filled(act, "decay")
                    nc.scalar.activation(decay[:, :, :].rearrange("p a b -> p (a b)"),
                                         ring.bank("decay")[:, :2 * DEC_BATCH], ACT.Exp).then_inc(
                                             ring.is_evacuated("decay"), 1)
                    ring.wait_evacuated(act, "decay")
                    act.sem_inc(exps_ready, 1)
                elif slot == 3:
                    act.wait_ge(cleared, 2)
                    ring.wait_filled(act, "gla_T")
                    bank = ring.bank("gla_T")[:, :4 * R].rearrange("p (n a t) -> p n a t", n=2, a=2)
                    for head in range(2):
                        rows = slice(head * DK, (head + 1) * DK)
                        nc.scalar.activation(q_pair_T[rows, :, head, :], bank[rows, 0, :, :], ACT.Copy,
                                             scale=DK ** -0.5)
                    for half in range(2):
                        nc.scalar.activation(q_own_T[:, half, :, 0:DEC_SEQ],
                                             bank[:, 0, half, :].rearrange("p (b t) -> p b t", b=DEC_BATCH),
                                             ACT.Copy, scale=DK ** -0.5)
                    nc.scalar.activation(k_cum_T[:, :, :], bank[:, 1, :, :], ACT.Copy).then_inc(
                        ring.is_evacuated("gla_T"), 1)
                elif slot == 5:
                    ring.wait_filled(act, "o")
                    nc.scalar.activation(o_gla[:, :, :].rearrange("p h e -> p (h e)"), ring.bank("o")[:R, :],
                                         ACT.Copy).then_inc(ring.is_evacuated("o"), 1)
                    ring.wait_evacuated(act, "o")
                    for h in range(GLA_HEADS):
                        nc.scalar.activation(squares[:, h, :], o_gla[:, h, :], ACT.Square, scale=DV ** -0.5,
                                             accum_out=o_mean[:, h:h + 1]).then_inc(o_mean_ready, 1)

            load_win(0)
            for pair in range(PAIRS + 1):
                for slot in range(SLOTS):
                    if compressed(pair, slot):
                        take_kc_T(*compressed(pair, slot))
                    if pair < PAIRS:
                        take_page_T(pair, slot)
                    if pair:
                        tail(pair - 1, slot)
                    elif slot < len(GLA):
                        gla_step(slot)
                    if pair < PAIRS and slot % GROUPS == GROUPS - 1:
                        take_cmp(pair, slot // GROUPS)
                if pair == 0:
                    ring.wait_evacuated(act, "state", DEC_BATCH - 1)
                    for h in range(GLA_HEADS):
                        rows = slice(h % 2 * DK, (h % 2 + 1) * DK)
                        act.dma_start(outs[7][0, :, h].rearrange("b d e -> d b e"),
                                      state[rows, h // 2, :, h % 2, :]).then_inc(state_out, 16)
            act.wait_ge(state_out, 16 * GLA_HEADS)
            act.wait_ge(rows_out, 16)

        @block.vector
        def _(dve):
            steps = [0]

            def done(instruction):
                steps[0] += 1
                instruction.then_inc(dve_step, 1)
                dve.wait_ge(dve_step, steps[0])

            def take_page_scores(pair, slot):
                b, g = slot // GROUPS, slot % GROUPS
                rows, cols = slice(b * R, (b + 1) * R), slice(g * BANK, (g + 1) * BANK)
                if pair == 1 and slot == 0:
                    ring.wait_filled(dve, "state", DEC_BATCH - 1)
                if pair >= 2 and slot == 0:
                    ring.wait_filled(dve, "slc_T", pair - 2, SLC_TURNS - 1)
                ring.wait_filled(dve, "page_scores", pair, slot)
                nc.vector.scalar_tensor_tensor(out=slc[pair % 2][rows, cols], in0=group_dist[rows, :],
                                               scalar=float(g * BANK), in1=ring.bank("page_scores", pair, slot)[rows, :],
                                               op0=ALU.add, op1=ALU.add).then_inc(
                                                   ring.is_evacuated("page_scores", pair, slot), 1)

            def neg_of(branch, source):
                nc.vector.tensor_scalar(neg_max[:, branch:branch + 1], source, consts[:, NEG_SLOPE:NEG_SLOPE + 1], None,
                                        ALU.mult).then_inc(
                    neg_max_ready, 1)

            def biased(out, score, dist, at):
                return nc.vector.tensor_tensor_reduce(out=out, in0=score, in1=dist, scale=1.0,
                                                      scalar=MASKED, op0=ALU.add, op1=ALU.max,
                                                      accum_out=maxima[:, at:at + 1])

            def select_blocks(pair):
                ring.wait_filled(dve, "imp", pair)
                bank = ring.bank("imp", pair)
                done(nc.vector.memset(ranking[:, :], FORCE_SCORE))
                nc.vector.tensor_reduce(ranking[:, 1:N_SEL - 2],
                                        bank[:, 2:PAST_CMP - 2].rearrange("p (n r) -> p n r", r=2), AX.X,
                                        ALU.add).then_inc(ring.is_evacuated("imp", pair), 1)
                ring.wait_evacuated(dve, "imp", pair)
                for _ in range(2):
                    done(nc.vector.max(top8[:, :], ranking[:, :]))
                    done(nc.vector.match_replace(ranking[:, :], top8[:, :], ranking[:, :], MASKED))
                done(nc.vector.tensor_scalar(unselected[:, :], ranking[:, :], -1e29, MASKED, ALU.is_gt, ALU.mult))

            def tail(pair, slot):
                s = slc[pair % 2]
                if slot == 0:
                    if pair:
                        ring.wait_filled(dve, "cmp_T", pair - 1)
                        dve.wait_ge(branch_taken, 3 * pair)
                        ring.wait_filled(dve, "win_T", pair - 1, 1)
                    ring.wait_filled(dve, "cmp", pair)
                    biased(cmp[:, :], ring.bank("cmp", pair)[:, :PAST_CMP], cmp_dist[:, :], 0).then_inc(
                        ring.is_evacuated("cmp", pair), 1)
                    ring.wait_evacuated(dve, "cmp", pair)
                    neg_of(0, maxima[:, 0:1])
                    ring.wait_filled(dve, "new", pair)
                    bank = ring.bank("new", pair)
                    new = consts[:, NEW_DIST:NEW_DIST + DEC_SEQ]
                    nc.vector.tensor_tensor(s[:, PAST_LEN:], bank[:, 0:DEC_SEQ], new, ALU.add)
                    nc.vector.tensor_tensor(win[:, WINDOW:], bank[:, DEC_SEQ:2 * DEC_SEQ], new, ALU.add).then_inc(
                        ring.is_evacuated("new", pair), 1)
                    dve.wait_ge(probs_ready, 3 * pair + 1)
                    done(nc.vector.reciprocal(weight[:, 0:1], sums[:, 0:1]))
                    nc.vector.tensor_scalar(cmp[:, :], cmp[:, :], weight[:, 0:1], None, ALU.mult).then_inc(
                        cmp_normed, 1)
                elif slot == 2:
                    select_blocks(pair)
                elif slot == 3:
                    for b in range(2):
                        rows = slice(b * R, (b + 1) * R)
                        ring.wait_filled(dve, "win", pair, b)
                        nc.vector.tensor_tensor(win[rows, :WINDOW], ring.bank("win", pair, b)[rows, :],
                                                win_dist[rows, :], ALU.add).then_inc(
                                                    ring.is_evacuated("win", pair, b), 1)
                    ring.wait_evacuated(dve, "win", pair, 0)
                    ring.wait_evacuated(dve, "win", pair, 1)
                    ring.wait_evacuated(dve, "new", pair)
                    done(nc.vector.tensor_reduce(maxima[:, 1:2], win[:, :], AX.X, ALU.max))
                    neg_of(1, maxima[:, 1:2])
                elif slot == 4:
                    ring.wait_evacuated(dve, "page_scores", pair, SLOTS - 1)
                    ring.wait_evacuated(dve, "new", pair)
                    old = s[:, :PAST_LEN].rearrange("p (n k) -> p n k", k=SEL_BLOCK)
                    flags = broadcast(unselected[:, 0:N_SEL - 1].rearrange("p (n a) -> p n a", a=1),
                                      [P, N_SEL - 1, SEL_BLOCK])
                    biased(old, old, flags, 2)
                    last = unselected[:, N_SEL - 1:N_SEL].to_broadcast([P, DEC_SEQ])
                    done(biased(s[:, PAST_LEN:], s[:, PAST_LEN:], last, 3))
                    done(nc.vector.tensor_tensor(maxima[:, 2:3], maxima[:, 2:3], maxima[:, 3:4], ALU.max))
                    neg_of(2, maxima[:, 2:3])
                elif slot == 6:
                    take_probs_T(dve, nc.vector, ("win_T", pair, 0), [P] * 4)
                elif slot >= 7 and (slot - 7) % 2 == 0:
                    g = slot - 7
                    take_probs_T(dve, nc.vector, ("slc_T", pair, g),
                                 [P if j < N_PAGES else DEC_SEQ for j in range(4 * g, min(4 * g + 4, KEY_TILES))])
                if slot == SLOTS - 1:
                    take_branches(pair)

            def take_branches(pair):
                dve.wait_ge(probs_ready, 3 * (pair + 1))
                done(nc.vector.reciprocal(weight[:, 1:3], sums[:, 1:3]))
                dve.wait_ge(values_done, N_PLACES_PER_PAIR * (pair + 1))
                if pair:
                    dve.wait_ge(branch_stored, 16 * 4 * pair)
                nc.vector.tensor_copy(branch_out[:, 0, :], short_out[:, 0:P]).then_inc(branch_taken, 1)
                nc.vector.tensor_scalar(branch_out[:, 2, :], short_out[:, P:2 * P], weight[:, 1:2], None,
                                        ALU.mult).then_inc(branch_taken, 1)
                nc.vector.tensor_scalar(branch_out[:, 1, :], slc_out[:, 0:P], weight[:, 2:3], None,
                                        ALU.mult).then_inc(branch_taken, 1)

            def gla_step(slot):
                if slot == 0:
                    dve.wait_ge(silu_step, 1)
                    done(nc.vector.tensor_scalar(silu[:, :], silu[:, :], 1.0, None, ALU.add))
                    nc.vector.reciprocal(silu[:, :], silu[:, :]).then_inc(silu_step, 1)
                elif slot == 1:
                    ring.wait_filled(dve, "z")
                    z = ring.bank("z")[:R, :GLA_WIDTH]
                    done(nc.vector.tensor_scalar(z_min[:, :], z, 0.0, None, ALU.min))
                    nc.vector.scalar_tensor_tensor(out=log_a[:, :], in0=z, scalar=-1.0, in1=z_min[:, :],
                                                   op0=ALU.mult, op1=ALU.min).then_inc(ring.is_evacuated("z"), 1)
                    ring.wait_evacuated(dve, "z")
                    dve.sem_inc(abs_ready, 1)
                elif slot == 3:
                    dve.wait_ge(decayed_ready, 3)
                    nc.vector.tensor_tensor(
                        k_own, broadcast(k_last[:, :].rearrange("p (a c) -> p a c", a=1), [R, DEC_BATCH, GLA_WIDTH]),
                        broadcast(consts[:R, IS_SAMPLE:IS_SAMPLE + DEC_BATCH].rearrange("p (b a) -> p b a", a=1),
                                  [R, DEC_BATCH, GLA_WIDTH]), ALU.mult).then_inc(k_own_ready, 1)
                elif slot == 4:
                    dve.wait_ge(cleared, 2)
                    ring.wait_filled(dve, "att")
                    keep = broadcast(consts[:R, UPTO:UPTO + R].bitcast(U32).rearrange("p (a t) -> p a t", a=1),
                                     [R, GLA_HEADS, R])
                    nc.vector.copy_predicated(att_T[:, :, :], keep, ring.bank("att")[:R, :GLA_HEADS * R].rearrange(
                        "p (h t) -> p h t", h=GLA_HEADS)).then_inc(ring.is_evacuated("att"), 1)
                    ring.wait_evacuated(dve, "att")
                    dve.sem_inc(att_ready, 1)
                elif slot >= 6:
                    b = slot - 6
                    if b == 0:
                        ring.wait_filled(dve, "o")
                        dve.wait_ge(exps_ready, 4)
                    ring.wait_filled(dve, "state", b)
                    bank = ring.bank("state", b)[:, :].rearrange("p (a h e) -> p a h e", a=2, h=2)
                    for half in range(2):
                        for head in range(2):
                            rows = slice(head * DK, (head + 1) * DK)
                            last = nc.vector.scalar_tensor_tensor(
                                out=state[rows, half, b, head, :], in0=state[rows, half, b, head, :],
                                scalar=decay[rows, half, b:b + 1], in1=bank[rows, half, head, :],
                                op0=ALU.mult, op1=ALU.add)
                    last.then_inc(ring.is_evacuated("state", b), 1)

            dve.wait_ge(tables_ready, 1)
            for pair in range(PAIRS + 1):
                for slot in range(SLOTS):
                    if scored(pair, slot):
                        take_page_scores(*scored(pair, slot))
                    if pair:
                        tail(pair - 1, slot)
                    elif slot < len(GLA):
                        gla_step(slot)


def output_projection(nc, mix_rows, branch_rows, gates, x_rows, x1_rows, w_out, ln_ffn, identity, minus_half, normed_hi, normed_lo):
    with ExitStack() as ctx:
        def sb(name, shape, dtype=F32):
            return ctx.enter_context(nc.sbuf_tensor(name, shape, dtype))

        sem = ctx.enter_context(stage_semaphores(nc, "output"))

        w_raw = [sb(f"w_out_raw{n}", [P, 2, D_MODEL]) for n in range(2)]
        w_hi = sb("w_out_hi", [P, KT, D_MODEL], F32R)
        w_lo = sb("w_out_lo", [P, KT, D_MODEL], F32R)
        ln_col = sb("ln_ffn_col", [P, KT])
        mix = [sb(f"mix_in{n}", [P, D_MODEL]) for n in range(2)]
        x_in = [sb(f"x_res{n}", [P, D_MODEL]) for n in range(2)]
        mix_hi = [sb(f"mix_T_hi{n}", [P, KT, P], F32R) for n in range(2)]
        mix_lo = [sb(f"mix_T_lo{n}", [P, KT, P], F32R) for n in range(2)]
        x1 = [sb(f"x1_{n}", [P, D_MODEL]) for n in range(2)]
        x1n = [sb(f"x1n_{n}", [P, D_MODEL]) for n in range(2)]
        square = sb("x1_square", [P, D_MODEL])
        branches = sb("branches", [SAMPLE_ROWS, 3, NSA_WIDTH])
        mean_sq = sb("x1_mean_sq", [P, TILES])
        rstd = sb("x1_rstd", [P, TILES])

        w_landed = [sem(f"w_out_landed{n}") for n in range(2)]
        w_hi_ready = sem("w_out_hi_ready")
        w_lo_ready = sem("w_out_lo_ready")
        mix_hi_ready = sem("mix_hi_ready")
        ln_landed = sem("ln_ffn_landed")
        mix_landed = [sem(f"mix_landed{n}") for n in range(2)]
        x_landed = [sem(f"x_res_landed{n}") for n in range(2)]
        branches_landed = sem("branches_landed")
        branch_step = sem("branch_step")
        x1_stored = [sem(f"x1_stored{n}") for n in range(2)]
        mean_ready = sem("x1_mean_ready")
        rstd_ready = sem("x1_rstd_ready")
        x1n_ready = sem("x1n_ready")
        hi_ready = sem("normed_hi_ready")

        order = [("mix_T", 0, 0), ("mix_T", 0, 1)]
        for i in range(TILES):
            if i + 1 < TILES:
                order += [("mix_T", i + 1, 0), ("mix_T", i + 1, 1)]
            order += [("out", i, 0), ("out", i, 1)]
            if i:
                order += [("x1_T", i - 1, 0), ("x1_T", i - 1, 1)]
        order += [("x1_T", TILES - 1, 0), ("x1_T", TILES - 1, 1)]
        ring = turns(nc, ctx, sem, "out_bank", 8, order)

        block = ctx.enter_context(nc.Block())

        @block.sync
        def _(sp):
            sp.dma_start(ln_col[:, :], ln_ffn.rearrange("l (k p) -> p (l k)", p=P),
                         allow_slow_non_contiguous=True).then_inc(ln_landed, 16)
            for i in range(TILES):
                r, n = ROWS[i], i % 2
                if i >= 2:
                    ring.wait_filled(sp, "mix_T", i - 2, 1)
                    ring.wait_evacuated(sp, "out", i - 2, 1)
                first = 0 if i < PROMPT_TILES else NSA_WIDTH
                sp.dma_start(mix[n][:r, first:], mix_rows[i * P:i * P + r, first:]).then_inc(mix_landed[n], 16)
                sp.dma_start(x_in[n][:r, :], x_rows(i)).then_inc(x_landed[n], 16)
                if i == 0:
                    for k in range(KT // 2):
                        if k >= 2:
                            sp.wait_ge(w_lo_ready, k - 1)
                        sp.dma_start(w_raw[k % 2][:, :, :], w_out[0, 2 * k * P:(2 * k + 2) * P, :].rearrange(
                            "(k p) n -> p k n", p=P)).then_inc(w_landed[k % 2], 16)
                    for b in range(DEC_BATCH):
                        sp.dma_start(branches[b * DEC_SEQ:(b + 1) * DEC_SEQ, :, :].rearrange(
                            "t s (h d) -> t s h d", d=HD), branch_rows[b].rearrange(
                                "k g t s d -> t s (k g) d")).then_inc(branches_landed, 16)

        @block.gpsimd
        def _(pool):
            for i in range(TILES):
                r, n = ROWS[i], i % 2
                ring.wait_evacuated(pool, "out", i, 0)
                ring.wait_evacuated(pool, "out", i, 1)
                pool.dma_start(x1_rows[i * P:i * P + r, :], x1[n][:r, :]).then_inc(x1_stored[n], 16)
                pool.wait_ge(mean_ready, i + 1)
                nc.gpsimd.tensor_scalar(rstd[:r, i:i + 1], mean_sq[:r, i:i + 1], EPS, None,
                                        ALU.add).then_inc(rstd_ready, 1)
                pool.wait_ge(rstd_ready, 2 * i + 1)
                nc.gpsimd.tensor_tensor(rstd[:r, i:i + 1], rstd[:r, i:i + 1], minus_half[:r, 0:1],
                                        ALU.pow).then_inc(rstd_ready, 1)
            pool.wait_ge(x1_stored[0], 16 * 5)
            pool.wait_ge(x1_stored[1], 16 * 4)

        @block.tensor
        def _(pe):
            def transposes(key, source, r):
                for half in range(2):
                    ring.wait_free(pe, *key, half)
                    for j in range(4):
                        k = 4 * half + j
                        last = nc.tensor.transpose(ring.bank(*key, half)[:, j * r:(j + 1) * r],
                                                   source[:r, k * P:(k + 1) * P], identity[:r, :r])
                    last.then_inc(ring.is_filled(*key, half), 1)

            pe.wait_ge(mix_landed[0], 16)
            transposes(("mix_T", 0), mix[0], ROWS[0])
            for i in range(TILES):
                r, n = ROWS[i], i % 2
                if i + 1 < TILES:
                    pe.wait_ge(mix_landed[1 - n], 16 * ((i + 1) // 2 + 1))
                    if i + 1 == PROMPT_TILES:
                        pe.wait_ge(branch_step, 3)
                    transposes(("mix_T", i + 1), mix[1 - n], ROWS[i + 1])
                ring.wait_evacuated(pe, "mix_T", i, 0)
                ring.wait_evacuated(pe, "mix_T", i, 1)
                for c in range(2):
                    ring.wait_free(pe, "out", i, c)
                    for k in range(KT):
                        if i == 0 and c == 0 and k % 2 == 0:
                            pe.wait_ge(w_lo_ready, k // 2 + 1)
                        out = ring.bank("out", i, c)[:r, :]
                        hi, lo = mix_hi[n][:, k, :r], mix_lo[n][:, k, :r]
                        cols = slice(c * BANK, (c + 1) * BANK)
                        nc.tensor.matmul(out, hi, w_lo[:, k, cols], start=(k == 0), stop=False)
                        nc.tensor.matmul(out, hi, w_hi[:, k, cols], start=False, stop=False)
                        last = nc.tensor.matmul(out, lo, w_hi[:, k, cols], start=False, stop=(k == KT - 1))
                    last.then_inc(ring.is_filled("out", i, c), 1)
                if i:
                    pe.wait_ge(x1n_ready, i)
                    transposes(("x1_T", i - 1), x1n[1 - n], ROWS[i - 1])
            pe.wait_ge(x1n_ready, TILES)
            transposes(("x1_T", TILES - 1), x1n[(TILES - 1) % 2], ROWS[TILES - 1])

        @block.scalar
        def _(act):
            def split_w_hi(k):
                act.wait_ge(w_landed[k % 2], 16 * (k // 2 + 1))
                nc.scalar.activation(w_hi[:, 2 * k:2 * k + 2, :], w_raw[k % 2][:, :, :], ACT.Copy).then_inc(
                    w_hi_ready, 1)

            def split_mix_hi(i):
                r = ROWS[i]
                if i >= 2:
                    ring.wait_filled(act, "out", i - 2, 1)
                for half in range(2):
                    ring.wait_filled(act, "mix_T", i, half)
                    nc.scalar.activation(mix_hi[i % 2][:, 4 * half:4 * half + 4, :r],
                                         ring.bank("mix_T", i, half)[:, :4 * r].rearrange("p (k t) -> p k t", k=4),
                                         ACT.Copy).then_inc(mix_hi_ready, 1)

            split_mix_hi(0)
            for k in range(KT // 2):
                split_w_hi(k)
            for i in range(TILES):
                r = ROWS[i]
                if i + 1 < TILES:
                    split_mix_hi(i + 1)
                ring.wait_evacuated(act, "out", i, 0)
                ring.wait_evacuated(act, "out", i, 1)
                if i:
                    act.wait_ge(mean_ready, i)
                nc.scalar.activation(square[:r, :], x1[i % 2][:r, :], ACT.Square, scale=D_MODEL ** -0.5,
                                     accum_out=mean_sq[:r, i:i + 1]).then_inc(mean_ready, 1)

        @block.vector
        def _(dve):
            def scale_normed(i):
                r = ROWS[i]
                for half in range(2):
                    ring.wait_filled(dve, "x1_T", i, half)
                    ln = ln_col[:, 4 * half:4 * half + 4].rearrange("p (k a) -> p k a", a=1).to_broadcast([P, 4, r])
                    nc.vector.tensor_tensor(normed_hi[:, 4 * half:4 * half + 4, i * P:i * P + r],
                                            ring.bank("x1_T", i, half)[:, :4 * r].rearrange("p (k t) -> p k t", k=4),
                                            ln, ALU.mult).then_inc(hi_ready, 1)
                for half in range(2):
                    dve.wait_ge(hi_ready, 2 * i + half + 1)
                    for j in range(4):
                        k = 4 * half + j
                        hi = normed_hi[:, k, i * P:i * P + r].bitcast(F32)
                        last = nc.vector.scalar_tensor_tensor(
                            out=normed_lo[:, k, i * P:i * P + r], in0=ring.bank("x1_T", i, half)[:, j * r:(j + 1) * r],
                            scalar=ln_col[:, k:k + 1], in1=hi, op0=ALU.mult, op1=ALU.subtract)
                    last.then_inc(ring.is_evacuated("x1_T", i, half), 1)

            def mix_branches():
                dve.wait_ge(branches_landed, 16 * DEC_BATCH)
                gate = gates[:SAMPLE_ROWS, :].rearrange("p (b h a) -> p b h a", b=3, a=1)
                wide = branches[:, :, :].rearrange("p b (h d) -> p b h d", d=HD)
                nc.vector.tensor_tensor(wide, wide, broadcast(gate, [SAMPLE_ROWS, 3, HEADS, HD]),
                                        ALU.mult).then_inc(branch_step, 1)
                dve.wait_ge(branch_step, 1)
                ring.wait_filled(dve, "mix_T", PROMPT_TILES - 2, 1)
                out = mix[PROMPT_TILES % 2][:SAMPLE_ROWS, 0:NSA_WIDTH]
                nc.vector.tensor_tensor(out, branches[:, 0, :], branches[:, 1, :], ALU.add).then_inc(branch_step, 1)
                dve.wait_ge(branch_step, 2)
                nc.vector.tensor_tensor(out, out, branches[:, 2, :], ALU.add).then_inc(branch_step, 1)

            def split_w_lo(k):
                dve.wait_ge(w_hi_ready, k + 1)
                nc.vector.tensor_tensor(w_lo[:, 2 * k:2 * k + 2, :], w_raw[k % 2][:, :, :],
                                        w_hi[:, 2 * k:2 * k + 2, :].bitcast(F32), ALU.subtract).then_inc(w_lo_ready, 1)

            def split_mix_lo(i):
                r = ROWS[i]
                for half in range(2):
                    dve.wait_ge(mix_hi_ready, 2 * i + half + 1)
                    ks = slice(4 * half, 4 * half + 4)
                    nc.vector.tensor_tensor(mix_lo[i % 2][:, ks, :r],
                                            ring.bank("mix_T", i, half)[:, :4 * r].rearrange("p (k t) -> p k t", k=4),
                                            mix_hi[i % 2][:, ks, :r].bitcast(F32), ALU.subtract).then_inc(
                                                ring.is_evacuated("mix_T", i, half), 1)

            split_mix_lo(0)
            for k in range(KT // 2):
                split_w_lo(k)
            dve.wait_ge(ln_landed, 16)
            for i in range(TILES):
                r, n = ROWS[i], i % 2
                if i == PROMPT_TILES - 1:
                    mix_branches()
                if i + 1 < TILES:
                    split_mix_lo(i + 1)
                dve.wait_ge(x_landed[n], 16 * (i // 2 + 1))
                if i >= 2:
                    dve.wait_ge(x1_stored[n], 16 * (i // 2))
                    dve.wait_ge(mean_ready, i - 1)
                for c in range(2):
                    cols = slice(c * BANK, (c + 1) * BANK)
                    ring.wait_filled(dve, "out", i, c)
                    nc.vector.tensor_tensor(x1[n][:r, cols], ring.bank("out", i, c)[:r, :], x_in[n][:r, cols],
                                            ALU.add).then_inc(ring.is_evacuated("out", i, c), 1)
                if i:
                    scale_normed(i - 1)
                dve.wait_ge(rstd_ready, 2 * (i + 1))
                if i >= 2:
                    ring.wait_filled(dve, "x1_T", i - 2, 1)
                nc.vector.tensor_scalar(x1n[n][:r, :], x1[n][:r, :], rstd[:r, i:i + 1], None,
                                        ALU.mult).then_inc(x1n_ready, 1)
            scale_normed(TILES - 1)


def feed_forward_up(nc, normed_hi, normed_lo, hidden, w_gate, w_up):
    with ExitStack() as ctx:
        def sb(name, shape, dtype=F32):
            return ctx.enter_context(nc.sbuf_tensor(name, shape, dtype))

        sem = ctx.enter_context(stage_semaphores(nc, "ffn_up"))

        raw = sb("gate_up_raw", [P, 2, KT, P])
        hi = [sb(f"gate_up_hi{n}", [P, 2, KT, P], F32R) for n in range(2)]
        lo = [sb(f"gate_up_lo{n}", [P, 2, KT, P], F32R) for n in range(2)]
        silu = [sb(f"silu{c}", [P, 3 * P]) for c in range(3)]

        raw_landed = sem("raw_landed")
        hi_ready = sem("hi_ready")
        lo_ready = sem("lo_ready")
        products_ready = [sem(f"products_ready{c}") for c in range(3)]
        exp_ready = sem("silu_exp_ready")
        silu_step = sem("silu_step")
        hidden_ready = [sem(f"hidden_ready{c}") for c in range(3)]
        bank = [ctx.enter_context(nc.psum_tensor(f"up_bank{n}", [P, BANK], F32)) for n in range(6)]

        block = ctx.enter_context(nc.Block())

        @block.sync
        def _(sp):
            def load_raw(f):
                for m, w in enumerate((w_gate, w_up)):
                    sp.dma_start(raw[:, m, :, :], w[0, :, bass.ds(f * P, P)].rearrange(
                        "(k p) f -> p k f", p=P)).then_inc(raw_landed, 16)

            load_raw(0)
            with nc.sync.Fori(1, FT) as f:
                sp.wait_ge(lo_ready, f)
                sp.wait_ge(hi_ready, 1)
                load_raw(f)

        @block.tensor
        def _(pe):
            with nc.tensor.Fori(0, FT // 2) as it:
                for n in range(2):
                    pe.wait_ge(lo_ready, 2 * it + n + 1)
                    for c, (at, cols) in enumerate(PIECES):
                        pe.wait_ge(hidden_ready[c], 2 * it + n + 1)
                        for m in range(2):
                            out = bank[2 * c + m][:, :cols]
                            for k in range(KT):
                                w_hi, w_lo = hi[n][:, m, k, :], lo[n][:, m, k, :]
                                x_hi, x_lo = normed_hi[:, k, at:at + cols], normed_lo[:, k, at:at + cols]
                                nc.tensor.matmul(out, w_hi, x_lo, start=(k == 0), stop=False)
                                nc.tensor.matmul(out, w_hi, x_hi, start=False, stop=False)
                                last = nc.tensor.matmul(out, w_lo, x_hi, start=False, stop=(k == KT - 1))
                        last.then_inc(products_ready[c], 1)

        @block.scalar
        def _(act):
            def split_hi(n, f):
                act.wait_ge(raw_landed, 32 * f + 32)
                nc.scalar.activation(hi[n][:, :, :, :], raw[:, :, :, :], ACT.Copy).then_inc(hi_ready, 1)

            def exponentials(f):
                for c, (at, cols) in enumerate(PIECES):
                    act.wait_ge(products_ready[c], f + 1)
                    nc.scalar.activation(silu[c][:, :cols], bank[2 * c][:, :cols], ACT.Exp,
                                         scale=-1.0).then_inc(exp_ready, 1)

            for n in range(2):
                split_hi(n, n)
            with nc.scalar.Fori(0, FT // 2 - 1) as it:
                for n in range(2):
                    exponentials(2 * it + n)
                    split_hi(n, 2 * it + n + 2)
            exponentials(FT - 2)
            exponentials(FT - 1)

        @block.gpsimd
        def _(pool):
            with nc.gpsimd.Fori(0, FT // 2) as it:
                for n in range(2):
                    pool.wait_ge(hi_ready, 2 * it + n + 1)
                    nc.gpsimd.tensor_tensor(lo[n][:, :, :, :], raw[:, :, :, :], hi[n][:, :, :, :].bitcast(F32),
                                            ALU.subtract).then_inc(lo_ready, 1)

        @block.vector
        def _(dve):
            for c in range(3):
                dve.sem_inc(hidden_ready[c], 1)
            with nc.vector.Fori(0, FT) as f:
                for c, (at, cols) in enumerate(PIECES):
                    s = silu[c][:, :cols]
                    dve.wait_ge(exp_ready, 3 * f + c + 1)
                    nc.vector.tensor_scalar(s, s, 1.0, None, ALU.add).then_inc(silu_step, 1)
                    dve.wait_ge(silu_step, 9 * f + 3 * c + 1)
                    nc.vector.reciprocal(s, s).then_inc(silu_step, 1)
                    dve.wait_ge(silu_step, 9 * f + 3 * c + 2)
                    nc.vector.tensor_tensor(s, bank[2 * c][:, :cols], s, ALU.mult).then_inc(silu_step, 1)
                    dve.wait_ge(silu_step, 9 * f + 3 * c + 3)
                    nc.vector.tensor_tensor(hidden[:, bass.ds(f, 1), at:at + cols].rearrange("p a t -> p (a t)"),
                                            bank[2 * c + 1][:, :cols], s, ALU.mult).then_inc(hidden_ready[c], 1)


def feed_forward_down(nc, hidden, normed_hi, normed_lo, x1_rows, w_down, y_rows, identity):
    SLAB = 2 * P
    PASSES = D_MODEL // SLAB
    HALF = FT // 2
    X_PLACES, W_PLACES = 4, HALF
    with ExitStack() as ctx:
        def sb(name, shape, dtype=F32):
            return ctx.enter_context(nc.sbuf_tensor(name, shape, dtype))

        sem = ctx.enter_context(stage_semaphores(nc, "ffn_down"))

        raw = [sb(f"down_raw{h}", [P, HALF, SLAB]) for h in range(2)]
        y_T = sb("y_T", [P, 2, TOKENS])
        x1 = sb("x1_slab", [P, TILES, SLAB])

        def places(whole):
            flat = whole[:, :, :].rearrange("p k t -> p (k t)")
            at = X_PLACES * TOKENS
            return (flat[:, 0:at].rearrange("p (n t) -> p n t", n=X_PLACES),
                    flat[:, at:at + W_PLACES * SLAB].rearrange("p (n d) -> p n d", n=W_PLACES))

        x_hi, w_hi = places(normed_hi)
        x_lo, w_lo = places(normed_lo)

        raw_landed = [sem(f"raw_landed{h}") for h in range(2)]
        x1_landed = sem("x1_landed")
        x_hi_ready = sem("x_hi_ready")
        x_lo_ready = sem("x_lo_ready")
        w_hi_ready = sem("w_hi_ready")
        w_lo_ready = sem("w_lo_ready")
        steps_done = sem("steps_done")
        y_T_ready = sem("y_T_ready")
        y_filled = sem("y_filled")
        y_added = sem("y_added")
        y_stored = sem("y_stored")
        bank = [ctx.enter_context(nc.psum_tensor(f"down_bank{n}", [P, BANK], F32)) for n in range(8)]
        groups = [(half, c) for half in range(2) for c in range(3)]

        block = ctx.enter_context(nc.Block())

        @block.sync
        def _(sp):
            def load_raw(m, h):
                sp.dma_start(raw[h][:, :, :], w_down[0, h * HALF * P:(h + 1) * HALF * P, bass.ds(m * SLAB, SLAB)]
                             .rearrange("(f p) d -> p f d", p=P)).then_inc(raw_landed[h], 16)

            def load_x1(m):
                cols = bass.ds(m * SLAB, SLAB)
                sp.dma_start(x1[:, 0:PROMPT_TILES, :],
                             x1_rows[0:SEQ, cols].rearrange("(i p) d -> p i d", p=P)).then_inc(x1_landed, 16)
                sp.dma_start(x1[:SAMPLE_ROWS, PROMPT_TILES, :], x1_rows[SEQ:TOKENS, cols]).then_inc(x1_landed, 16)

            def store_y(m):
                cols = bass.ds(m * SLAB, SLAB)
                sp.dma_start(y_rows[0][0, :, cols].rearrange("(i p) d -> p i d", p=P),
                             x1[:, 0:PROMPT_TILES, :]).then_inc(y_stored, 16)
                sp.dma_start(y_rows[1].rearrange("b t d -> (b t) d")[:, cols],
                             x1[:SAMPLE_ROWS, PROMPT_TILES, :]).then_inc(y_stored, 16)

            load_raw(0, 0)
            load_raw(0, 1)
            load_x1(0)
            with nc.sync.Fori(0, PASSES - 1) as m:
                for h in range(2):
                    sp.wait_ge(w_lo_ready, FT * m + HALF * (h + 1))
                    sp.wait_ge(w_hi_ready, 1)
                    load_raw(m + 1, h)
                sp.wait_ge(y_added, 6 * m + 8)
                sp.wait_ge(w_hi_ready, 1)
                store_y(m)
                sp.wait_ge(y_stored, 32 * m + 32)
                sp.wait_ge(w_hi_ready, 1)
                load_x1(m + 1)
            sp.wait_ge(y_added, 6 * PASSES + 2)
            store_y(PASSES - 1)
            sp.wait_ge(y_stored, 32 * PASSES)

        @block.scalar
        def _(act):
            def split_x(f):
                nc.scalar.activation(x_hi[:, f % X_PLACES, :], hidden[:, f, :], ACT.Copy).then_inc(x_hi_ready, 1)

            def split_w(m, f):
                if f % HALF == 0:
                    act.wait_ge(raw_landed[f // HALF], 16 * m + 16)
                if f >= HALF:
                    act.wait_ge(steps_done, FT * m + f - HALF + 2)
                nc.scalar.activation(w_hi[:, f % HALF, :], raw[f // HALF][:, f % HALF, :], ACT.Copy).then_inc(
                    w_hi_ready, 1)

            split_x(0)
            with nc.scalar.Fori(0, PASSES) as m:
                split_w(m, 0)
                for f in range(1, FT):
                    act.wait_ge(steps_done, FT * m + max(f - X_PLACES + 2, 1))
                    split_x(f)
                    split_w(m, f)
                act.wait_ge(steps_done, FT * m + FT)
                split_x(0)
                act.wait_ge(steps_done, FT * m + FT + 1)
                for g, (half, c) in enumerate(groups):
                    at, cols = PIECES[c]
                    nc.scalar.activation(y_T[:, half, at:at + cols], bank[g][:, :cols], ACT.Copy).then_inc(y_T_ready, 1)

        @block.gpsimd
        def _(pool):
            with nc.gpsimd.Fori(0, PASSES) as m:
                for f in range(FT):
                    pool.wait_ge(w_hi_ready, FT * m + f + 1)
                    nc.gpsimd.tensor_tensor(w_lo[:, f % HALF, :], raw[f // HALF][:, f % HALF, :],
                                            w_hi[:, f % HALF, :].bitcast(F32), ALU.subtract).then_inc(w_lo_ready, 1)

        @block.tensor
        def _(pe):
            pe.sem_inc(steps_done, 1)
            with nc.tensor.Fori(0, PASSES) as m:
                for f in range(FT):
                    pe.wait_ge(x_lo_ready, FT * m + f + 1)
                    pe.wait_ge(w_lo_ready, FT * m + f + 1)
                    xp, wp = f % X_PLACES, f % HALF
                    for g, (half, c) in enumerate(groups):
                        at, cols = PIECES[c]
                        out = bank[g][:, :cols]
                        hi, lo = (w[:, wp, half * P:(half + 1) * P] for w in (w_hi, w_lo))
                        nc.tensor.matmul(out, hi, x_lo[:, xp, at:at + cols], start=(f == 0), stop=False)
                        nc.tensor.matmul(out, hi, x_hi[:, xp, at:at + cols], start=False, stop=False)
                        last = nc.tensor.matmul(out, lo, x_hi[:, xp, at:at + cols], start=False, stop=(f == FT - 1))
                    last.then_inc(steps_done, 1)
                for g, (half, c) in enumerate(groups):
                    at, cols = PIECES[c]
                    pe.wait_ge(y_T_ready, 6 * m + g + 1)
                    pe.wait_ge(y_added, 6 * m + g + 1)
                    for t in range(3):
                        r = min(P, cols - t * P)
                        last = nc.tensor.transpose(bank[6 + g % 2][:r, t * P:(t + 1) * P],
                                                   y_T[:, half, at + t * P:at + t * P + r], identity[:, :])
                    last.then_inc(y_filled, 1)

        @block.vector
        def _(dve):
            def split_x(f, count):
                dve.wait_ge(x_hi_ready, count)
                nc.vector.tensor_tensor(x_lo[:, f % X_PLACES, :], hidden[:, f, :],
                                        x_hi[:, f % X_PLACES, :].bitcast(F32), ALU.subtract).then_inc(x_lo_ready, 1)

            dve.sem_inc(y_added, 2)
            split_x(0, 1)
            with nc.vector.Fori(0, PASSES) as m:
                for f in range(1, FT + 1):
                    split_x(f % FT, FT * m + f + 1)
                dve.wait_ge(x1_landed, 32 * m + 32)
                for g, (half, c) in enumerate(groups):
                    at, cols = PIECES[c]
                    t0, whole = at // P, cols // P
                    dve.wait_ge(y_filled, 6 * m + g + 1)
                    y = x1[:, t0:t0 + whole, half * P:(half + 1) * P]
                    add = nc.vector.tensor_tensor(y, bank[6 + g % 2][:, :whole * P].rearrange(
                        "p (i d) -> p i d", d=P), y, ALU.add)
                    if cols % P:
                        y = x1[:SAMPLE_ROWS, t0 + whole, half * P:(half + 1) * P]
                        add = nc.vector.tensor_tensor(y, bank[6 + g % 2][:SAMPLE_ROWS, whole * P:(whole + 1) * P], y,
                                                      ALU.add)
                    add.then_inc(y_added, 1)


def program(nc, a, outs):
    mix_rows = nc.dram_tensor("mix_rows", (TOKENS, D_MODEL), F32, kind="Internal").ap()
    branch_rows = nc.dram_tensor("branch_rows", (DEC_BATCH, KV_HEADS, GROUP, DEC_SEQ, 3, HD), F32,
                                 kind="Internal").ap()
    x1_rows = nc.dram_tensor("x1_rows", (TOKENS, D_MODEL), F32, kind="Internal").ap()

    def x_rows(i):
        if i < PROMPT_TILES:
            return a["x_prompt"][0, i * P:(i + 1) * P, :]
        return a["x_sample"].rearrange("b t d -> (b t) d")

    with ExitStack() as ctx:
        identity = ctx.enter_context(nc.sbuf_tensor("identity", [P, P], F32))
        minus_half = ctx.enter_context(nc.sbuf_tensor("minus_half", [P, 16], F32))
        gates = ctx.enter_context(nc.sbuf_tensor("gates0", [P, 3 * HEADS], F32))
        make_constants(nc, identity, minus_half)
        with ExitStack() as attention:
            shared = Shared(nc, attention, identity, minus_half, gates)
            prompt_stage(nc, a, outs, mix_rows, x_rows, shared)
            samples_stage(nc, a, outs, mix_rows, branch_rows, shared)
        normed_hi = ctx.enter_context(nc.sbuf_tensor("normed_hi", [P, KT, TOKENS], F32R))
        normed_lo = ctx.enter_context(nc.sbuf_tensor("normed_lo", [P, KT, TOKENS], F32R))
        output_projection(nc, mix_rows, branch_rows, gates, x_rows, x1_rows, a["w_out"], a["ln_ffn"], identity, minus_half,
                          normed_hi, normed_lo)
        hidden = ctx.enter_context(nc.sbuf_tensor("hidden", [P, FT, TOKENS], F32))
        feed_forward_up(nc, normed_hi, normed_lo, hidden, a["w_gate"], a["w_up"])
        feed_forward_down(nc, hidden, normed_hi, normed_lo, x1_rows, a["w_down"], outs[0:2], identity)


def make_constants(nc, identity, minus_half):
    with stage_semaphores(nc, "constants") as sem, nc.Block() as block:
        cleared = sem("identity_cleared")

        @block.gpsimd
        def _(pool):
            nc.gpsimd.memset(minus_half[:, :], -0.5)
            nc.gpsimd.memset(identity[:, :], 0.0).then_inc(cleared, 1)
            pool.wait_ge(cleared, 1)
            nc.gpsimd.affine_select(out=identity[:, :], in_=identity[:, :], compare_op=ALU.not_equal, fill=1.0,
                                    base=0, pattern=[[-1, P]], channel_multiplier=1)


INPUTS = ["x_prompt", "x_sample", "cache_nsa_kv", "state_nsa_win", "state_gla", "page_table", "ln_mix", "w_in",
          "q_norm", "k_norm", "cmp_pos_w", "w_a2", "b_a", "gla_norm", "w_out", "ln_ffn", "w_gate", "w_up", "w_down"]
OUTPUTS = [(1, SEQ, D_MODEL), (DEC_BATCH, DEC_SEQ, D_MODEL), (1, 1, SEQ, 4, KV_HEADS, HD),
           (1, 1, WINDOW, 2, KV_HEADS, HD), (1, 1, GLA_HEADS, DK, DV), (1, DEC_BATCH, DEC_SEQ, 4, KV_HEADS, HD),
           (1, DEC_BATCH, WINDOW, 2, KV_HEADS, HD), (1, DEC_BATCH, GLA_HEADS, DK, DV)]


def kernel(**inputs):
    import numpy as np
    import concourse.bacc as bacc
    from concourse.bass_utils import run_bass_kernel_spmd

    nc = bacc.Bacc("TRN2", target_bir_lowering=False, num_devices=1)
    arrays, aps = {}, {}
    inputs["sample_consts"] = sample_constants()
    for name in [*INPUTS, "sample_consts"]:
        array = np.ascontiguousarray(inputs[name])
        arrays[f"in_{name}"] = array
        aps[name] = nc.dram_tensor(f"in_{name}", array.shape, mybir.dt.from_np(array.dtype), kind="ExternalInput").ap()
    outs = [nc.dram_tensor(f"out_{n}", shape, F32, kind="ExternalOutput").ap() for n, shape in enumerate(OUTPUTS)]
    program(nc, aps, outs)
    result = run_bass_kernel_spmd(nc, [arrays], core_ids=[0])
    return tuple(result.results[0][f"out_{n}"] for n in range(len(OUTPUTS)))
```
